# Optimizing a Trainium2 kernel written in Bass

```python
import jax
import jax.numpy as jnp
from jax import lax
import numpy as np

"""One hybrid decoder layer (causal), adaLN-conditioned.

Inputs:  x (BATCH, SEQ, D_MODEL) float32, c (BATCH, D_MODEL) float32,
         positions (BATCH, SEQ) int32, plus per-layer weights stacked on a leading DEPTH axis.
Output:  (BATCH, SEQ, D_MODEL).

Sub-layer 1 (token mixing): RMSNorm + adaLN shift/scale -> one combined q/k/v projection whose
columns are split between (A) dilated sliding-window attention (3 head groups with (window, dilation)
= (128,1), (512,4), (2048,16), keys gathered by stride, group outputs combined by softmax denominators;
QK-norm + partial rotary) and (B) stick-breaking attention (no positional encoding, strictly causal).
Each branch is projected to D_MODEL, merged with per-channel sigmoid gates from the normalised input,
then one output projection; adaLN gate on the residual update.
Sub-layer 2 (channel mixing): RMSNorm + adaLN shift/scale -> hierarchical MoE (top-1 group, top-2
SwiGLU experts inside the group) -> adaLN gate on the residual update.
"""

D_MODEL = 1024
BATCH = 1
SEQ = 512
DEPTH = 1

HEAD_DIM = 64
DIL_PATTERNS = ((128, 1), (512, 4), (2048, 16))
DIL_HEADS_PER_GROUP = 4
N_DIL_GROUPS = len(DIL_PATTERNS)
DIL_HEADS = N_DIL_GROUPS * DIL_HEADS_PER_GROUP
DIL_WIDTH = DIL_HEADS * HEAD_DIM
DIL_OUT_WIDTH = DIL_HEADS_PER_GROUP * HEAD_DIM
SB_HEADS = 4
SB_WIDTH = SB_HEADS * HEAD_DIM
QKV_WIDTH = 3 * DIL_WIDTH + 3 * SB_WIDTH
QBLOCK = 128
ROPE_THETA = 500000.0
ROPE_DIM = HEAD_DIM // 4
N_GROUPS = 4
EXPERTS_PER_GROUP = 8
N_EXPERTS = N_GROUPS * EXPERTS_PER_GROUP
TOP_K_INNER = 2
D_EXPERT = 512
EXPERT_CHUNK = 256
RMS_EPS = 1e-6

kernel_name = 'hybrid_dilated_stickbreak_hmoe_layer'

def rms_norm(x, g):
    xf = x.astype(jnp.float32)
    y = xf * lax.rsqrt(jnp.mean(xf * xf, axis=-1, keepdims=True) + RMS_EPS)
    return (y * g.astype(jnp.float32)).astype(x.dtype)

def partial_rope(x, cos, sin):
    half = ROPE_DIM // 2
    xr = x[..., :ROPE_DIM].astype(jnp.float32)
    x1, x2 = xr[..., :half], xr[..., half:]
    rot = jnp.concatenate([x1 * cos - x2 * sin, x2 * cos + x1 * sin], axis=-1)
    return jnp.concatenate([rot.astype(x.dtype), x[..., ROPE_DIM:]], axis=-1)

def dilated_attention(q, k, v):
    b, s = q.shape[0], q.shape[1]
    n_blocks = s // QBLOCK
    scale = HEAD_DIM ** -0.5
    hpg = DIL_HEADS_PER_GROUP
    kf = k.astype(jnp.float32)
    vf = v.astype(jnp.float32)
    k_groups = [kf[:, :, g * hpg:(g + 1) * hpg] for g in range(N_DIL_GROUPS)]
    v_groups = [vf[:, :, g * hpg:(g + 1) * hpg] for g in range(N_DIL_GROUPS)]

    def block(i):
        start = i * QBLOCK
        t = start + jnp.arange(QBLOCK, dtype=jnp.int32)
        qb = lax.dynamic_slice_in_dim(q, start, QBLOCK, axis=1).astype(jnp.float32)
        outs, lses = [], []
        for g, (window, dil) in enumerate(DIL_PATTERNS):
            n_keys = window // dil + 1
            idx = t[:, None] - dil * jnp.arange(n_keys, dtype=jnp.int32)[None, :]
            valid = idx >= 0
            idx = jnp.maximum(idx, 0)
            kg = jnp.take(k_groups[g], idx, axis=1)
            vg = jnp.take(v_groups[g], idx, axis=1)
            sc = jnp.einsum('bqhd,bqjhd->bhqj', qb[:, :, g * hpg:(g + 1) * hpg], kg) * scale
            sc = jnp.where(valid[None, None], sc, -jnp.inf)
            lse = jax.nn.logsumexp(sc, axis=-1)
            p = jnp.exp(sc - lse[..., None])
            outs.append(jnp.einsum('bhqj,bqjhd->bqhd', p, vg))
            lses.append(lse)
        w = jax.nn.softmax(jnp.stack(lses, axis=0), axis=0)
        w = jnp.transpose(w, (0, 1, 3, 2))[..., None]
        return jnp.sum(w * jnp.stack(outs, axis=0), axis=0)

    out = lax.map(block, jnp.arange(n_blocks, dtype=jnp.int32))
    out = jnp.transpose(out, (1, 0, 2, 3, 4)).reshape(b, s, DIL_OUT_WIDTH)
    return out.astype(q.dtype)

def stick_breaking_attention(q, k, v):
    b, s = q.shape[0], q.shape[1]
    n_blocks = s // QBLOCK
    scale = HEAD_DIM ** -0.5
    kf = k.astype(jnp.float32)
    vf = v.astype(jnp.float32)
    key_pos = jnp.arange(s, dtype=jnp.int32)

    def block(i):
        start = i * QBLOCK
        t = start + jnp.arange(QBLOCK, dtype=jnp.int32)
        qb = lax.dynamic_slice_in_dim(q, start, QBLOCK, axis=1).astype(jnp.float32)
        z = jnp.einsum('bqhd,bshd->bhqs', qb, kf) * scale
        mask = (key_pos[None, :] < t[:, None])[None, None]
        log_1m = jnp.where(mask, jax.nn.log_sigmoid(-z), 0.0)
        suffix = lax.cumsum(log_1m, axis=3, reverse=True)
        between = jnp.concatenate([suffix[..., 1:], jnp.zeros_like(suffix[..., :1])], axis=-1)
        a = jnp.where(mask, jnp.exp(jax.nn.log_sigmoid(z) + between), 0.0)
        return jnp.einsum('bhqs,bshd->bqhd', a, vf)

    out = lax.map(block, jnp.arange(n_blocks, dtype=jnp.int32))
    out = jnp.transpose(out, (1, 0, 2, 3, 4)).reshape(b, s, SB_WIDTH)
    return out.astype(q.dtype)

def hierarchical_moe(u, w_rg, b_rg, w_re, b_re, w_g, w_u, w_d):
    n_tok, d = u.shape
    uf = u.astype(jnp.float32)
    p_group = jax.nn.softmax(uf @ w_rg.astype(jnp.float32) + b_rg.astype(jnp.float32), axis=-1)
    pg_top, g_sel = lax.top_k(p_group, 1)
    logits_e = (uf @ w_re.astype(jnp.float32) + b_re.astype(jnp.float32)).reshape(n_tok, N_GROUPS, EXPERTS_PER_GROUP)
    logits_sel = jnp.take_along_axis(logits_e, g_sel[:, :, None], axis=1)[:, 0]
    pi_top, e_in = lax.top_k(jax.nn.softmax(logits_sel, axis=-1), TOP_K_INNER)
    weights = pg_top * pi_top / jnp.sum(pi_top, axis=-1, keepdims=True)
    expert_id = g_sel * EXPERTS_PER_GROUP + e_in

    n_assign = n_tok * TOP_K_INNER
    flat_e = expert_id.reshape(-1).astype(jnp.int32)
    flat_w = weights.reshape(-1)
    flat_tok = jnp.repeat(jnp.arange(n_tok, dtype=jnp.int32), TOP_K_INNER)
    order = jnp.argsort(flat_e)
    sorted_e = flat_e[order]
    counts = jnp.bincount(flat_e, length=N_EXPERTS).astype(jnp.int32)
    starts = jnp.cumsum(counts) - counts
    padded = (counts + EXPERT_CHUNK - 1) // EXPERT_CHUNK * EXPERT_CHUNK
    padded_ends = jnp.cumsum(padded)
    padded_starts = padded_ends - padded
    dest = padded_starts[sorted_e] + jnp.arange(n_assign, dtype=jnp.int32) - starts[sorted_e]
    n_chunks = -(-n_assign // EXPERT_CHUNK) + N_EXPERTS
    n_slots = n_chunks * EXPERT_CHUNK
    slot_tok = jnp.full((n_slots,), n_tok, jnp.int32).at[dest].set(flat_tok[order])
    slot_w = jnp.zeros((n_slots,), jnp.float32).at[dest].set(flat_w[order])
    chunk_e = jnp.minimum(
        jnp.searchsorted(padded_ends, jnp.arange(n_chunks, dtype=jnp.int32) * EXPERT_CHUNK, side='right'),
        N_EXPERTS - 1).astype(jnp.int32)
    u_pad = jnp.concatenate([u, jnp.zeros((1, d), u.dtype)], axis=0)
    chunk_x = u_pad[slot_tok].reshape(n_chunks, EXPERT_CHUNK, d)

    def expert_chunk(args):
        xc, e = args
        h = jax.nn.silu(xc @ w_g[e]) * (xc @ w_u[e])
        return h @ w_d[e]

    y = lax.map(expert_chunk, (chunk_x, chunk_e)).reshape(n_slots, d)
    y = y * slot_w[:, None].astype(y.dtype)
    return jnp.zeros((n_tok + 1, d), y.dtype).at[slot_tok].add(y)[:n_tok]

def setup_inputs(seed: int = 0) -> dict:
    key = jax.random.key(seed)
    ks = jax.random.split(key, 24)
    L = DEPTH
    D = D_MODEL

    def nrm(k, shape, fan_in):
        return jax.random.normal(k, shape, jnp.float32) * fan_in ** -0.5

    def gain(k, shape):
        return 1.0 + 0.01 * jax.random.normal(k, shape, jnp.float32)

    x = jax.random.normal(ks[0], (BATCH, SEQ, D), jnp.float32)
    c = jax.random.normal(ks[1], (BATCH, D), jnp.float32)
    positions = (jax.random.randint(ks[2], (BATCH, 1), 0, 4096, dtype=jnp.int32)
                 + jnp.arange(SEQ, dtype=jnp.int32)[None, :])
    return {
        'x': x,
        'c': c,
        'positions': positions,
        'w_ada': nrm(ks[3], (L, D, 6 * D), D) * 0.5,
        'b_ada': 0.01 * jax.random.normal(ks[4], (L, 6 * D), jnp.float32),
        'g_norm_mix': gain(ks[5], (L, D)),
        'g_norm_ffn': gain(ks[6], (L, D)),
        'w_in': nrm(ks[7], (L, D, QKV_WIDTH), D),
        'w_branch_gate': nrm(ks[8], (L, D, 2 * D), D),
        'q_norm_g': gain(ks[9], (L, HEAD_DIM)),
        'k_norm_g': gain(ks[10], (L, HEAD_DIM)),
        'w_branch_dil': nrm(ks[11], (L, DIL_OUT_WIDTH, D), DIL_OUT_WIDTH),
        'w_branch_sb': nrm(ks[12], (L, SB_WIDTH, D), SB_WIDTH),
        'w_out': nrm(ks[13], (L, D, D), D),
        'w_router_group': nrm(ks[14], (L, D, N_GROUPS), D),
        'b_router_group': 0.01 * jax.random.normal(ks[15], (L, N_GROUPS), jnp.float32),
        'w_router_expert': nrm(ks[16], (L, D, N_EXPERTS), D),
        'b_router_expert': 0.01 * jax.random.normal(ks[17], (L, N_EXPERTS), jnp.float32),
        'w_expert_gate': nrm(ks[18], (L, N_EXPERTS, D, D_EXPERT), D),
        'w_expert_up': nrm(ks[19], (L, N_EXPERTS, D, D_EXPERT), D),
        'w_expert_down': nrm(ks[20], (L, N_EXPERTS, D_EXPERT, D), D_EXPERT),
    }

def reference(x, c, positions, w_ada, b_ada, g_norm_mix, g_norm_ffn, w_in, w_branch_gate,
              q_norm_g, k_norm_g, w_branch_dil, w_branch_sb, w_out, w_router_group,
              b_router_group, w_router_expert, b_router_expert, w_expert_gate, w_expert_up,
              w_expert_down):
    b, s, d = x.shape
    inv_freq = ROPE_THETA ** (-jnp.arange(0, ROPE_DIM, 2, dtype=jnp.float32) / ROPE_DIM)
    ang = positions.astype(jnp.float32)[..., None] * inv_freq
    cos = jnp.cos(ang)[:, :, None, :]
    sin = jnp.sin(ang)[:, :, None, :]
    c_act = jax.nn.silu(c.astype(jnp.float32))

    for l in range(DEPTH):
        mod = (c_act @ w_ada[l].astype(jnp.float32) + b_ada[l].astype(jnp.float32)).astype(x.dtype)
        shift1, scale1, gate1, shift2, scale2, gate2 = jnp.split(mod[:, None, :], 6, axis=-1)

        h = rms_norm(x, g_norm_mix[l]) * (1 + scale1) + shift1
        proj = h @ w_in[l]
        cuts = np.cumsum([DIL_WIDTH, DIL_WIDTH, DIL_WIDTH, SB_WIDTH, SB_WIDTH]).tolist()
        qa, ka, va, qb, kb, vb = jnp.split(proj, cuts, axis=-1)
        qa = qa.reshape(b, s, DIL_HEADS, HEAD_DIM)
        ka = ka.reshape(b, s, DIL_HEADS, HEAD_DIM)
        va = va.reshape(b, s, DIL_HEADS, HEAD_DIM)
        qa = partial_rope(rms_norm(qa, q_norm_g[l]), cos, sin)
        ka = partial_rope(rms_norm(ka, k_norm_g[l]), cos, sin)
        o_dil = dilated_attention(qa, ka, va)
        o_sb = stick_breaking_attention(qb.reshape(b, s, SB_HEADS, HEAD_DIM),
                                        kb.reshape(b, s, SB_HEADS, HEAD_DIM),
                                        vb.reshape(b, s, SB_HEADS, HEAD_DIM))
        g_dil, g_sb = jnp.split(jax.nn.sigmoid(h @ w_branch_gate[l]), 2, axis=-1)
        merged = g_dil * (o_dil @ w_branch_dil[l]) + g_sb * (o_sb @ w_branch_sb[l])
        x = x + gate1 * (merged @ w_out[l])

        h2 = rms_norm(x, g_norm_ffn[l]) * (1 + scale2) + shift2
        y = hierarchical_moe(h2.reshape(b * s, d), w_router_group[l], b_router_group[l],
                             w_router_expert[l], b_router_expert[l], w_expert_gate[l],
                             w_expert_up[l], w_expert_down[l])
        x = x + gate2 * y.reshape(b, s, d)
    return x


_drawn_inputs = setup_inputs


def setup_inputs(seed=0):
    import zlib

    import numpy as np

    out = dict(_drawn_inputs(seed))
    spreads = {}
    factors = {'b_ada': 4.833,
     'g_norm_mix': 8.0,
     'g_norm_ffn': 6.332,
     'q_norm_g': 8.0,
     'k_norm_g': 8.0,
     'b_router_group': 64.0,
     'b_router_expert': 8.0}
    for name, (base, spread) in spreads.items():
        noise = np.random.default_rng([zlib.crc32(name.encode()), seed]).standard_normal(out[name].shape)
        drawn = base * np.exp(spread * noise) if base else spread * noise
        out[name] = jnp.asarray(drawn.astype(out[name].dtype))
    for name, factor in factors.items():
        out[name] = (out[name] * factor).astype(out[name].dtype)
    return out
```

```python
from contextlib import ExitStack

import numpy as np

import concourse.bass as bass
from concourse import mybir

ALU = mybir.AluOpType
ACT = mybir.ActivationFunctionType
F32 = mybir.dt.float32
I32 = mybir.dt.int32
AX_X = mybir.AxisListType.X

P = 128
D = 1024
SEQ = 512
NT = SEQ // P
KC = D // P
HD = 64
NH = 4
GW = NH * HD
ROPE_DIM = HD // 4
HALF = ROPE_DIM // 2
ROPE_THETA = 500000.0
RMS_EPS = 1e-6
NG = 4
EPG = 8
NE = NG * EPG
FE = 512
CAP = 64
ROUNDS = SEQ // CAP
CH = 512
NEG = -1e30
UNUSED = 4096.0
SLOT_W = KC * CH
EXP_W = 3 * SLOT_W
NBUF = 3

QA, KA, VA = 0, 3 * GW, 6 * GW
QB, KB, VB = 9 * GW, 10 * GW, 11 * GW
C_SB, C_VNAT, C_QK0, C_QRES, C_KRES, C_VRES = range(6)
SB_OFF = [0, 512, 1024, 896]
SB_COLS = 1280


def two_pi_parts():
    rest, parts = np.float64(2 * np.pi), []
    for bits in (8, 8, 8):
        e = int(np.floor(np.log2(rest))) - bits + 1
        part = np.floor(rest / 2.0 ** e) * 2.0 ** e
        parts.append(float(part))
        rest = rest - part
    return parts + [float(np.float32(rest))]


def hybrid_layer(nc, x, c, positions, w_ada, b_ada, g_norm_mix, g_norm_ffn, w_in, w_branch_gate,
                 q_norm_g, k_norm_g, w_branch_dil, w_branch_sb, w_out, w_router_group,
                 b_router_group, w_router_expert, b_router_expert, w_expert_gate, w_expert_up,
                 w_expert_down, out):
    inv_freq = np.float32(ROPE_THETA) ** (-np.arange(0, ROPE_DIM, 2, dtype=np.float32) / np.float32(ROPE_DIM))

    ctx = ExitStack()
    with ctx:
        def sb(name, shape, dt=F32):
            return ctx.enter_context(nc.sbuf_tensor(name, shape, dt))

        def sem(name):
            return ctx.enter_context(nc.semaphore(name))

        dil_rows = nc.dram_tensor("dil_rows", (SEQ, GW + 2 * NH), F32, kind="Internal").ap()
        y_rows = nc.dram_tensor("y_rows", (SEQ * 2 * 2, CH), F32, kind="Internal").ap()

        arena = sb("arena", [P, NBUF * EXP_W])
        xs = sb("xs", [P, NT, D])
        xn = sb("xn", [P, NT, D])
        hT = sb("hT", [P, KC, SEQ])
        ident = sb("ident", [P, P])
        ones = sb("ones", [P, P])
        strict = sb("strict", [P, P])
        tri = sb("tri", [P, P])
        small = sb("small", [P, 1168])
        wr = sb("wr", [P, KC, NG + NE])
        br = sb("br", [1, NG + NE])
        gains = sb("gains", [P, 2, HD])
        trig = sb("trig", [P, 2 * 2 * NT * ROPE_DIM])
        cos16, sin16 = (trig[:, P * i:P * i + P].rearrange("p (t d) -> p t d", t=2 * NT) for i in range(2))
        crep_f = sb("crep", [P, KC * 32])
        crep = crep_f[:].rearrange("p (k m) -> p k m", k=KC)
        modr = sb("modr", [P, CH])
        grow = sb("grow", [P, CH])
        cols = sb("cols", [P, 4, KC])
        gn = sb("gn", [P, 2, KC])
        st = sb("st", [P, 64])
        pos_i = sb("pos_i", [P, 2 * NT], I32)
        c_in = sb("c_in", [P, KC])

        mask12 = small[:, 0:256].rearrange("p (g n) -> p g n", g=2)
        mask0 = small[:, 256:512]
        negstrict = small[:, 512:640]
        ustage = small[:, 640:1168].rearrange("p (b n) -> p b n", b=2)

        gn_rows = small[0:16, 640:768]
        diff_i, diff_m = small[:, 912:1040].bitcast(I32), small[:, 1040:1168]
        stats = sb("stats", [P, 4, 12])
        cstats = sb("cstats", [P, 2, 16])
        o_dil = small[:, 0:GW]

        def stat(s):
            return stats[:, s % 4, :]

        def cstat(i):
            return cstats[:, i % 2, :]

        def wslot(j):
            return arena[:, j * SLOT_W:(j + 1) * SLOT_W].rearrange("p (k n) -> p k n", k=KC)

        base = 2 * EXP_W
        QT = arena[:, base:base + 3072].rearrange("p (c n) -> p c n", c=6)
        KT = arena[:, base + 3072:base + 6144].rearrange("p (c n) -> p c n", c=6)
        VN = arena[:, base + 6144:base + 8192].rearrange("p (t n) -> p t n", t=NT)
        VR = arena[:, base + 8192:base + 10240].rearrange("p (t n) -> p t n", t=NT)
        SBT = arena[:, base + 10240:base + 12288].rearrange("p (c n) -> p c n", c=4)
        OT_DIL = QT[:, 0:2, :]
        OT_SB = SBT[:, 0:2, :]
        gT = arena[:, 4 * SLOT_W:6 * SLOT_W].rearrange("p (c n) -> p c n", c=2 * KC)
        wbr = arena[:, 2 * SLOT_W:3 * SLOT_W].rearrange("p (b k n) -> p b k n", b=2, k=2)

        xnf = xn[:].rearrange("p t n -> p (t n)")
        ada_slot = xnf[:, 0:2048]
        xg = xnf[:, 2048:3072].rearrange("p (b n) -> p b n", b=2)
        sq = xnf[:, 3072:4096].rearrange("p (b n) -> p b n", b=2)
        sm = xnf[:, 0:2048].rearrange("p (b h n) -> p b h n", b=2, h=NH)
        pT = xnf[:, 2048:4096].rearrange("p (b n) -> p b n", b=2)
        zs, lg1, sp_ = xnf[:, 0:1536], xnf[:, 1280:2816], xnf[:, 2560:4096]
        gate1b = xn[:, NT - 1, :]

        def ada_piece(k):
            at = base + 2048 * k if k < 6 else 5 * SLOT_W + 2048 * (k - 6)
            return arena[:, at:at + 2048]

        def w_gu(b):
            return arena[:, b * EXP_W:b * EXP_W + 2 * SLOT_W].rearrange("p (g k n) -> p g k n", g=2, k=KC)

        def w_dn(b):
            return arena[:, b * EXP_W + 2 * SLOT_W:(b + 1) * EXP_W].rearrange("p (f n) -> p f n", f=FE // P)

        wk = hT[:].rearrange("p c n -> p (c n)")
        xe = wk[:, 0:512]
        xeT = wk[:, 512:1024].rearrange("p (q h s) -> p q h s", q=4, h=2)
        xmul = wk[:, 1024:1536]
        hh = wk[:, 1536:1792]
        hhT = wk[:, 1792:2048].rearrange("p (q n) -> p q n", q=2)
        tsig = wk[:, 2048:2304]
        tden = wk[:, 2304:2560]
        ye = wk[:, 2560:3584].rearrange("p (b n) -> p b n", b=2)
        hot = wk[:, 3584:4096].rearrange("p (b t s) -> p b t s", b=2, t=NT)
        gate2h = modr[:]

        RA = small[:, 0:640]
        A1, A2, AA, RK, RE = (RA[:, 128 * i:128 * i + 128].rearrange("p (t e) -> p t e", t=NT) for i in range(5))
        lg = small[:, 640:784].rearrange("p (t n) -> p t n", t=NT)
        rt = small[:, 784:912]
        slotW = small[:, 912:944]
        slotI = small[:, 944:976].bitcast(I32)

        def oh_view(i):
            return small[:, 976:1104] if i % 2 == 0 else RA[:, 256:384]

        def tb_view(i):
            return rt[:, 64 * (i % 2):64 * (i % 2) + 64]

        rs = trig[:, 0:208]
        sin_arg, trig_k, cos_arg = (grow[:, 64 * i:64 * i + 64].rearrange("p (t f) -> p t f", t=2 * NT)
                                    for i in range(3))
        idx = sb("idx", [P, 1], I32)
        wcol = sb("wcol", [P, 1])
        iot = crep_f[:, 0:2 * CAP].rearrange("p (a s) -> p a s", a=2)
        tokc = crep_f[:, 2 * CAP:2 * CAP + NT]
        halfc = crep_f[:, 2 * CAP + NT:2 * CAP + NT + 1]
        cnt_i = sb("cnt_i", [P, 1], I32)

        ps = ctx.enter_context(nc.psum_tensor("ps", [P, 8, CH], F32))
        psf = ps[:].rearrange("p b n -> p (b n)")

        x_in = [sem(f"x_in{t}") for t in range(NT)]
        pos_in, c_ld, gn_in, gains_in, wr_in = sem("pos_in"), sem("c_ld"), sem("gn_in"), sem("gains_in"), sem("wr_in")
        bias_in = sem("bias_in")
        ada_in = [sem(f"ada_in{k}") for k in range(8)]
        ada2_in = sem("ada2_in")
        win_in = [sem(f"win_in{j}") for j in range(6)]
        wg_in = [sem(f"wg_in{j}") for j in range(4)]
        wo_in = [sem(f"wo_in{j}") for j in range(2)]
        wb_in = sem("wb_in")
        consts = sem("consts")
        slot_consts = sem("slot_consts")
        pool_seq = sem("pool_seq")
        dve_seq = sem("dve_seq")
        act_seq = sem("act_seq")
        gn_T = sem("gn_T")
        crep_ok = sem("crep_ok")
        ada_used = sem("ada_used")
        mod_rows = sem("mod_rows")
        mod_cols = sem("mod_cols")
        row_tile = sem("row_tile")
        gates_kept = sem("gates_kept")
        cols_ok = sem("cols_ok")
        trig_arg, trig_ok = sem("trig_arg"), sem("trig_ok")
        ss_ok, var_ok, seed_ok, xn_ok = sem("ss_ok"), sem("var_ok"), sem("seed_ok"), sem("xn_ok")
        hT_ps, hT_dve, hT_act = sem("hT_ps"), sem("hT_dve"), sem("hT_act")
        proj_done, proj_act, gain_ok = sem("proj_done"), sem("proj_act"), sem("gain_ok")
        rope_ok, qk_ready, qk_tr, qk_stored = sem("rope_ok"), sem("qk_ready"), sem("qk_tr"), sem("qk_stored")
        gate_ps, gate_exp, gate_ok = sem("gate_ps"), sem("gate_exp"), sem("gate_ok")
        sc_ps, sc_max, sc_exp = sem("sc_ps"), sem("sc_max"), sem("sc_exp")
        pT_ps, pT_act, pT_dve = sem("pT_ps"), sem("pT_act"), sem("pT_dve")
        u_ps, u_kept, stats_kept = sem("u_ps"), sem("u_kept"), sem("stats_kept")
        u_out = [sem(f"u_out{i}") for i in range(2)]
        u_back = [sem(f"u_back{i}") for i in range(2)]
        mx_ok, mx_exp, o_ok, oT_ps, oT_ok = sem("mx_ok"), sem("mx_exp"), sem("o_ok"), sem("oT_ps"), sem("oT_ok")
        z_ps, z_abs, z_cp, lnz, sp_ok = sem("z_ps"), sem("z_abs"), sem("z_cp"), sem("lnz"), sem("sp_ok")
        sf_ps, arg_ok, a_ok, osb_ps, osb_ok = sem("sf_ps"), sem("arg_ok"), sem("a_ok"), sem("osb_ps"), sem("osb_ok")
        br_ps, merged = sem("br_ps"), sem("merged")
        g1_ps, g1_ok, o_ps, x1_ok = sem("g1_ps"), sem("g1_ok"), sem("o_ps"), sem("x1_ok")
        ss2_ok, var2_ok, seed2_ok, xn2_ok = sem("ss2_ok"), sem("var2_ok"), sem("seed2_ok"), sem("xn2_ok")
        h2_ps, h2_dve, h2_act, lg_ps = sem("h2_ps"), sem("h2_dve"), sem("h2_act"), sem("lg_ps")
        r_arg, r_exp, rk_in, rk_ps, tb_in, tb_ps, tables_ok = (
            sem("r_arg"), sem("r_exp"), sem("rk_in"), sem("rk_ps"), sem("tb_in"), sem("tb_ps"), sem("tables_ok"))
        g2_ps, g2_ok = sem("g2_ps"), sem("g2_ok")
        gu_in = [sem(f"gu_in{b}") for b in range(NBUF)]
        dn_in = [sem(f"dn_in{b}") for b in range(NBUF)]
        hot_ok, gx_ps, xe_ok, xt_ps, xt_ok = sem("hot_ok"), sem("gx_ps"), sem("xe_ok"), sem("xt_ps"), sem("xt_ok")
        gu_ps, sig_exp, h_ok, ht_ps, ht_ok = sem("gu_ps"), sem("sig_exp"), sem("h_ok"), sem("ht_ps"), sem("ht_ok")
        dn_ps, wcol_ok, idx_ok, y_ok, y_out = sem("dn_ps"), sem("wcol_ok"), sem("idx_ok"), sem("y_ok"), sem("y_out")
        moe_dve = sem("moe_dve")
        round_seq = sem("round_seq")
        y_back = [sem(f"y_back{t}") for t in range(NT)]
        fin_ok, out_st = sem("fin_ok"), sem("out_st")

        block = ctx.enter_context(nc.Block())

        def w_in_cols(ch):
            return {C_SB: [(QB, 512)], C_VNAT: [(VA, GW), (VB, GW)], C_QK0: [(QA, GW), (KA, GW)],
                    C_QRES: [(QA + GW, 512)], C_KRES: [(KA + GW, 512)], C_VRES: [(VA + GW, 512)]}[ch]

        def tokens(ch, t):
            return slice(t, SEQ, NT) if ch in (C_QRES, C_KRES, C_VRES) else slice(t * P, (t + 1) * P)

        NU = 6 * NT
        QK_FIRST, QK_LAST = C_QK0 * NT, C_KRES * NT + NT - 1

        def s_bank(s):
            return 2 * (s % 2)

        def scores_view(s):
            b = s_bank(s)
            return psf[:, b * CH:(b + 2) * CH].rearrange("p (h n) -> p h n", h=NH)

        def place(h):
            return 2 * (h % 2) + h // 2

        def key_from(s):
            return P if s == NT else 0

        def later(e):
            return not isinstance(e, int) or e > 0

        def more_rounds(eng, body):
            eng.wait_ge(tables_ok, 1)
            most = eng.value_load(cnt_i[0:1, 0:1], min_val=0, max_val=SEQ)
            with eng.If(most > CAP):
                with eng.Fori(1, ROUNDS) as rnd:
                    with eng.If(most > rnd * CAP):
                        body(rnd)
            return most

        @block.sync
        def _(sp):
            for t in range(NT):
                sp.dma_start(xs[:, t, :], x[0, t * P:(t + 1) * P, :]).then_inc(x_in[t], 16)
            ada_rows = w_ada[0].rearrange("(p k) n -> p k n", k=KC)
            for k in range(KC):
                sp.dma_start(ada_piece(k), ada_rows[:, k, 0:2048]).then_inc(ada_in[k], 16)

            w_in_r = w_in[0].rearrange("(k p) n -> p k n", p=P)
            w_bg_r = w_branch_gate[0].rearrange("(k p) n -> p k n", p=P)
            for ch in range(6):
                if ch == 5:
                    sp.wait_ge(ada_used, KC)
                at = 0
                for c0, n in w_in_cols(ch):
                    sp.dma_start(wslot(ch)[:, :, at:at + n], w_in_r[:, :, c0:c0 + n]).then_inc(win_in[ch], 16)
                    at += n
                if ch == 2:
                    sp.wait_ge(hT_ps, KC)
                    sp.dma_start(ada_slot, ada_rows[:, 0, 2048:4096]).then_inc(ada2_in, 16)
            for n in range(1, 2 * KC):
                sp.wait_ge(ada_used, KC + n)
                lo = 2048 * (1 + n // KC)
                sp.dma_start(ada_slot, ada_rows[:, n % KC, lo:lo + 2048]).then_inc(ada2_in, 16)
                if n % NT == NT - 1:
                    j = n // NT
                    sp.wait_ge(proj_done, NT * (j + 1))
                    sp.dma_start(wslot(j), w_bg_r[:, :, j * CH:(j + 1) * CH]).then_inc(wg_in[j], 16)
            for j in range(2):
                sp.wait_ge(gate_ps, NT * (j + 1))
                sp.dma_start(wslot(j), w_out[0].rearrange("(k p) n -> p k n", p=P)[:, :, j * CH:(j + 1) * CH]
                             ).then_inc(wo_in[j], 16)
            sp.wait_ge(gate_ps, 3 * NT)
            for b, w in enumerate((w_branch_dil, w_branch_sb)):
                sp.dma_start(wbr[:, b], w[0].rearrange("(k p) n -> p k n", p=P)).then_inc(wb_in, 16)

            def load_gu(e, b):
                for g, w in enumerate((w_expert_gate, w_expert_up)):
                    src = w[0, bass.ds(e, 1)].rearrange("e (k p) n -> p (e k) n", p=P)
                    sp.dma_start(w_gu(b)[:, g], src).then_inc(gu_in[b], 16)

            def load_dn(e, b):
                src = w_expert_down[0, bass.ds(e, 1)].rearrange("e (k p) n -> p (e k) n", p=P)
                sp.dma_start(w_dn(b), src).then_inc(dn_in[b], 16)

            sp.wait_ge(br_ps, KC)
            load_gu(0, 2)
            load_dn(0, 2)
            sp.wait_ge(merged, KC)
            load_gu(1, 1)
            load_dn(1, 1)
            sp.wait_ge(o_ps, 2 * NT)
            load_gu(2, 0)
            load_dn(2, 0)

            def refill(e, b):
                sp.wait_ge(gu_ps, e + 1)
                load_gu(e + NBUF, b)
                sp.wait_ge(dn_ps, e + 1)
                load_dn(e + NBUF, b)

            with sp.Fori(0, 9) as i:
                for j in range(NBUF):
                    refill(i * NBUF + j, NBUF - 1 - j)
            for e in (27, 28):
                refill(e, NBUF - 1 - e % NBUF)


            def sp_round(rnd):
                with sp.Fori(0, NE) as e:
                    sp.wait_ge(dn_ps, rnd * NE + e)
                    load_gu(e, 0)
                    load_dn(e, 0)

            most = more_rounds(sp, sp_round)
            sp.wait_ge(y_out, ((most + (CAP - 1)) // CAP) * (16 * NE))
            for t in range(NT):
                sp.dma_start(arena[:, 2048 * t:2048 * (t + 1)],
                             y_rows[4 * P * t:4 * P * (t + 1), :].rearrange("(p r) n -> p (r n)", r=4)
                             ).then_inc(y_back[t], 16)
            for t in range(NT):
                sp.wait_ge(fin_ok, t + 1)
                sp.dma_start(out[0, t * P:(t + 1) * P, :], xs[:, t, :]).then_inc(out_st, 16)
            sp.wait_ge(out_st, 16 * NT)

        @block.gpsimd
        def _(pool):
            n = [0]

            def link(ins):
                n[0] += 1
                ins.then_inc(pool_seq, 1)
                pool.wait_ge(pool_seq, n[0])

            link(pool.memset(ident[:], 0.0))
            link(pool.affine_select(ident[:], ident[:], [[-1, P]], ALU.not_equal, 1.0, base=0, channel_multiplier=1))
            pool.memset(ones[:], 1.0).then_inc(consts, 1)
            link(pool.memset(strict[:], 0.0))
            pool.affine_select(strict[:], strict[:], [[-1, P]], ALU.is_ge, 1.0, base=0,
                               channel_multiplier=1).then_inc(consts, 1)
            link(pool.memset(tri[:], 0.0))
            pool.affine_select(tri[:], tri[:], [[1, P]], ALU.is_gt, 1.0, base=0,
                               channel_multiplier=-1).then_inc(consts, 1)
            link(pool.memset(small[:, 0:640], 0.0))
            link(pool.affine_select(mask12, mask12, [[0, 2], [-1, P]], ALU.is_ge, NEG, base=0, channel_multiplier=1))
            pool.iota(diff_i, [[-1, P]], base=2 * P, channel_multiplier=1).then_inc(consts, 1)
            link(pool.affine_select(mask0, mask0, [[1, 2 * P]], ALU.is_ge, NEG, base=0, channel_multiplier=-1))
            link(pool.affine_select(mask0, mask0, [[-1, 2 * P]], ALU.is_ge, NEG, base=P, channel_multiplier=1))
            link(pool.affine_select(negstrict, negstrict, [[1, P]], ALU.is_gt, NEG, base=0, channel_multiplier=-1))
            for u in range(QK_FIRST, QK_LAST + 1):
                m, t, ch = u - QK_FIRST, u % NT, u // NT
                tt = t + (NT if ch != C_QK0 else 0)
                v = xg[:, m % 2, :].rearrange("p (h d) -> p h d", h=8)
                xr = v[:, :, 0:ROPE_DIM]
                swp = sq[:, m % 2, 0:128].rearrange("p (h d) -> p h d", h=8)
                csb = cos16[:, tt:tt + 1, :].to_broadcast([P, 8, ROPE_DIM])
                snb = sin16[:, tt:tt + 1, :].to_broadcast([P, 8, ROPE_DIM])
                if m == 0:
                    pool.wait_ge(trig_ok, 3)
                pool.wait_ge(var_ok, 1 + m + 1)
                pool.wait_ge(gain_ok, m + 1)
                pool.tensor_tensor(swp[:, :, 0:HALF], xr[:, :, HALF:ROPE_DIM], snb[:, :, 0:HALF],
                                   ALU.mult).then_inc(pool_seq, 1)
                pool.tensor_tensor(swp[:, :, HALF:ROPE_DIM], xr[:, :, 0:HALF], snb[:, :, HALF:ROPE_DIM],
                                   ALU.mult).then_inc(pool_seq, 1)
                n[0] += 2
                pool.wait_ge(pool_seq, n[0])
                link(pool.tensor_tensor(xr, xr, csb, ALU.mult))
                pool.tensor_tensor(xr, xr, swp, ALU.add).then_inc(rope_ok, 1)

            pool.wait_ge(ada_used, 3 * KC)
            pool.iota(iot[:], [[0, 2], [1, CAP]], base=0, channel_multiplier=0,
                      allow_small_or_imprecise_dtypes=True).then_inc(slot_consts, 1)
            pool.iota(tokc[:], [[2 * P, NT]], base=-int(UNUSED), channel_multiplier=2,
                      allow_small_or_imprecise_dtypes=True).then_inc(slot_consts, 1)
            link(pool.memset(halfc[:, :], 2 * UNUSED))
            pool.wait_ge(slot_consts, 2)
            pool.memset(halfc[64:128, :], 2 * UNUSED + 1).then_inc(slot_consts, 1)
            pool.wait_ge(slot_consts, 3)

            rows = dil_rows.rearrange("(a r) n -> r a n", r=NT)
            for r in range(NT):
                pool.wait_ge(u_kept, r + 1)
                pool.wait_ge(stats_kept, r + 1)
                pool.dma_start(rows[r], ustage[:, r % 2, :]).then_inc(u_out[r % 2], 16)
            for b in range(2):
                pool.wait_ge(u_out[b], 32)
            for i in range(NT):
                if i >= 2:
                    pool.wait_ge(o_ok, i - 1)
                pool.dma_start(ustage[:, i % 2, :], dil_rows[i * P:(i + 1) * P, :]).then_inc(u_back[i % 2], 16)

            pool.wait_ge(tables_ok, 1)

            last_row = pool.to_reg(4 * SEQ - 1)

            def store(e, b, n=None):
                n = e if n is None else n
                pool.wait_ge(y_ok, n + 1)
                if later(n):
                    pool.wait_ge(y_out, n * 16)
                pool.tensor_copy(idx[:], slotI[:, bass.ds(e, 1)]).then_inc(idx_ok, 1)
                pool.wait_ge(tables_ok, 1)
                pool.wait_ge(idx_ok, n + 1)
                pool.indirect_dma_start(
                    out=y_rows, out_offset=bass.IndirectOffsetOnAxis(ap=idx[:, 0:1], axis=0),
                    in_=ye[:, b, :], in_offset=None, bounds_check=last_row, oob_is_err=False,
                ).then_inc(y_out, 16)

            store(0, 0)
            with pool.Fori(0, (NE - 2) // 2) as i:
                for j in range(2):
                    store(i * 2 + (1 + j), 1 - j)
            store(NE - 1, 1)

            def pool_round(rnd):
                with pool.Fori(0, NE) as e:
                    pool.wait_ge(tables_ok, rnd + 1)
                    store(e, 0, rnd * NE + e)

            more_rounds(pool, pool_round)

        @block.tensor
        def _(pe):
            pe.wait_ge(consts, 4)
            pe.wait_ge(gn_in, 32)
            pe.transpose(ps[:, 5, 0:16], gn_rows, ident[0:16, 0:16]).then_inc(gn_T, 1)

            def ada(lhs_k, rhs, first, last):
                for j in range(4):
                    mm = pe.matmul(ps[32 * j:32 * j + 32, 7, :], crep[:, lhs_k, :], rhs[:, j * CH:(j + 1) * CH],
                                   start=first, stop=last, tile_position=(0, 32 * j))
                mm.then_inc(ada_used, 1)

            col_steps = [0]

            def mod_columns(r, js, at):
                pe.wait_ge(mod_rows, r + 1)
                for i, j in enumerate(js):
                    if i > 0:
                        col_steps[0] += 1
                        mm.then_inc(row_tile, 1)
                        pe.wait_ge(row_tile, col_steps[0])
                    for q in range(4):
                        mm = pe.matmul(ps[:, 6, at + 4 * i + q:at + 4 * i + q + 1],
                                       modr[32 * j:32 * j + 1, q * P:(q + 1) * P],
                                       ones[32 * j:32 * j + 1, 0:1], start=True, stop=True)
                mm.then_inc(mod_cols, 1)

            pe.wait_ge(crep_ok, 1)
            for k in range(KC):
                pe.wait_ge(ada_in[k], 16)
                ada(k, ada_piece(k), k == 0, k == KC - 1)
            mod_columns(0, (0, 1, 2, 3), 0)

            for cc in range(KC):
                if cc == 0:
                    pe.wait_ge(xn_ok, NT)
                if cc >= 4:
                    pe.wait_ge(hT_dve if cc % 2 == 0 else hT_act, (cc - 4) // 2 + 1)
                for t in range(NT):
                    mm = pe.transpose(ps[:, cc % 4, t * P:(t + 1) * P], xn[:, t, cc * P:(cc + 1) * P], ident[:])
                mm.then_inc(hT_ps, 1)

            def transposes_of(u):
                m = u - QK_FIRST
                pe.wait_ge(qk_ready, m + 1)
                if m >= 2:
                    pe.wait_ge(qk_stored, m - 1)
                for q in range(4):
                    mm = pe.transpose(ps[:, 4 + m % 2, q * P:(q + 1) * P], xg[:, m % 2, q * P:(q + 1) * P], ident[:])
                mm.then_inc(qk_tr, 1)

            for u in range(NU):
                ch, t = divmod(u, NT)
                if t == 0:
                    pe.wait_ge(win_in[ch], 16 * len(w_in_cols(ch)))
                if u == 0:
                    pe.wait_ge(hT_dve, KC // 2)
                    pe.wait_ge(hT_act, KC // 2)
                if u >= 3:
                    pe.wait_ge(proj_act, u - 2)
                    if QK_FIRST <= u - 3 <= QK_LAST:
                        pe.wait_ge(gain_ok, u - 3 - QK_FIRST + 1)
                for k in range(KC):
                    if ch == C_SB:
                        lhsT, rhs = wslot(ch)[:, k, t * P:(t + 1) * P], hT[:, k, :]
                    else:
                        lhsT, rhs = hT[:, k, tokens(ch, t)], wslot(ch)[:, k, :]
                    mm = pe.matmul(ps[:, u % 3, :], lhsT, rhs, start=(k == 0), stop=(k == KC - 1))
                mm.then_inc(proj_done, 1)
                if u < 2 * KC:
                    if u == 0:
                        pe.wait_ge(mod_rows, 1)
                    if u == KC:
                        mod_columns(1, (2, 3), 16)
                    pe.wait_ge(ada2_in, 16 * (u + 1))
                    ada(u % KC, ada_slot, u % KC == 0, u % KC == KC - 1)
                if u == 2 * KC:
                    mod_columns(2, (0, 1), 24)
                if QK_FIRST <= u - 1 <= QK_LAST:
                    transposes_of(u - 1)

            def gate(f):
                if f % NT == 0:
                    pe.wait_ge(wg_in[f // NT], 16)
                if f >= 2:
                    pe.wait_ge(gate_exp, f - 1)
                for k in range(KC):
                    mm = pe.matmul(ps[:, 6 + f % 2, :], wslot(f // NT)[:, k, (f % NT) * P:(f % NT + 1) * P],
                                   hT[:, k, :], start=(k == 0), stop=(k == KC - 1))
                mm.then_inc(gate_ps, 1)

            def scores(s):
                if s == 0:
                    pe.wait_ge(qk_stored, QK_LAST - QK_FIRST + 1)
                    pe.wait_ge(proj_act, NU)
                if s >= 2:
                    pe.wait_ge(pT_act, s - 1)
                    pe.wait_ge(pT_dve, s - 1)
                S = scores_view(s)
                for h in range(NH):
                    o = HD * (h % 2)
                    w = place(h)
                    if s < NT:
                        for g in range(2):
                            pair = 2 + 2 * g + h // 2
                            mm = pe.matmul(S[:, w, g * P:(g + 1) * P], QT[o:o + HD, pair, s * P:(s + 1) * P],
                                           KT[o:o + HD, pair, s * P:(s + 1) * P], start=True, stop=True)
                    else:
                        i, k0 = s - NT, key_from(s)
                        mm = pe.matmul(S[:, w, k0:2 * P], QT[o:o + HD, h // 2, i * P:(i + 1) * P],
                                       KT[o:o + HD, h // 2, (i - 1) * P + k0:(i + 1) * P], start=True, stop=True)
                mm.then_inc(sc_ps, 1)

            def transpose_probs(s):
                pe.wait_ge(sc_exp, s + 1)
                b = s_bank(s)
                for h in range(NH):
                    for g in range(key_from(s) // P, 2):
                        mm = pe.transpose(psf[:, b * CH + (2 * h + g) * P:b * CH + (2 * h + g + 1) * P],
                                          sm[:, s % 2, h, g * P:(g + 1) * P], ident[:])
                mm.then_inc(pT_ps, 1)

            def values(s):
                pe.wait_ge(pT_act, s + 1)
                pe.wait_ge(pT_dve, s + 1)
                if s >= 2:
                    pe.wait_ge(u_kept, s - 1)
                if s - 2 >= NT:
                    pe.wait_ge(oT_ok, s - 1 - NT)
                for h in range(NH):
                    gs = range(key_from(s) // P, 2)
                    for g in gs:
                        if s < NT:
                            v = VR[:, s, g * GW + h * HD:g * GW + (h + 1) * HD]
                        else:
                            v = VN[:, s - NT - 1 + g, h * HD:(h + 1) * HD]
                        w = place(h)
                        mm = pe.matmul(ps[:, 4 + s % 2, w * HD:(w + 1) * HD],
                                       pT[:, s % 2, (2 * w + g) * P:(2 * w + g + 1) * P], v,
                                       start=(g == gs[0]), stop=(g == 1))
                mm.then_inc(u_ps, 1)

            def out_transposes(i):
                pe.wait_ge(o_ok, i + 1)
                for q in range(2):
                    mm = pe.transpose(ps[:, 4 + i % 2, 256 + q * P:256 + (q + 1) * P],
                                      o_dil[:, q * P:(q + 1) * P], ident[:])
                mm.then_inc(oT_ps, 1)

            scores(0)
            for s in range(2 * NT):
                gate(s)
                transpose_probs(s)
                if s + 1 < 2 * NT:
                    scores(s + 1)
                if s >= 1:
                    values(s - 1)
                if s - 2 >= NT:
                    out_transposes(s - 2 - NT)

            def sb_z(h):
                b = 3 * (h % 2)
                if h == 0:
                    pe.wait_ge(pT_act, 2 * NT)
                    pe.wait_ge(pT_dve, 2 * NT)
                if h == 1:
                    pe.wait_ge(oT_ok, NT)
                if h >= 2:
                    pe.wait_ge(osb_ok, h - 1)
                o = HD * (h % 2)
                for j in range(NT):
                    a = b * CH + SB_OFF[j]
                    mm = pe.matmul(psf[:, a:a + SEQ - j * P], SBT[o:o + HD, 2 + h // 2, j * P:(j + 1) * P],
                                   SBT[o:o + HD, h // 2, j * P:SEQ], start=True, stop=True)
                mm.then_inc(z_ps, 1)

            def sb_suffix(h):
                b = 3 * (h % 2)
                pe.wait_ge(sp_ok, h + 1)
                for j in range(NT):
                    for j2 in range(j, NT):
                        a = b * CH + SB_OFF[j] + (j2 - j) * P
                        mm = pe.matmul(psf[:, a:a + SEQ - j2 * P], (tri if j2 == j else ones)[:],
                                       sp_[:, SB_OFF[j2]:SB_OFF[j2] + SEQ - j2 * P],
                                       start=(j2 == j), stop=(j2 == NT - 1), skip_group_check=True)
                mm.then_inc(sf_ps, 1)

            def sb_values(h):
                pe.wait_ge(a_ok, h + 1)
                o = HD * (h % 2)
                for j in range(NT):
                    mm = pe.matmul(ps[o:o + HD, 3 * (h % 2), j * P:SEQ], VN[:, j, GW + h * HD:GW + (h + 1) * HD],
                                   zs[:, SB_OFF[j]:SB_OFF[j] + SEQ - j * P], start=(j == 0), stop=(j == NT - 1),
                                   skip_group_check=True)
                mm.then_inc(osb_ps, 1)

            gate(8)
            values(2 * NT - 1)
            out_transposes(2)
            sb_z(0)
            gate(9)
            out_transposes(3)
            for h in range(NH):
                sb_suffix(h)
                if h + 1 < NH:
                    sb_z(h + 1)
                    gate(10 + 2 * h)
                sb_values(h)
                if h + 1 < NH:
                    gate(11 + 2 * h)

            pe.wait_ge(gate_exp, 2 * KC)
            pe.wait_ge(gates_kept, 2)
            for j in range(2):
                mm = pe.matmul(ps[:, 6 + j, :], ones[32 * j:32 * j + 1, :], grow[32 * j:32 * j + 1, :],
                               start=True, stop=True)
            mm.then_inc(g1_ps, 1)
            pe.wait_ge(wb_in, 32)
            pe.wait_ge(osb_ok, NH)
            for f in range(KC):
                if f >= 2:
                    pe.wait_ge(merged, f - 1)
                for b, oT in enumerate((OT_DIL, OT_SB)):
                    for k in range(2):
                        mm = pe.matmul(ps[:, 2 * (f % 2) + b, :], wbr[:, b, k, f * P:(f + 1) * P], oT[:, k, :],
                                       start=(k == 0), stop=(k == 1))
                mm.then_inc(br_ps, 1)
            pe.wait_ge(merged, KC)
            for u in range(2 * NT):
                t, j = divmod(u, 2)
                if u < 2:
                    pe.wait_ge(wo_in[j], 16)
                if u >= 2:
                    pe.wait_ge(x1_ok, u - 1)
                for k in range(KC):
                    mm = pe.matmul(ps[:, 4 + j, :], hT[:, k, t * P:(t + 1) * P], wslot(j)[:, k, :],
                                   start=(k == 0), stop=(k == KC - 1))
                mm.then_inc(o_ps, 1)

            pe.wait_ge(g1_ok, 2)
            for j in range(2):
                r = 64 + 32 * j
                mm = pe.matmul(ps[64 * j:64 * j + 64, 6, :], ones[r:r + 1, 0:64], grow[r:r + 1, :],
                               start=True, stop=True)
            mm.then_inc(g2_ps, 1)
            for cc in range(KC):
                if cc == 0:
                    pe.wait_ge(xn2_ok, NT)
                if cc >= 4:
                    pe.wait_ge(h2_dve if cc % 2 == 0 else h2_act, (cc - 4) // 2 + 1)
                for t in range(NT):
                    mm = pe.transpose(ps[:, cc % 4, t * P:(t + 1) * P], xn[:, t, cc * P:(cc + 1) * P], ident[:])
                mm.then_inc(h2_ps, 1)
            pe.wait_ge(h2_dve, KC // 2)
            pe.wait_ge(h2_act, KC // 2)
            pe.wait_ge(wr_in, 16 * 4)
            NR = NG + NE
            for t in range(NT):
                for k in range(KC):
                    pe.matmul(ps[:, 4, t * NR:(t + 1) * NR], hT[:, k, t * P:(t + 1) * P], wr[:, k, :],
                              start=(k == 0), stop=False)
                mm = pe.matmul(ps[:, 4, t * NR:(t + 1) * NR], ones[0:1, :], br[:], start=False, stop=True)
            mm.then_inc(lg_ps, 1)
            def slot_tables(done):
                for i in range(2 * NT):
                    pe.wait_ge(tb_in, done + i + 1)
                    mm = pe.matmul(ps[:, 7, 0:2 * NE], oh_view(i), tb_view(i), start=(i == 0), stop=(i == 2 * NT - 1))
                    mm.then_inc(tb_ps, 1)

            pe.wait_ge(rk_in, 1)
            for t in range(NT):
                for t2 in range(t + 1):
                    pe.matmul(ps[:, 5, t * NE:(t + 1) * NE], (strict if t2 == t else ones)[:], AA[:, t2, :],
                              start=(t2 == 0), stop=(t2 == t))
            for t in range(NT):
                mm = pe.matmul(ps[:, 5, 4 * NE:5 * NE], ones[:], AA[:, t, :], start=(t == 0), stop=(t == NT - 1))
            mm.then_inc(rk_ps, 1)
            slot_tables(0)

            def gather(e, hb):
                pe.wait_ge(hot_ok, e + 1)
                if later(e):
                    pe.wait_ge(xe_ok, e)
                for t in range(NT):
                    for h in range(2):
                        mm = pe.matmul(ps[64 * h:64 * h + 64, 0, :], hot[:, hb, t, :],
                                       xn[:, t, h * CH:(h + 1) * CH], start=(t == 0), stop=(t == NT - 1),
                                       skip_group_check=True)
                mm.then_inc(gx_ps, 1)

            def transpose_x(e):
                pe.wait_ge(xe_ok, e + 1)
                if later(e):
                    pe.wait_ge(xt_ok, e)
                for q in range(4):
                    mm = pe.transpose(ps[:, 1, q * P:(q + 1) * P], xe[:, q * P:(q + 1) * P], ident[:])
                mm.then_inc(xt_ps, 1)

            def gate_up(e, b, loads):
                pe.wait_ge(gu_in[b], loads * 32)
                pe.wait_ge(xt_ok, e + 1)
                if later(e):
                    pe.wait_ge(h_ok, e)
                for k in range(KC):
                    for h in range(2):
                        mm = pe.matmul(ps[64 * h:64 * h + 64, 2, :], xeT[:, k % 4, k // 4, :],
                                       w_gu(b)[:, :, k, 256 * h:256 * h + 256], start=(k == 0),
                                       stop=(k == KC - 1), skip_group_check=True)
                mm.then_inc(gu_ps, 1)

            def transpose_h(e):
                pe.wait_ge(h_ok, e + 1)
                for q in range(2):
                    mm = pe.transpose(ps[:, 3, q * P:(q + 1) * P], hh[:, q * P:(q + 1) * P], ident[:])
                mm.then_inc(ht_ps, 1)

            def down(e, b, loads):
                pe.wait_ge(dn_in[b], loads * 16)
                pe.wait_ge(ht_ok, e + 1)
                if later(e):
                    pe.wait_ge(y_ok, e)
                for f in range(FE // P):
                    for h in range(2):
                        mm = pe.matmul(ps[64 * h:64 * h + 64, 4, :],
                                       hhT[:, f % 2, 64 * (f // 2):64 * (f // 2) + 64],
                                       w_dn(b)[:, f, h * CH:(h + 1) * CH], start=(f == 0),
                                       stop=(f == FE // P - 1), skip_group_check=True)
                mm.then_inc(dn_ps, 1)

            def expert(e, b, hb, loads, more=True):
                gate_up(e, b, loads)
                if more:
                    gather(e + 1, 1 - hb)
                transpose_h(e)
                if more:
                    transpose_x(e + 1)
                down(e, b, loads)

            gather(0, 0)
            transpose_x(0)
            expert(0, NBUF - 1, 0, 1)
            with pe.Fori(0, (NE - 2) // (2 * NBUF)) as i:
                for j in range(1, 2 * NBUF + 1):
                    expert(i * (2 * NBUF) + j, NBUF - 1 - j % NBUF, j % 2, i * 2 + (j // NBUF + 1))
            expert(NE - 1, NBUF - 1 - (NE - 1) % NBUF, 1, (NE - 1) // NBUF + 1, more=False)

            def pe_round(rnd):
                slot_tables(rnd * (2 * NT))
                with pe.Fori(0, NE) as e:
                    k = rnd * NE + e
                    gather(k, 0)
                    transpose_x(k)
                    gate_up(k, 0, rnd * NE + (e - (NE - 11)))
                    transpose_h(k)
                    down(k, 0, rnd * NE + (e - (NE - 11)))

            more_rounds(pe, pe_round)

        @block.scalar
        def _(act):
            n = [0]

            def link(ins):
                n[0] += 1
                ins.then_inc(act_seq, 1)
                act.wait_ge(act_seq, n[0])

            with nc.allow_non_contiguous_dma(reason="512 positions, by token tile"):
                act.dma_start(pos_i[:, 0:NT], positions[0].rearrange("(t p) -> p t", p=P)).then_inc(pos_in, 16)
            act.dma_start(pos_i[:, NT:2 * NT], positions[0].rearrange("(p r) -> p r", r=NT)).then_inc(pos_in, 16)
            act.dma_start(c_in[:], c[0].rearrange("(p k) -> p k", k=KC)).then_inc(c_ld, 16)
            for i, g in enumerate((g_norm_mix, g_norm_ffn)):
                act.dma_start(gn_rows[8 * i:8 * i + 8, :], g[0].rearrange("(k p) -> k p", p=P)
                              ).then_inc(gn_in, 16)

            def load_bias(r):
                for j in range(4):
                    lo = 2048 * r + CH * j
                    act.dma_start(modr[32 * j:32 * j + 32, :],
                                  b_ada[0:1, lo:lo + CH].to_broadcast([32, CH])).then_inc(bias_in, 16)

            load_bias(0)
            for i, g in enumerate((q_norm_g, k_norm_g)):
                act.dma_start(gains[:, i, :], g[0:1, :].to_broadcast([P, HD])).then_inc(gains_in, 16)
            act.dma_start(wr[:, :, 0:NG], w_router_group[0].rearrange("(k p) n -> p k n", p=P)).then_inc(wr_in, 16)
            act.dma_start(wr[:, :, NG:], w_router_expert[0].rearrange("(k p) n -> p k n", p=P)).then_inc(wr_in, 16)
            act.dma_start(br[:, 0:NG], b_router_group).then_inc(wr_in, 16)
            act.dma_start(br[:, NG:], b_router_expert).then_inc(wr_in, 16)

            act.wait_ge(trig_arg, 1)
            act.activation(cos16[:, :, 0:HALF], cos_arg, ACT.Sin).then_inc(trig_ok, 1)
            act.activation(sin16[:, :, HALF:ROPE_DIM], sin_arg, ACT.Sin).then_inc(trig_ok, 1)
            act.wait_ge(c_ld, 16)
            act.activation(st[:, 0:KC], c_in[:], ACT.Exp, scale=-1.0).then_inc(act_seq, 1)
            n[0] += 1
            for t in range(NT):
                act.wait_ge(x_in[t], 16)
                act.activation(xn[:, t, :], xs[:, t, :], ACT.Square, accum_out=st[:, 16 + t:17 + t]
                               ).then_inc(ss_ok, 1)

            def seed(v, y, ready, count, done):
                act.wait_ge(ready, count)
                link(act.activation(y, v, ACT.Ln))
                act.activation(y, y, ACT.Exp, scale=-0.5).then_inc(done, 1)

            seed(st[:, 20:24], st[:, 24:28], var_ok, 1, seed_ok)

            def to_hT(stored, cc, a, b, ready):
                act.wait_ge(ready, cc + 1)
                act.activation(hT[:, cc, :], ps[:, cc % 4, :], ACT.Identity, scale=cols[:, a, cc:cc + 1],
                               bias=cols[:, b, cc:cc + 1]).then_inc(stored, 1)

            act.wait_ge(cols_ok, 1)
            for cc in range(1, KC, 2):
                to_hT(hT_act, cc, 0, 1, hT_ps)
            for r in (1,):
                act.wait_ge(mod_cols, r)
                load_bias(r)

            def store_qk(u):
                m, t, ch = u - QK_FIRST, u % NT, u // NT
                act.wait_ge(qk_tr, m + 1)
                src = ps[:, 4 + m % 2, :].rearrange("p (c n) -> p c n", c=4)
                if ch == C_QK0:
                    act.activation(QT[:, 0:2, t * P:(t + 1) * P], src[:, 0:2, :], ACT.Copy).then_inc(act_seq, 1)
                    n[0] += 1
                    act.wait_ge(act_seq, n[0])
                    act.activation(KT[:, 0:2, t * P:(t + 1) * P], src[:, 2:4, :], ACT.Copy).then_inc(qk_stored, 1)
                else:
                    dst = QT if ch == C_QRES else KT
                    act.activation(dst[:, 2:6, t * P:(t + 1) * P], src, ACT.Copy).then_inc(qk_stored, 1)

            for u in range(NU):
                ch, t = divmod(u, NT)
                act.wait_ge(proj_done, u + 1)
                bank = ps[:, u % 3, :]
                if ch == C_SB:
                    act.activation(SBT[:, t, :], bank, ACT.Copy, scale=HD ** -0.5 if t < 2 else 1.0
                                   ).then_inc(proj_act, 1)
                elif ch == C_VNAT:
                    act.activation(VN[:, t, :], bank, ACT.Copy).then_inc(proj_act, 1)
                elif ch == C_VRES:
                    act.activation(VR[:, t, :], bank, ACT.Copy).then_inc(proj_act, 1)
                else:
                    m = u - QK_FIRST
                    if m >= 2:
                        act.wait_ge(rope_ok, m - 1)
                    act.activation(sq[:, m % 2, :], bank, ACT.Square).then_inc(proj_act, 1)
                    seed(st[:, 32:40], st[:, 40:48], var_ok, 1 + m + 1, seed_ok)
                if u == KC + 1:
                    act.wait_ge(mod_cols, 2)
                    act.wait_ge(gates_kept, 1)
                    load_bias(2)
                if QK_FIRST <= u - 1 <= QK_LAST:
                    store_qk(u - 1)

            def gate_exp_(f):
                act.wait_ge(gate_ps, f + 1)
                act.activation(gT[:, f, :], ps[:, 6 + f % 2, :], ACT.Exp, scale=-1.0).then_inc(gate_exp, 1)

            def softmax_exp(s):
                act.wait_ge(sc_max, s + 1)
                k0 = key_from(s)
                for h in range(NH):
                    ins = act.activation(sm[:, s % 2, h, k0:], sm[:, s % 2, h, k0:], ACT.Exp,
                                         bias=stat(s)[:, 8 + h:9 + h], accum_out=stat(s)[:, h:h + 1])
                    if h < NH - 1:
                        link(ins)
                ins.then_inc(sc_exp, 1)

            def probs_store(s):
                act.wait_ge(pT_ps, s + 1)
                if s >= 2:
                    act.wait_ge(u_ps, s - 1)
                b, k0 = s_bank(s), key_from(s)
                src = ps[:, b, :].rearrange("p (h n) -> p h n", h=2)[:, :, k0:]
                dst = pT[:, s % 2, 0:CH].rearrange("p (h n) -> p h n", h=2)[:, :, k0:]
                act.activation(dst, src, ACT.Copy).then_inc(pT_act, 1)

            def mix_exp(i):
                act.wait_ge(mx_ok, i + 1)
                act.activation(cstat(i)[:, 0:8], cstat(i)[:, 0:8], ACT.Exp).then_inc(mx_exp, 1)

            for s in range(2 * NT):
                softmax_exp(s)
                gate_exp_(s)
                probs_store(s)
                if s >= NT + 1:
                    mix_exp(s - NT - 1)
            gate_exp_(8)
            mix_exp(NT - 1)

            def sb_logs(h):
                act.wait_ge(z_ps, h + 1)
                a = lg1[:, 0:SB_COLS]
                b = 3 * (h % 2) * CH
                if h == 0:
                    act.wait_ge(u_ps, 2 * NT)
                act.activation(a, psf[:, b:b + SB_COLS], ACT.Abs).then_inc(z_abs, 1)
                act.wait_ge(z_abs, h + 1)
                link(act.activation(a, a, ACT.Exp, scale=-1.0))
                act.activation(a, a, ACT.Ln, bias=1.0).then_inc(lnz, 1)

            def sb_exp(h):
                act.wait_ge(arg_ok, h + 1)
                act.activation(zs[:, 0:SB_COLS], zs[:, 0:SB_COLS], ACT.Exp).then_inc(a_ok, 1)

            def sb_store(h):
                o = HD * (h % 2)
                act.wait_ge(osb_ps, h + 1)
                act.activation(OT_SB[o:o + HD, h // 2, :], ps[o:o + HD, 3 * (h % 2), :], ACT.Copy
                               ).then_inc(osb_ok, 1)

            sb_logs(0)
            gate_exp_(9)
            for h in range(NH):
                sb_exp(h)
                if h + 1 < NH:
                    sb_logs(h + 1)
                    gate_exp_(10 + 2 * h)
                sb_store(h)
                if h + 1 < NH:
                    gate_exp_(11 + 2 * h)

            act.wait_ge(g1_ps, 1)
            for j in range(2):
                act.activation(gate1b[:, j * CH:(j + 1) * CH], ps[:, 6 + j, :], ACT.Copy).then_inc(g1_ok, 1)

            for t in range(NT):
                act.wait_ge(x1_ok, 2 * t + 2)
                act.activation(xn[:, t, :], xs[:, t, :], ACT.Square, accum_out=st[:, 16 + t:17 + t]
                               ).then_inc(ss2_ok, 1)
                seed(st[:, 20 + t:21 + t], st[:, 24 + t:25 + t], var2_ok, t + 1, seed2_ok)
            act.wait_ge(g2_ps, 1)
            act.activation(gate2h, ps[:, 6, :], ACT.Copy).then_inc(g2_ok, 1)
            for cc in range(1, KC, 2):
                to_hT(h2_act, cc, 2, 3, h2_ps)
            act.wait_ge(r_arg, 1)
            act.activation(rs[:, 0:16], rs[:, 0:16], ACT.Exp).then_inc(r_exp, 1)
            act.wait_ge(r_arg, 2)
            act.activation(rs[:, 40:44], rs[:, 40:44], ACT.Exp).then_inc(r_exp, 1)

            def store_x(e):
                act.wait_ge(gx_ps, e + 1)
                if later(e):
                    act.wait_ge(xt_ps, e)
                act.activation(xe, ps[:, 0, :], ACT.Copy).then_inc(xe_ok, 1)

            def sig(e):
                act.wait_ge(gu_ps, e + 1)
                act.activation(tsig, ps[:, 2, 0:256], ACT.Exp, scale=-1.0).then_inc(sig_exp, 1)

            def expert(e, more=True):
                sig(e)
                if more:
                    store_x(e + 1)

            store_x(0)
            expert(0)
            with act.Fori(1, NE - 1) as e:
                expert(e)
            sig(NE - 1)

            def act_round(rnd):
                with act.Fori(0, NE) as e:
                    store_x(rnd * NE + e)
                    sig(rnd * NE + e)

            more_rounds(act, act_round)

        @block.vector
        def _(dve):
            n = [0]

            def link(ins):
                n[0] += 1
                ins.then_inc(dve_seq, 1)
                dve.wait_ge(dve_seq, n[0])

            dve.wait_ge(consts, 4)
            dve.wait_ge(pool_seq, 8)
            link(dve.tensor_scalar(diff_i, diff_i, 3, None, ALU.bitwise_and))
            link(dve.tensor_scalar(diff_m, diff_i, 0.0, NEG, ALU.not_equal, ALU.mult))
            link(dve.tensor_tensor(mask12[:, 1, :], mask12[:, 1, :], diff_m, ALU.add))

            dve.wait_ge(pos_in, 32)
            A, K, C = sin_arg, trig_k, cos_arg
            link(dve.tensor_copy(grow[:, 192:200], pos_i[:]))
            for f in range(HALF):
                dve.memset(grow[:, 200 + f:201 + f], float(inv_freq[f])).then_inc(dve_seq, 1)
                n[0] += 1
            dve.wait_ge(dve_seq, n[0])
            link(dve.tensor_tensor(A, grow[:, 192:200].unsqueeze(2).to_broadcast([P, 2 * NT, HALF]),
                                   grow[:, 200:208].unsqueeze(1).to_broadcast([P, 2 * NT, HALF]), ALU.mult))
            magic = 1.5 * 2.0 ** 23
            link(dve.tensor_scalar(K, A, float(1 / (2 * np.pi)), magic, ALU.mult, ALU.add))
            link(dve.tensor_scalar(K, K, magic, None, ALU.subtract))
            for part in two_pi_parts():
                link(dve.scalar_tensor_tensor(out=A, in0=K, scalar=-part, in1=A, op0=ALU.mult, op1=ALU.add))
            link(dve.tensor_scalar(C, A, float(np.pi / 2), None, ALU.add))
            link(dve.tensor_scalar(K, C, float(np.pi), -2 * float(np.pi), ALU.is_gt, ALU.mult))
            link(dve.tensor_tensor(C, C, K, ALU.add))
            pi_in = float(np.nextafter(np.float32(np.pi), np.float32(0)))
            link(dve.tensor_scalar(C, C, pi_in, -pi_in, ALU.min, ALU.max))
            dve.tensor_scalar(A, A, pi_in, -pi_in, ALU.min, ALU.max).then_inc(trig_arg, 1)
            dve.wait_ge(trig_ok, 2)
            link(dve.tensor_copy(cos16[:, :, HALF:], cos16[:, :, 0:HALF]))
            dve.tensor_scalar(sin16[:, :, 0:HALF], sin16[:, :, HALF:], -1.0, None, ALU.mult).then_inc(trig_ok, 1)

            dve.wait_ge(act_seq, 1)
            link(dve.tensor_scalar(st[:, 0:8], st[:, 0:8], 1.0, None, ALU.add))
            link(dve.reciprocal(st[:, 0:8], st[:, 0:8]))
            link(dve.tensor_tensor(st[:, 0:8], st[:, 0:8], c_in[:], ALU.mult))
            dve.tensor_copy(crep[:], st[:, 0:8].unsqueeze(2).to_broadcast([P, KC, 32])).then_inc(crep_ok, 1)
            dve.wait_ge(gn_T, 1)
            link(dve.tensor_copy(gn[:], ps[:, 5, 0:16].rearrange("p (g k) -> p g k", g=2)))
            dve.wait_ge(gains_in, 32)
            link(dve.tensor_scalar(gains[:, 0, :], gains[:, 0, :], HD ** -0.5, None, ALU.mult))

            def refine(v, y, tmp):
                link(dve.tensor_tensor(tmp, y, y, ALU.mult))
                link(dve.scalar_tensor_tensor(out=tmp, in0=tmp, scalar=-0.5, in1=v, op0=ALU.mult, op1=ALU.mult))
                link(dve.scalar_tensor_tensor(out=y, in0=tmp, scalar=1.5, in1=y, op0=ALU.add, op1=ALU.mult))

            dve.wait_ge(ss_ok, NT)
            dve.tensor_scalar(st[:, 20:24], st[:, 16:20], 1.0 / D, RMS_EPS, ALU.mult, ALU.add).then_inc(var_ok, 1)
            dve.wait_ge(seed_ok, 1)
            refine(st[:, 20:24], st[:, 24:28], st[:, 28:32])
            for t in range(NT):
                dve.tensor_scalar(xn[:, t, :], xs[:, t, :], st[:, 24 + t:25 + t], None, ALU.mult).then_inc(xn_ok, 1)

            def mod_round(r):
                dve.wait_ge(ada_used, KC * (r + 1))
                dve.wait_ge(bias_in, 64 * (r + 1))
                dve.tensor_tensor(modr[:], modr[:], ps[:, 7, :], ALU.add).then_inc(mod_rows, 1)
                dve.wait_ge(mod_rows, r + 1)
                if r == 1:
                    dve.tensor_copy(grow[0:64, :], modr[0:64, :]).then_inc(gates_kept, 1)
                if r == 2:
                    dve.tensor_copy(grow[64:128, :], modr[64:128, :]).then_inc(gates_kept, 1)

            mod_round(0)
            dve.wait_ge(mod_cols, 1)
            link(dve.tensor_copy(cols[:, 1, :], ps[:, 6, 0:8]))
            dve.scalar_tensor_tensor(out=cols[:, 0, :], in0=ps[:, 6, 8:16], scalar=1.0, in1=gn[:, 0, :],
                                     op0=ALU.add, op1=ALU.mult).then_inc(cols_ok, 1)
            dve.wait_ge(cols_ok, 1)

            def to_hT(stored, cc, a, b, ready):
                dve.wait_ge(ready, cc + 1)
                dve.tensor_scalar(hT[:, cc, :], ps[:, cc % 4, :], cols[:, a, cc:cc + 1], cols[:, b, cc:cc + 1],
                                  ALU.mult, ALU.add).then_inc(stored, 1)

            for cc in range(0, KC, 2):
                to_hT(hT_dve, cc, 0, 1, hT_ps)

            for u in range(NU):
                ch, t = divmod(u, NT)
                if QK_FIRST <= u <= QK_LAST:
                    m = u - QK_FIRST
                    dve.wait_ge(proj_act, u + 1)
                    if m >= 2:
                        dve.wait_ge(qk_tr, m - 1)
                    if m == 0:
                        dve.wait_ge(hT_ps, KC)
                    src = ps[:, u % 3, :].rearrange("p (g h d) -> p g h d", g=2, h=4)
                    if ch == C_QK0:
                        g = gains[:].unsqueeze(2).to_broadcast([P, 2, 4, HD])
                    else:
                        g = gains[:, ch - C_QRES, :].unsqueeze(1).unsqueeze(1).to_broadcast([P, 2, 4, HD])
                    xgu = xg[:, m % 2, :]
                    dve.tensor_tensor(xgu.rearrange("p (g h d) -> p g h d", g=2, h=4), src, g, ALU.mult
                                      ).then_inc(gain_ok, 1)
                    link(dve.tensor_reduce(st[:, 48:56], sq[:, m % 2, :].rearrange("p (h d) -> p h d", h=8),
                                           AX_X, ALU.add))
                    dve.tensor_scalar(st[:, 32:40], st[:, 48:56], 1.0 / HD, RMS_EPS, ALU.mult, ALU.add
                                      ).then_inc(var_ok, 1)
                    dve.wait_ge(seed_ok, 1 + m + 1)
                    refine(st[:, 32:40], st[:, 40:48], st[:, 48:56])
                    dve.wait_ge(rope_ok, m + 1)
                    xh = xgu.rearrange("p (h d) -> p h d", h=8)
                    dve.tensor_tensor(xh, xh, st[:, 40:48].unsqueeze(2).to_broadcast([P, 8, HD]), ALU.mult
                                      ).then_inc(qk_ready, 1)
                if u == KC - 1:
                    mod_round(1)
                if u == KC + 1:
                    dve.wait_ge(mod_cols, 2)
                    link(dve.tensor_copy(cols[:, 3, :], ps[:, 6, 16:24]))
                if u == 2 * KC - 1:
                    mod_round(2)
                if u == 2 * KC + 1:
                    dve.wait_ge(mod_cols, 3)
                    link(dve.scalar_tensor_tensor(out=cols[:, 2, :], in0=ps[:, 6, 24:32], scalar=1.0,
                                                  in1=gn[:, 1, :], op0=ALU.add, op1=ALU.mult))

            def softmax_max(s):
                dve.wait_ge(sc_ps, s + 1)
                if s == 0:
                    dve.wait_ge(qk_tr, QK_LAST - QK_FIRST + 1)
                    dve.wait_ge(ada_used, 3 * KC)
                if s >= 2:
                    dve.wait_ge(pT_ps, s - 1)
                k0 = key_from(s)
                m = mask12 if s < NT else mask0.rearrange("p (g n) -> p g n", g=2)
                m = m[:, k0 // P:2, :].unsqueeze(1).to_broadcast([P, NH, 2 - k0 // P, P])
                S = scores_view(s)[:, :, k0:].rearrange("p h (g n) -> p h g n", n=P)
                d = sm[:, s % 2, :, k0:]
                link(dve.tensor_tensor(d.rearrange("p h (g n) -> p h g n", n=P), S, m, ALU.add))
                link(dve.tensor_reduce(stat(s)[:, 4:8], d, AX_X, ALU.max))
                dve.tensor_scalar(stat(s)[:, 8:12], stat(s)[:, 4:8], -1.0, None, ALU.mult).then_inc(sc_max, 1)

            def probs_store(s):
                dve.wait_ge(pT_ps, s + 1)
                if s >= 2:
                    dve.wait_ge(u_ps, s - 1)
                b, k0 = s_bank(s), key_from(s)
                src = ps[:, b + 1, :].rearrange("p (h n) -> p h n", h=2)[:, :, k0:]
                dst = pT[:, s % 2, CH:2 * CH].rearrange("p (h n) -> p h n", h=2)[:, :, k0:]
                dve.tensor_copy(dst, src).then_inc(pT_dve, 1)

            def keep_u(s):
                dve.wait_ge(u_ps, s + 1)
                if s >= 2:
                    dve.wait_ge(u_out[s % 2], 16)
                dve.tensor_copy(ustage[:, s % 2, 0:GW], ps[:, 4 + s % 2, 0:GW]).then_inc(u_kept, 1)
                dve.tensor_copy(ustage[:, s % 2, GW:GW + 8], stat(s)[:, 0:8]).then_inc(stats_kept, 1)

            def mix_args(i):
                s = NT + i
                dve.wait_ge(sc_exp, s + 1)
                dve.wait_ge(u_back[i % 2], 16 * (i // 2 + 1))
                m12, m0 = ustage[:, i % 2, GW + 4:GW + 8], stat(s)[:, 4:8]
                cs = cstat(i)
                link(dve.tensor_tensor(cs[:, 8:12], m0, m12, ALU.max))
                link(dve.tensor_tensor(cs[:, 0:4], m0, cs[:, 8:12], ALU.subtract))
                dve.tensor_tensor(cs[:, 4:8], m12, cs[:, 8:12], ALU.subtract).then_inc(mx_ok, 1)

            def mix(i):
                s, cs = NT + i, cstat(i)
                dve.wait_ge(mx_exp, i + 1)
                link(dve.tensor_tensor(cs[:, 8:12], cs[:, 0:4], stat(s)[:, 0:4], ALU.mult))
                link(dve.tensor_tensor(cs[:, 12:16], cs[:, 4:8], ustage[:, i % 2, GW:GW + 4], ALU.mult))
                link(dve.tensor_tensor(cs[:, 8:12], cs[:, 8:12], cs[:, 12:16], ALU.add))
                link(dve.reciprocal(cs[:, 8:12], cs[:, 8:12]))
                link(dve.tensor_tensor(cs[:, 0:4], cs[:, 0:4], cs[:, 8:12], ALU.mult))
                link(dve.tensor_tensor(cs[:, 4:8], cs[:, 4:8], cs[:, 8:12], ALU.mult))
                dve.wait_ge(u_ps, s + 1)
                if i > 0:
                    dve.wait_ge(oT_ps, i)
                od = o_dil.rearrange("p (b a d) -> p a b d", a=2, b=2)
                u12 = ustage[:, i % 2, 0:GW].rearrange("p (a b d) -> p a b d", a=2, b=2)

                def by_head(v):
                    return v.rearrange("p (a b) -> p a b", a=2).unsqueeze(3).to_broadcast([P, 2, 2, HD])

                link(dve.tensor_tensor(u12, u12, by_head(cs[:, 4:8]), ALU.mult))
                dve.tensor_tensor(od, ps[:, 4 + s % 2, 0:GW].rearrange("p (a b d) -> p a b d", a=2, b=2),
                                  by_head(cs[:, 0:4]), ALU.mult).then_inc(u_kept, 1)
                dve.wait_ge(u_kept, s + 1)
                dve.tensor_tensor(od, od, u12, ALU.add).then_inc(o_ok, 1)

            def out_T(i):
                dve.wait_ge(oT_ps, i + 1)
                dve.tensor_copy(OT_DIL[:, :, i * P:(i + 1) * P],
                                ps[:, 4 + i % 2, 256:512].rearrange("p (c n) -> p c n", c=2)).then_inc(oT_ok, 1)

            def gate_finish(f):
                dve.wait_ge(gate_exp, f + 1)
                link(dve.tensor_scalar(gT[:, f, :], gT[:, f, :], 1.0, None, ALU.add))
                dve.reciprocal(gT[:, f, :], gT[:, f, :]).then_inc(gate_ok, 1)

            softmax_max(0)
            for s in range(2 * NT):
                gate_finish(s)
                probs_store(s)
                if s + 1 < 2 * NT:
                    softmax_max(s + 1)
                if 1 <= s <= NT:
                    keep_u(s - 1)
                if s >= NT + 1:
                    mix_args(s - NT - 1)
                    mix(s - NT - 1)
                if s - 2 >= NT:
                    out_T(s - 2 - NT)
            gate_finish(8)
            mix_args(NT - 1)
            mix(NT - 1)
            out_T(2)

            def sb_copy(h):
                dve.wait_ge(z_ps, h + 1)
                dve.wait_ge(z_abs, h + 1)
                if h == 0:
                    dve.wait_ge(u_ps, 2 * NT)
                else:
                    dve.wait_ge(osb_ps, h)
                b = 3 * (h % 2) * CH
                dve.tensor_copy(zs[:, 0:SB_COLS], psf[:, b:b + SB_COLS]).then_inc(z_cp, 1)

            def diag(v):
                return v[:, 0:1536].rearrange("p (a n) -> p a n", a=3)[:, :, 0:P], v[:, SB_OFF[3]:SB_OFF[3] + P]

            def sb_softplus(h):
                dve.wait_ge(lnz, h + 1)
                dve.wait_ge(z_cp, h + 1)
                if h > 0:
                    dve.wait_ge(sf_ps, h)
                link(dve.scalar_tensor_tensor(out=sp_[:, 0:SB_COLS], in0=zs[:, 0:SB_COLS], scalar=0.0,
                                              in1=lg1[:, 0:SB_COLS], op0=ALU.max, op1=ALU.add))
                a, b = diag(sp_)
                link(dve.tensor_tensor(a, a, strict[:].unsqueeze(1).to_broadcast([P, 3, P]), ALU.mult))
                dve.tensor_tensor(b, b, strict[:], ALU.mult).then_inc(sp_ok, 1)

            def sb_args(h):
                dve.wait_ge(sf_ps, h + 1)
                b = 3 * (h % 2) * CH
                link(dve.tensor_tensor(zs[:, 0:SB_COLS], zs[:, 0:SB_COLS], psf[:, b:b + SB_COLS], ALU.subtract))
                a, b = diag(zs)
                link(dve.tensor_tensor(a, a, negstrict.unsqueeze(1).to_broadcast([P, 3, P]), ALU.add))
                dve.tensor_tensor(b, b, negstrict, ALU.add).then_inc(arg_ok, 1)

            sb_copy(0)
            sb_softplus(0)
            gate_finish(9)
            out_T(3)
            for h in range(NH):
                sb_args(h)
                if h + 1 < NH:
                    gate_finish(10 + 2 * h)
                    sb_copy(h + 1)
                    sb_softplus(h + 1)
                    gate_finish(11 + 2 * h)

            dve.wait_ge(gate_ok, 2 * KC)
            for f in range(KC):
                dve.wait_ge(br_ps, f + 1)
                link(dve.tensor_tensor(gT[:, f, :], gT[:, f, :], ps[:, 2 * (f % 2), :], ALU.mult))
                link(dve.tensor_tensor(gT[:, KC + f, :], gT[:, KC + f, :], ps[:, 2 * (f % 2) + 1, :], ALU.mult))
                dve.tensor_tensor(hT[:, f, :], gT[:, f, :], gT[:, KC + f, :], ALU.add).then_inc(merged, 1)

            dve.wait_ge(g1_ok, 2)
            for u in range(2 * NT):
                t, j = divmod(u, 2)
                dve.wait_ge(o_ps, u + 1)
                link(dve.tensor_tensor(ps[:, 4 + j, :], ps[:, 4 + j, :], gate1b[:, j * CH:(j + 1) * CH], ALU.mult))
                xt = xs[:, t, j * CH:(j + 1) * CH]
                dve.tensor_tensor(xt, xt, ps[:, 4 + j, :], ALU.add).then_inc(x1_ok, 1)
                if j == 1:
                    dve.wait_ge(ss2_ok, t + 1)
                    dve.tensor_scalar(st[:, 20 + t:21 + t], st[:, 16 + t:17 + t], 1.0 / D, RMS_EPS,
                                      ALU.mult, ALU.add).then_inc(var2_ok, 1)
                    dve.wait_ge(seed2_ok, t + 1)
                    refine(st[:, 20 + t:21 + t], st[:, 24 + t:25 + t], st[:, 28 + t:29 + t])
                    dve.tensor_scalar(xn[:, t, :], xs[:, t, :], st[:, 24 + t:25 + t], None, ALU.mult
                                      ).then_inc(xn2_ok, 1)
            for cc in range(0, KC, 2):
                to_hT(h2_dve, cc, 2, 3, h2_ps)

            dve.wait_ge(lg_ps, 1)
            dve.wait_ge(slot_consts, 3)
            link(dve.tensor_copy(lg, ps[:, 4, 0:NT * (NG + NE)].rearrange("p (t n) -> p t n", t=NT)))
            G, E = lg[:, :, 0:NG], lg[:, :, NG:].rearrange("p t (g e) -> p t g e", g=NG)
            row = lambda i: rs[:, 44 + 4 * i:48 + 4 * i]
            gmax, best, v1, v2, pg, w1, w2, tmp4 = (row(i) for i in range(8))
            gex = rs[:, 0:16].rearrange("p (t g) -> p t g", t=NT)
            goh = rs[:, 76:92].rearrange("p (t g) -> p t g", t=NT)
            lsel = rs[:, 92:124].rearrange("p (t e) -> p t e", t=NT)
            o1 = rs[:, 124:156].rearrange("p (t e) -> p t e", t=NT)
            o2 = rs[:, 156:188].rearrange("p (t e) -> p t e", t=NT)
            num = iot[:, 0, 0:EPG]

            def first_max(onehot, vals, top, width):
                full = [P, NT, width]
                link(dve.tensor_reduce(top, vals, AX_X, ALU.max))
                link(dve.tensor_tensor(onehot, vals, top.unsqueeze(2).to_broadcast(full), ALU.is_equal))
                back = rt[:, 0:NT * width].rearrange("p (t e) -> p t e", t=NT)
                link(dve.tensor_scalar(rt[:, 64:64 + width], num[:, 0:width], -float(EPG), None, ALU.add))
                link(dve.tensor_tensor(back, onehot, rt[:, 64:64 + width].unsqueeze(1).to_broadcast(full), ALU.mult))
                link(dve.tensor_reduce(best, back, AX_X, ALU.min))
                link(dve.tensor_tensor(onehot, back, best.unsqueeze(2).to_broadcast(full), ALU.is_equal))

            first_max(goh, G, gmax, NG)
            dve.tensor_tensor(gex, G, gmax.unsqueeze(2).to_broadcast([P, NT, NG]), ALU.subtract).then_inc(r_arg, 1)
            pick = rt.rearrange("p (t g e) -> p t g e", t=NT, g=NG)
            link(dve.tensor_tensor(pick, E, goh.unsqueeze(3).to_broadcast([P, NT, NG, EPG]), ALU.mult))
            link(dve.tensor_reduce(lsel, pick.rearrange("p t g e -> p t e g"), AX_X, ALU.add))
            first_max(o1, lsel, v1, EPG)
            link(dve.scalar_tensor_tensor(out=lsel, in0=o1, scalar=NEG, in1=lsel, op0=ALU.mult, op1=ALU.add))
            first_max(o2, lsel, v2, EPG)
            dve.tensor_tensor(rs[:, 40:44], v2, v1, ALU.subtract).then_inc(r_arg, 1)
            dve.wait_ge(r_exp, 2)
            link(dve.tensor_reduce(pg, gex, AX_X, ALU.add))
            link(dve.tensor_scalar(w1, rs[:, 40:44], 1.0, None, ALU.add))
            link(dve.tensor_tensor(w1, w1, pg, ALU.mult))
            link(dve.reciprocal(w1, w1))
            link(dve.tensor_tensor(w2, w1, rs[:, 40:44], ALU.mult))
            full = [P, NT, NG, EPG]
            for a, o in ((A1, o1), (A2, o2)):
                link(dve.tensor_tensor(a.rearrange("p t (g e) -> p t g e", g=NG),
                                       goh.unsqueeze(3).to_broadcast(full), o.unsqueeze(2).to_broadcast(full), ALU.mult))
            dve.tensor_tensor(AA, A1, A2, ALU.add).then_inc(rk_in, 1)
            dve.wait_ge(rk_ps, 1)
            link(dve.tensor_copy(RK, ps[:, 5, 0:NT * NE].rearrange("p (t e) -> p t e", t=NT)))
            link(dve.scalar_tensor_tensor(out=RE, in0=RK, scalar=1.0, in1=AA, op0=ALU.add, op1=ALU.mult))
            link(dve.tensor_scalar(RE, RE, -1.0, None, ALU.add))
            link(dve.tensor_reduce(tmp4[:, 0:1], ps[:, 5, 4 * NE:5 * NE], AX_X, ALU.max))
            link(dve.tensor_copy(cnt_i[:], tmp4[:, 0:1]))
            rk4 = rs[:, 188:196].rearrange("p (j t) -> p j t", j=2)
            rt3 = rt.rearrange("p (t e) -> p t e", t=NT)
            for j, a in enumerate((A1, A2)):
                link(dve.tensor_tensor(rt3, a, RK, ALU.mult))
                link(dve.tensor_reduce(rk4[:, j, :], rt3, AX_X, ALU.add))
            code = rs[:, 196:204].rearrange("p (j t) -> p j t", j=2)
            for j in range(2):
                link(dve.tensor_scalar(code[:, j, :], tokc[:], float(j), None, ALU.add))

            def slot_tables(done, step):
                for i in range(2 * NT):
                    j, t = divmod(i, NT)
                    dve.wait_ge(tb_ps, done + max(i - 1, 0))
                    step(dve.tensor_scalar(oh_view(i), iot[:].rearrange("p a s -> p (a s)"), rk4[:, j, t:t + 1],
                                           None, ALU.is_equal))
                    a, w = (A1, w1) if j == 0 else (A2, w2)
                    step(dve.tensor_scalar(tb_view(i)[:, 0:NE], a[:, t, :], code[:, j, t:t + 1], None, ALU.mult))
                    dve.tensor_scalar(tb_view(i)[:, NE:2 * NE], a[:, t, :], w[:, t:t + 1], None, ALU.mult
                                      ).then_inc(tb_in, 1)
                dve.wait_ge(tb_ps, done + 2 * NT)
                step(dve.tensor_copy(slotW, ps[:, 7, NE:2 * NE]))
                dve.tensor_scalar(slotI, ps[:, 7, 0:NE], 2.0, halfc[:, 0:1], ALU.mult, ALU.add
                                  ).then_inc(tables_ok, 1)

            slot_tables(0, link)
            dve.wait_ge(tables_ok, 1)
            dve.wait_ge(g2_ok, 1)

            def one_hot(e, hb, gathers=None):
                if gathers is None:
                    gathers = e - 1
                if later(e) and later(gathers):
                    dve.wait_ge(gx_ps, gathers)
                dve.tensor_tensor(hot[:, hb], iot[:, 0:1, :].to_broadcast([P, NT, CAP]),
                                  RE[:, :, bass.ds(e, 1)].to_broadcast([P, NT, CAP]), ALU.is_equal
                                  ).then_inc(hot_ok, 1)

            def store_xT(e):
                dve.wait_ge(xt_ps, e + 1)
                full = [P, 4, 2, CAP]
                a2 = cols[:, 2, :].rearrange("p (h q) -> p q h", h=2).unsqueeze(3).to_broadcast(full)
                b2 = cols[:, 3, :].rearrange("p (h q) -> p q h", h=2).unsqueeze(3).to_broadcast(full)
                xm = xmul.rearrange("p (q h s) -> p q h s", q=4, h=2)
                dve.tensor_tensor(xm, ps[:, 1, :].rearrange("p (q h s) -> p q h s", q=4, h=2), a2, ALU.mult
                                  ).then_inc(moe_dve, 1)
                return xm, b2

            NSTEP = 5

            def store_xT2(e, xm, b2, step):
                dve.wait_ge(moe_dve, step)
                if later(e):
                    dve.wait_ge(gu_ps, e)
                dve.tensor_tensor(xeT, xm, b2, ALU.add).then_inc(xt_ok, 1)

            def expert(e, hb, more=True, col=None):
                s0 = e * NSTEP + 1
                if more:
                    one_hot(e + 1, 1 - hb)
                if later(e):
                    dve.wait_ge(y_ok, e)
                col = e if col is None else col
                dve.tensor_copy(wcol[:], slotW[:, bass.ds(col, 1)]).then_inc(moe_dve, 1)
                dve.wait_ge(sig_exp, e + 1)
                dve.tensor_scalar(tden, tsig, 1.0, None, ALU.add).then_inc(moe_dve, 1)
                dve.wait_ge(moe_dve, s0 + 2)
                dve.reciprocal(tden, tden).then_inc(moe_dve, 1)
                dve.wait_ge(moe_dve, s0 + 3)
                dve.tensor_tensor(tden, tden, ps[:, 2, 0:256], ALU.mult).then_inc(moe_dve, 1)
                dve.wait_ge(moe_dve, s0 + 4)
                dve.tensor_tensor(hh, tden, ps[:, 2, 256:512], ALU.mult).then_inc(h_ok, 1)
                dve.wait_ge(ht_ps, e + 1)
                dve.tensor_copy(hhT, ps[:, 3, 0:256].rearrange("p (q n) -> p q n", q=2)).then_inc(ht_ok, 1)
                if more:
                    xm, b2 = store_xT(e + 1)
                    store_xT2(e + 1, xm, b2, s0 + 5)
                dve.wait_ge(dn_ps, e + 1)
                if later(e):
                    dve.wait_ge(y_out, e * 16)
                dve.scalar_tensor_tensor(out=ye[:, hb, :], in0=ps[:, 4, :], scalar=wcol[:, 0:1], in1=gate2h,
                                         op0=ALU.mult, op1=ALU.mult).then_inc(y_ok, 1)

            one_hot(0, 0)
            xm, b2 = store_xT(0)
            store_xT2(0, xm, b2, 1)
            expert(0, 0)
            with dve.Fori(0, (NE - 2) // 2) as i:
                for j in (1, 2):
                    expert(i * 2 + j, j % 2)
            expert(NE - 1, 1, more=False)

            def dve_round(rnd):
                dve.wait_ge(y_out, rnd * (16 * NE))
                at = [0]

                def step(ins):
                    at[0] += 1
                    ins.then_inc(round_seq, 1)
                    dve.wait_ge(round_seq, (rnd - 1) * ROUND_STEPS + at[0])

                step(dve.tensor_scalar(rs[:, 188:196], rs[:, 188:196], -float(CAP), None, ALU.add))
                step(dve.tensor_scalar(RE, RE, -float(CAP), None, ALU.add))
                slot_tables(rnd * (2 * NT), step)
                assert at[0] == ROUND_STEPS
                with dve.Fori(0, NE) as e:
                    dve.wait_ge(tables_ok, rnd + 1)
                    k = rnd * NE + e
                    one_hot(e, 0, k)
                    xm, b2 = store_xT(k)
                    store_xT2(k, xm, b2, k * NSTEP + 1)
                    expert(k, 0, more=False, col=e)

            ROUND_STEPS = 3 + 4 * NT
            more_rounds(dve, dve_round)

            for t in range(NT):
                dve.wait_ge(y_back[t], 16)
                y = arena[:, 2048 * t:2048 * (t + 1)].rearrange("p (j n) -> p j n", j=2)
                link(dve.tensor_tensor(xs[:, t, :], xs[:, t, :], y[:, 0, :], ALU.add))
                dve.tensor_tensor(xs[:, t, :], xs[:, t, :], y[:, 1, :], ALU.add).then_inc(fin_ok, 1)


_INS = ['x', 'c', 'positions', 'w_ada', 'b_ada', 'g_norm_mix', 'g_norm_ffn', 'w_in', 'w_branch_gate',
        'q_norm_g', 'k_norm_g', 'w_branch_dil', 'w_branch_sb', 'w_out', 'w_router_group',
        'b_router_group', 'w_router_expert', 'b_router_expert', 'w_expert_gate', 'w_expert_up',
        'w_expert_down']


def kernel(**inputs):
    import numpy as _np
    import concourse.bacc as _bacc
    from concourse import mybir as _mybir
    from concourse.bass_utils import run_bass_kernel_spmd as _run

    nc = _bacc.Bacc("TRN2", target_bir_lowering=False, num_devices=1)
    arrays, args = {}, []
    for name in _INS:
        a = _np.ascontiguousarray(inputs[name])
        arrays[f"in_{name}"] = a
        args.append(nc.dram_tensor(f"in_{name}", a.shape, _mybir.dt.from_np(a.dtype), kind="ExternalInput").ap())
    out = nc.dram_tensor("out", (1, SEQ, D), F32, kind="ExternalOutput").ap()
    hybrid_layer(nc, *args, out)
    r = _run(nc, [arrays], core_ids=[0])
    return r.results[0]["out"]
```

```python
from contextlib import ExitStack

import numpy as np

import concourse.bass as bass
from concourse import mybir

ALU = mybir.AluOpType
ACT = mybir.ActivationFunctionType
F32 = mybir.dt.float32
F32R = mybir.dt.float32r
I32 = mybir.dt.int32
AX_X = mybir.AxisListType.X

P = 128
D = 1024
SEQ = 512
NT = SEQ // P
KC = D // P
HD = 64
NH = 4
GW = NH * HD
ROPE_DIM = HD // 4
HALF = ROPE_DIM // 2
ROPE_THETA = 500000.0
RMS_EPS = 1e-6
NG = 4
EPG = 8
NE = NG * EPG
FE = 512
CAP = 64
ROUNDS = SEQ // CAP
CH = 512
NEG = -1e30
UNUSED = 4096.0
SLOT_W = KC * CH
EXP_W = 3 * SLOT_W
NBUF = 3

QA, KA, VA = 0, 3 * GW, 6 * GW
QB, KB, VB = 9 * GW, 10 * GW, 11 * GW
C_SB, C_VNAT, C_QK0, C_QRES, C_KRES, C_VRES = range(6)
SB_OFF = [0, 512, 1024, 896]
SB_COLS = 1280


def two_pi_parts():
    rest, parts = np.float64(2 * np.pi), []
    for bits in (8, 8, 8):
        e = int(np.floor(np.log2(rest))) - bits + 1
        part = np.floor(rest / 2.0 ** e) * 2.0 ** e
        parts.append(float(part))
        rest = rest - part
    return parts + [float(np.float32(rest))]


def hybrid_layer(nc, x, c, positions, w_ada, b_ada, g_norm_mix, g_norm_ffn, w_in, w_branch_gate,
                 q_norm_g, k_norm_g, w_branch_dil, w_branch_sb, w_out, w_router_group,
                 b_router_group, w_router_expert, b_router_expert, w_expert_gate, w_expert_up,
                 w_expert_down, out):
    inv_freq = np.float32(ROPE_THETA) ** (-np.arange(0, ROPE_DIM, 2, dtype=np.float32) / np.float32(ROPE_DIM))

    ctx = ExitStack()
    with ctx:
        def sb(name, shape, dt=F32):
            return ctx.enter_context(nc.sbuf_tensor(name, shape, dt))

        def sem(name):
            return ctx.enter_context(nc.semaphore(name))

        dil_rows = nc.dram_tensor("dil_rows", (SEQ, GW + 2 * NH), F32, kind="Internal").ap()
        y_rows = nc.dram_tensor("y_rows", (SEQ * 2 * 2, CH), F32, kind="Internal").ap()

        with nc.sbuf_tensor("arena", [P, NBUF * EXP_W], F32) as arena, \
                nc.sbuf_tensor("xs", [P, NT, D], F32) as xs, \
                nc.sbuf_tensor("hT", [P, KC, SEQ], F32) as hT:
            pass
        slot_r = [sb(f"slot_r{j}", [P, KC, CH], F32R) for j in range(3 * NBUF)]
        xs_r = sb("xs_r", [P, NT, D], F32R)
        hT_r = sb("hT_r", [P, KC, SEQ], F32R)
        xn = sb("xn", [P, NT, D])
        ident = sb("ident", [P, P])
        ones = sb("ones", [P, P])
        strict = sb("strict", [P, P])
        tri = sb("tri", [P, P])
        small = sb("small", [P, 1168])
        wr = sb("wr", [P, KC, NG + NE])
        br = sb("br", [1, NG + NE])
        gains = sb("gains", [P, 2, HD])
        trig = sb("trig", [P, 2 * 2 * NT * ROPE_DIM])
        cos16, sin16 = (trig[:, P * i:P * i + P].rearrange("p (t d) -> p t d", t=2 * NT) for i in range(2))
        crep_f = sb("crep", [P, KC * 32])
        crep = crep_f[:].rearrange("p (k m) -> p k m", k=KC)
        modr = sb("modr", [P, CH])
        grow = sb("grow", [P, CH])
        cols = sb("cols", [P, 4, KC])
        gn = sb("gn", [P, 2, KC])
        st = sb("st", [P, 64])
        pos_i = sb("pos_i", [P, 2 * NT], I32)
        c_in = sb("c_in", [P, KC])

        mask12 = small[:, 0:256].rearrange("p (g n) -> p g n", g=2)
        mask0 = small[:, 256:512]
        negstrict = small[:, 512:640]
        ustage = small[:, 640:1168].rearrange("p (b n) -> p b n", b=2)

        gn_rows = small[0:16, 640:768]
        diff_i, diff_m = small[:, 912:1040].bitcast(I32), small[:, 1040:1168]
        stats = sb("stats", [P, 4, 12])
        cstats = sb("cstats", [P, 2, 16])
        o_dil = small[:, 0:GW]

        def stat(s):
            return stats[:, s % 4, :]

        def cstat(i):
            return cstats[:, i % 2, :]

        def pair(j):
            return j % 3 if j < 6 else j % 2

        def w_raw(j):
            at = 2 * pair(j) * SLOT_W
            return arena[:, at:at + SLOT_W].rearrange("p (k n) -> p k n", k=KC)

        def w_part(j, i):
            return slot_r[2 * pair(j) + i]

        def w_lo(j):
            return w_part(j, 0)

        def w_hi(j):
            return w_part(j, 1)

        base = 2 * EXP_W
        QT = arena[:, base:base + 3072].rearrange("p (c n) -> p c n", c=6)
        KT = arena[:, base + 3072:base + 6144].rearrange("p (c n) -> p c n", c=6)
        VN = arena[:, base + 6144:base + 8192].rearrange("p (t n) -> p t n", t=NT)
        VR = arena[:, base + 8192:base + 10240].rearrange("p (t n) -> p t n", t=NT)
        SBT = arena[:, base + 10240:base + 12288].rearrange("p (c n) -> p c n", c=4)
        OT_DIL = QT[:, 0:2, :]
        OT_SB = SBT[:, 0:2, :]
        gT = arena[:, 4 * SLOT_W:6 * SLOT_W].rearrange("p (c n) -> p c n", c=2 * KC)
        wbr = arena[:, base + 1024:base + 1024 + SLOT_W].rearrange("p (b k n) -> p b k n", b=2, k=2)

        h_hi = xs_r[:].rearrange("p t n -> p (t n)").rearrange("p (c n) -> p c n", c=KC)
        h_lo = hT_r[:]
        m_hi = slot_r[4]
        h2t = arena[:, 5 * SLOT_W:5 * SLOT_W + 2 * KC * P].rearrange("p (b k n) -> p b k n", b=2, k=KC)
        xnf = xn[:].rearrange("p t n -> p (t n)")
        ada_slot = xnf[:, 0:2048]
        xg = xnf[:, 2048:3072].rearrange("p (b n) -> p b n", b=2)
        sq = xnf[:, 3072:4096].rearrange("p (b n) -> p b n", b=2)
        sm = xnf[:, 0:2048].rearrange("p (b h n) -> p b h n", b=2, h=NH)
        pT = xnf[:, 2048:4096].rearrange("p (b n) -> p b n", b=2)
        zs, lg1, sp_ = xnf[:, 0:1536], xnf[:, 1280:2816], xnf[:, 2560:4096]
        gate1b = xn[:, NT - 1, :]

        def ada_piece(k):
            at = base + 2048 * k if k < 6 else 5 * SLOT_W + 2048 * (k - 6)
            return arena[:, at:at + 2048]

        def w_gu(b):
            return arena[:, b * EXP_W:b * EXP_W + 2 * SLOT_W].rearrange("p (g k n) -> p g k n", g=2, k=KC)

        def w_dn(b):
            return arena[:, b * EXP_W + 2 * SLOT_W:(b + 1) * EXP_W].rearrange("p (f n) -> p f n", f=FE // P)

        wk = hT[:].rearrange("p c n -> p (c n)")
        xe = wk[:, 0:512]
        xeT = wk[:, 512:1024].rearrange("p (q h s) -> p q h s", q=4, h=2)
        xmul = wk[:, 1024:1536]
        hh = wk[:, 1536:1792]
        hhT = wk[:, 1792:2048].rearrange("p (q n) -> p q n", q=2)
        tsig = wk[:, 2048:2304]
        tden = wk[:, 2304:2560]
        ye = wk[:, 2560:3584].rearrange("p (b n) -> p b n", b=2)
        hot = wk[:, 3584:4096].rearrange("p (b t s) -> p b t s", b=2, t=NT)
        gate2h = modr[:]

        RA = small[:, 0:640]
        AA5 = RA[:, 2 * P:2 * P + (NT + 1) * NE]
        A1, A2, AA, RK, RE = (RA[:, 128 * i:128 * i + 128].rearrange("p (t e) -> p t e", t=NT) for i in range(5))
        lg = small[:, 640:784].rearrange("p (t n) -> p t n", t=NT)
        rt = small[:, 784:912]
        slotW = small[:, 912:944]
        slotI = small[:, 944:976].bitcast(I32)

        def oh_view(i):
            return small[:, 976:1104] if i % 2 == 0 else RA[:, 256:384]

        def tb_view(i):
            return rt[:, 64 * (i % 2):64 * (i % 2) + 64]

        rs = trig[:, 0:208]
        sin_arg, trig_k, cos_arg = (grow[:, 64 * i:64 * i + 64].rearrange("p (t f) -> p t f", t=2 * NT)
                                    for i in range(3))
        idx = [sb(f"idx{b}", [P, 1], I32) for b in range(2)]
        wcol = sb("wcol", [P, 1])
        iot = crep_f[:, 0:2 * CAP].rearrange("p (a s) -> p a s", a=2)
        tokc = crep_f[:, 2 * CAP:2 * CAP + NT]
        halfc = crep_f[:, 2 * CAP + NT:2 * CAP + NT + 1]
        cnt_i = sb("cnt_i", [P, 1], I32)

        ps = ctx.enter_context(nc.psum_tensor("ps", [P, 8, CH], F32))
        psf = ps[:].rearrange("p b n -> p (b n)")

        x_in = [sem(f"x_in{t}") for t in range(NT)]
        pos_in, c_ld, gn_in, gains_in, wr_in = sem("pos_in"), sem("c_ld"), sem("gn_in"), sem("gains_in"), sem("wr_in")
        bias_in = sem("bias_in")
        ada_in = [sem(f"ada_in{k}") for k in range(8)]
        ada2_in = sem("ada2_in")
        w_ld = [sem(f"w_ld{j}") for j in range(12)]
        wb_in = sem("wb_in")
        consts = sem("consts")
        slot_consts = sem("slot_consts")
        pool_seq = sem("pool_seq")
        dve_seq = sem("dve_seq")
        act_seq = sem("act_seq")
        gn_T = sem("gn_T")
        crep_ok = sem("crep_ok")
        ada_used = sem("ada_used")
        mod_rows = sem("mod_rows")
        mod_cols = sem("mod_cols")
        row_tile = sem("row_tile")
        gates_kept = sem("gates_kept")
        cols_ok = sem("cols_ok")
        trig_arg, trig_ok = sem("trig_arg"), sem("trig_ok")
        ss_ok, var_ok, seed_ok, xn_ok = sem("ss_ok"), sem("var_ok"), sem("seed_ok"), sem("xn_ok")
        hT_ps, hT_dve, hT_act = sem("hT_ps"), sem("hT_dve"), sem("hT_act")
        h_full, hi_ok, lo_ok = sem("h_full"), sem("hi_ok"), sem("lo_ok")
        whi_ok, wlo_ok = sem("whi_ok"), sem("wlo_ok")
        m_full, mhi_ok, mlo_ok = sem("m_full"), sem("mhi_ok"), sem("mlo_ok")
        proj_done, proj_act, gain_ok = sem("proj_done"), sem("proj_act"), sem("gain_ok")
        rope_ok, qk_ready, qk_tr, qk_stored = sem("rope_ok"), sem("qk_ready"), sem("qk_tr"), sem("qk_stored")
        gate_ps, gate_exp, gate_ok = sem("gate_ps"), sem("gate_exp"), sem("gate_ok")
        sc_ps, sc_max, sc_exp = sem("sc_ps"), sem("sc_max"), sem("sc_exp")
        pT_ps, pT_act, pT_dve = sem("pT_ps"), sem("pT_act"), sem("pT_dve")
        u_ps, u_kept, stats_kept = sem("u_ps"), sem("u_kept"), sem("stats_kept")
        u_out = [sem(f"u_out{i}") for i in range(2)]
        u_back = [sem(f"u_back{i}") for i in range(2)]
        mx_ok, mx_exp, o_ok, oT_ps, oT_ok = sem("mx_ok"), sem("mx_exp"), sem("o_ok"), sem("oT_ps"), sem("oT_ok")
        z_ps, z_abs, z_cp, lnz, sp_ok = sem("z_ps"), sem("z_abs"), sem("z_cp"), sem("lnz"), sem("sp_ok")
        sf_ps, arg_ok, a_ok, osb_ps, osb_ok = sem("sf_ps"), sem("arg_ok"), sem("a_ok"), sem("osb_ps"), sem("osb_ok")
        br_ps, merged = sem("br_ps"), sem("merged")
        g1_ps, g1_ok, o_ps, x1_ok = sem("g1_ps"), sem("g1_ok"), sem("o_ps"), sem("x1_ok")
        ss2_ok, var2_ok, seed2_ok, xn2_ok = sem("ss2_ok"), sem("var2_ok"), sem("seed2_ok"), sem("xn2_ok")
        h2_ps, h2_dve, h2_act, lg_ps = sem("h2_ps"), sem("h2_dve"), sem("h2_act"), sem("lg_ps")
        r_arg, r_exp, rk_in, rk_ps, tb_in, tb_ps, tables_ok = (
            sem("r_arg"), sem("r_exp"), sem("rk_in"), sem("rk_ps"), sem("tb_in"), sem("tb_ps"), sem("tables_ok"))
        g2_ps, g2_ok = sem("g2_ps"), sem("g2_ok")
        gu_in = [sem(f"gu_in{b}") for b in range(NBUF)]
        dn_in = [sem(f"dn_in{b}") for b in range(NBUF)]
        hot_ok, gx_ps, xe_ok, xt_ps, xt_ok = sem("hot_ok"), sem("gx_ps"), sem("xe_ok"), sem("xt_ps"), sem("xt_ok")
        gu_ps, sig_exp, h_ok, ht_ps, ht_ok = sem("gu_ps"), sem("sig_exp"), sem("h_ok"), sem("ht_ps"), sem("ht_ok")
        dn_ps, wcol_ok, idx_ok, y_ok = sem("dn_ps"), sem("wcol_ok"), sem("idx_ok"), sem("y_ok")
        y_out = [sem(f"y_out{b}") for b in range(2)]
        moe_dve = sem("moe_dve")
        round_seq = sem("round_seq")
        y_back = [sem(f"y_back{t}") for t in range(NT)]
        fin_ok, out_st = sem("fin_ok"), sem("out_st")

        block = ctx.enter_context(nc.Block())

        def w_in_cols(ch):
            return {C_SB: (QB, KB), C_VNAT: (VA, VB), C_QK0: (QA, KA), C_QRES: (QA + GW, QA + 2 * GW),
                    C_KRES: (KA + GW, KA + 2 * GW), C_VRES: (VA + GW, VA + 2 * GW)}[ch]

        def tokens(ch, t):
            return slice(t, SEQ, NT) if ch in (C_QRES, C_KRES, C_VRES) else slice(t * P, (t + 1) * P)

        NU = 6 * NT
        QK_FIRST, QK_LAST = C_QK0 * NT, C_KRES * NT + NT - 1

        def s_bank(s):
            return 2 * (s % 2)

        def scores_view(s):
            b = s_bank(s)
            return psf[:, b * CH:(b + 2) * CH].rearrange("p (h n) -> p h n", h=NH)

        def place(h):
            return 2 * (h % 2) + h // 2

        def key_from(s):
            return P if s == NT else 0

        def buffer_of(e):
            return (NBUF - 1 + e) % NBUF

        def later(e):
            return not isinstance(e, int) or e > 0

        def more_rounds(eng, body):
            eng.wait_ge(tables_ok, 1)
            top = eng.value_load(cnt_i[0:1, 0:1], min_val=0, max_val=SEQ - 1)
            with eng.If(top + 1 > CAP):
                with eng.Fori(1, ROUNDS) as rnd:
                    with eng.If(top + 1 > rnd * CAP):
                        body(rnd)
            return top

        @block.sync
        def _(sp):
            for t in range(NT):
                sp.dma_start(xs[:, t, :], x[0, t * P:(t + 1) * P, :]).then_inc(x_in[t], 16)
            ada_rows = w_ada[0].rearrange("(p k) n -> p k n", k=KC)

            w_in_r = w_in[0].rearrange("(k p) n -> p k n", p=P)
            w_bg_r = w_branch_gate[0].rearrange("(k p) n -> p k n", p=P)

            def load_half(ch, h):
                c0 = w_in_cols(ch)[h]
                sp.dma_start(w_raw(ch)[:, :, h * 256:(h + 1) * 256], w_in_r[:, :, c0:c0 + 256]
                             ).then_inc(w_ld[ch], 16)

            for k in range(KC):
                sp.dma_start(ada_piece(k), ada_rows[:, k, 0:2048]).then_inc(ada_in[k], 16)
                if k == 4:
                    load_half(0, 0)
                    load_half(0, 1)
            sp.wait_ge(hT_ps, KC)
            sp.dma_start(ada_slot, ada_rows[:, 0, 2048:4096]).then_inc(ada2_in, 16)
            load_half(1, 0)
            load_half(1, 1)
            for n in range(1, 2 * KC):
                sp.wait_ge(ada_used, KC + n)
                lo = 2048 * (1 + n // KC)
                sp.dma_start(ada_slot, ada_rows[:, n % KC, lo:lo + 2048]).then_inc(ada2_in, 16)
                if n in (1, 2):
                    load_half(2, n - 1)
                elif n % NT in (0, 1):
                    ch = n // NT + 2
                    sp.wait_ge(proj_done, NT * (ch - 2))
                    load_half(ch, n % NT)
            for j in range(4):
                if j < 2:
                    sp.wait_ge(proj_done, NT * (j + 4))
                else:
                    sp.wait_ge(gate_ps, NT * (j - 1))
                sp.dma_start(w_raw(6 + j), w_bg_r[:, :, j * CH:(j + 1) * CH]).then_inc(w_ld[6 + j], 16)
            sp.wait_ge(sc_ps, 2 * NT)
            for b, w in enumerate((w_branch_dil, w_branch_sb)):
                sp.dma_start(wbr[:, b], w[0].rearrange("(k p) n -> p k n", p=P)).then_inc(wb_in, 16)
            for j in range(2):
                sp.wait_ge(gate_ps, NT * (j + 3))
                sp.dma_start(w_raw(10 + j), w_out[0].rearrange("(k p) n -> p k n", p=P)[:, :, j * CH:(j + 1) * CH]
                             ).then_inc(w_ld[10 + j], 16)
            for t in range(NT):
                sp.dma_start(xs[:, t, :], x[0, t * P:(t + 1) * P, :]).then_inc(x_in[t], 16)

            def load_gu(e, b):
                for g, w in enumerate((w_expert_gate, w_expert_up)):
                    src = w[0, bass.ds(e, 1)].rearrange("e (k p) n -> p (e k) n", p=P)
                    sp.dma_start(w_gu(b)[:, g], src).then_inc(gu_in[b], 16)

            def load_dn(e, b):
                src = w_expert_down[0, bass.ds(e, 1)].rearrange("e (k p) n -> p (e k) n", p=P)
                sp.dma_start(w_dn(b), src).then_inc(dn_in[b], 16)

            sp.wait_ge(br_ps, KC)
            load_gu(0, 2)
            load_dn(0, 2)
            sp.wait_ge(o_ps, 2 * NT)
            load_gu(1, 0)
            load_dn(1, 0)
            sp.wait_ge(lg_ps, NT)
            load_gu(2, 1)
            load_dn(2, 1)

            def refill(e, b):
                sp.wait_ge(gu_ps, e + 1)
                load_gu(e + NBUF, b)
                sp.wait_ge(dn_ps, e + 1)
                load_dn(e + NBUF, b)

            with sp.Fori(0, 9) as i:
                for j in range(NBUF):
                    refill(i * NBUF + j, buffer_of(j))
            for e in (27, 28):
                refill(e, buffer_of(e))


            def sp_round(rnd):
                with sp.Fori(0, NE) as e:
                    sp.wait_ge(dn_ps, rnd * NE + e)
                    load_gu(e, 0)
                    load_dn(e, 0)

            top = more_rounds(sp, sp_round)
            sp.wait_ge(y_out[1], 16 * (NE // 2))
            sp.wait_ge(y_out[0], (top // CAP) * (16 * NE) + 16 * (NE // 2))
            for t in range(NT):
                sp.dma_start(arena[:, 2048 * t:2048 * (t + 1)],
                             y_rows[4 * P * t:4 * P * (t + 1), :].rearrange("(p r) n -> p (r n)", r=4)
                             ).then_inc(y_back[t], 16)
            for t in range(NT):
                sp.wait_ge(fin_ok, t + 1)
                sp.dma_start(out[0, t * P:(t + 1) * P, :], xs[:, t, :]).then_inc(out_st, 16)
            sp.wait_ge(out_st, 16 * NT)

        @block.gpsimd
        def _(pool):
            n = [0]

            def link(ins):
                n[0] += 1
                ins.then_inc(pool_seq, 1)
                pool.wait_ge(pool_seq, n[0])

            link(pool.memset(ident[:], 0.0))
            link(pool.affine_select(ident[:], ident[:], [[-1, P]], ALU.not_equal, 1.0, base=0, channel_multiplier=1))
            pool.memset(ones[:], 1.0).then_inc(consts, 1)
            link(pool.memset(strict[:], 0.0))
            pool.affine_select(strict[:], strict[:], [[-1, P]], ALU.is_ge, 1.0, base=0,
                               channel_multiplier=1).then_inc(consts, 1)
            link(pool.memset(tri[:], 0.0))
            pool.affine_select(tri[:], tri[:], [[1, P]], ALU.is_gt, 1.0, base=0,
                               channel_multiplier=-1).then_inc(consts, 1)
            link(pool.memset(small[:, 0:640], 0.0))
            link(pool.affine_select(mask12, mask12, [[0, 2], [-1, P]], ALU.is_ge, NEG, base=0, channel_multiplier=1))
            pool.iota(diff_i, [[-1, P]], base=2 * P, channel_multiplier=1).then_inc(consts, 1)
            link(pool.affine_select(mask0, mask0, [[1, 2 * P]], ALU.is_ge, NEG, base=0, channel_multiplier=-1))
            link(pool.affine_select(mask0, mask0, [[-1, 2 * P]], ALU.is_ge, NEG, base=P, channel_multiplier=1))
            link(pool.affine_select(negstrict, negstrict, [[1, P]], ALU.is_gt, NEG, base=0, channel_multiplier=-1))
            for u in range(QK_FIRST, QK_LAST + 1):
                m, t, ch = u - QK_FIRST, u % NT, u // NT
                tt = t + (NT if ch != C_QK0 else 0)
                v = xg[:, m % 2, :].rearrange("p (h d) -> p h d", h=8)
                xr = v[:, :, 0:ROPE_DIM]
                swp = sq[:, m % 2, 0:128].rearrange("p (h d) -> p h d", h=8)
                csb = cos16[:, tt:tt + 1, :].to_broadcast([P, 8, ROPE_DIM])
                snb = sin16[:, tt:tt + 1, :].to_broadcast([P, 8, ROPE_DIM])
                if m == 0:
                    pool.wait_ge(trig_ok, 3)
                pool.wait_ge(var_ok, 1 + m + 1)
                pool.wait_ge(gain_ok, m + 1)
                pool.tensor_tensor(swp[:, :, 0:HALF], xr[:, :, HALF:ROPE_DIM], snb[:, :, 0:HALF],
                                   ALU.mult).then_inc(pool_seq, 1)
                pool.tensor_tensor(swp[:, :, HALF:ROPE_DIM], xr[:, :, 0:HALF], snb[:, :, HALF:ROPE_DIM],
                                   ALU.mult).then_inc(pool_seq, 1)
                n[0] += 2
                pool.wait_ge(pool_seq, n[0])
                link(pool.tensor_tensor(xr, xr, csb, ALU.mult))
                pool.tensor_tensor(xr, xr, swp, ALU.add).then_inc(rope_ok, 1)

            pool.wait_ge(ada_used, 3 * KC)
            pool.iota(iot[:], [[0, 2], [1, CAP]], base=0, channel_multiplier=0,
                      allow_small_or_imprecise_dtypes=True).then_inc(slot_consts, 1)
            pool.iota(tokc[:], [[2 * P, NT]], base=-int(UNUSED), channel_multiplier=2,
                      allow_small_or_imprecise_dtypes=True).then_inc(slot_consts, 1)
            link(pool.memset(halfc[:, :], 2 * UNUSED))
            pool.wait_ge(slot_consts, 2)
            pool.memset(halfc[64:128, :], 2 * UNUSED + 1).then_inc(slot_consts, 1)
            pool.wait_ge(slot_consts, 3)

            rows = dil_rows.rearrange("(a r) n -> r a n", r=NT)
            for r in range(NT):
                pool.wait_ge(u_kept, r + 1)
                pool.wait_ge(stats_kept, r + 1)
                pool.dma_start(rows[r], ustage[:, r % 2, :]).then_inc(u_out[r % 2], 16)
            for b in range(2):
                pool.wait_ge(u_out[b], 32)
            for i in range(NT):
                if i >= 2:
                    pool.wait_ge(o_ok, i - 1)
                pool.dma_start(ustage[:, i % 2, :], dil_rows[i * P:(i + 1) * P, :]).then_inc(u_back[i % 2], 16)

            pool.wait_ge(tables_ok, 1)

            last_row = pool.to_reg(4 * SEQ - 1)

            def store(e, b, n, on_buffer):
                pool.wait_ge(y_ok, n + 1)
                if later(on_buffer):
                    pool.wait_ge(y_out[b], on_buffer * 16)
                pool.tensor_copy(idx[b][:], slotI[:, bass.ds(e, 1)]).then_inc(idx_ok, 1)
                pool.wait_ge(tables_ok, 1)
                pool.wait_ge(idx_ok, n + 1)
                pool.indirect_dma_start(
                    out=y_rows, out_offset=bass.IndirectOffsetOnAxis(ap=idx[b][:, 0:1], axis=0),
                    in_=ye[:, b, :], in_offset=None, bounds_check=last_row, oob_is_err=False,
                ).then_inc(y_out[b], 16)

            for b in range(2):
                store(b, b, b, 0)
            with pool.Fori(1, NE // 2) as i:
                for b in range(2):
                    store(i * 2 + b, b, i * 2 + b, i)

            def pool_round(rnd):
                with pool.Fori(0, NE) as e:
                    pool.wait_ge(tables_ok, rnd + 1)
                    store(e, 0, rnd * NE + e, rnd * NE + (e - NE // 2))

            more_rounds(pool, pool_round)

        @block.tensor
        def _(pe):
            pe.wait_ge(consts, 4)

            def ada(lhs_k, rhs, first, last):
                for j in range(4):
                    mm = pe.matmul(ps[32 * j:32 * j + 32, 7, :], crep[:, lhs_k, :], rhs[:, j * CH:(j + 1) * CH],
                                   start=first, stop=last, tile_position=(0, 32 * j))
                mm.then_inc(ada_used, 1)

            def mod_columns(r):
                pe.wait_ge(mod_rows, r + 1)
                if r > 0:
                    pe.wait_ge(cols_ok, r)
                for q in range(4):
                    mm = pe.transpose(ps[:, 6, q * P:(q + 1) * P], modr[:, q * P:(q + 1) * P], ident[:])
                mm.then_inc(mod_cols, 1)

            for cc in range(KC):
                if cc == 0:
                    pe.wait_ge(xn_ok, NT)
                if cc >= 4:
                    pe.wait_ge(hT_dve if cc % 2 == 0 else hT_act, (cc - 4) // 2 + 1)
                for t in range(NT):
                    mm = pe.transpose(ps[:, cc % 4, t * P:(t + 1) * P], xn[:, t, cc * P:(cc + 1) * P], ident[:])
                mm.then_inc(hT_ps, 1)

            pe.wait_ge(crep_ok, 1)
            for k in range(KC):
                pe.wait_ge(ada_in[k], 16)
                ada(k, ada_piece(k), k == 0, k == KC - 1)
            pe.wait_ge(gn_in, 32)
            pe.transpose(ps[:, 5, 0:16], gn_rows, ident[0:16, 0:16]).then_inc(gn_T, 1)
            mod_columns(0)

            def transposes_of(u):
                m = u - QK_FIRST
                pe.wait_ge(qk_ready, m + 1)
                if m >= 2:
                    pe.wait_ge(qk_stored, m - 1)
                for q in range(4):
                    mm = pe.transpose(ps[:, 4 + m % 2, q * P:(q + 1) * P], xg[:, m % 2, q * P:(q + 1) * P], ident[:])
                mm.then_inc(qk_tr, 1)

            def split_product(out_ps, a, b, k):
                passes = ((a[0], b[0]), (a[1], b[0]), (a[0], b[1]))
                for i, (lhsT, rhs) in enumerate(passes):
                    mm = pe.matmul(out_ps, lhsT, rhs, start=(k == 0 and i == 0), stop=(k == KC - 1 and i == 2))
                return mm

            for u in range(NU):
                ch, t = divmod(u, NT)
                if t == 0:
                    pe.wait_ge(whi_ok, 2 * ch + 2)
                    pe.wait_ge(wlo_ok, 2 * ch + 2)
                if u >= 3:
                    pe.wait_ge(proj_act, u - 2)
                    if QK_FIRST <= u - 3 <= QK_LAST:
                        pe.wait_ge(gain_ok, u - 3 - QK_FIRST + 1)
                for k in range(KC):
                    if u == 0:
                        pe.wait_ge(hi_ok, k + 1)
                        pe.wait_ge(lo_ok, k + 1)
                    if ch == C_SB:
                        a = [w(ch)[:, k, t * P:(t + 1) * P] for w in (w_hi, w_lo)]
                        b = [h[:, k, :] for h in (h_hi, h_lo)]
                    else:
                        a = [h[:, k, tokens(ch, t)] for h in (h_hi, h_lo)]
                        b = [w(ch)[:, k, :] for w in (w_hi, w_lo)]
                    mm = split_product(ps[:, u % 3, :], a, b, k)
                mm.then_inc(proj_done, 1)
                if u < 2 * KC:
                    if u == 0:
                        pe.wait_ge(mod_rows, 1)
                    if u == KC:
                        mod_columns(1)
                    pe.wait_ge(ada2_in, 16 * (u + 1))
                    ada(u % KC, ada_slot, u % KC == 0, u % KC == KC - 1)
                if u == 2 * KC:
                    mod_columns(2)
                if QK_FIRST <= u - 1 <= QK_LAST:
                    transposes_of(u - 1)

            def gate(f):
                j = 6 + f // NT
                if f == 0:
                    pe.wait_ge(cols_ok, 3)
                if f % NT == 0:
                    pe.wait_ge(whi_ok, 2 * j + 2)
                    pe.wait_ge(wlo_ok, 2 * j + 2)
                if f >= 2:
                    pe.wait_ge(gate_exp, f - 1)
                for k in range(KC):
                    a = [w(j)[:, k, (f % NT) * P:(f % NT + 1) * P] for w in (w_hi, w_lo)]
                    mm = split_product(ps[:, 6 + f % 2, :], a, [h[:, k, :] for h in (h_hi, h_lo)], k)
                mm.then_inc(gate_ps, 1)

            def scores(s):
                if s == 0:
                    pe.wait_ge(qk_stored, QK_LAST - QK_FIRST + 1)
                    pe.wait_ge(proj_act, NU)
                if s >= 2:
                    pe.wait_ge(pT_act, s - 1)
                    pe.wait_ge(pT_dve, s - 1)
                S = scores_view(s)
                for h in range(NH):
                    o = HD * (h % 2)
                    w = place(h)
                    if s < NT:
                        for g in range(2):
                            pair = 2 + 2 * g + h // 2
                            mm = pe.matmul(S[:, w, g * P:(g + 1) * P], QT[o:o + HD, pair, s * P:(s + 1) * P],
                                           KT[o:o + HD, pair, s * P:(s + 1) * P], start=True, stop=True)
                    else:
                        i, k0 = s - NT, key_from(s)
                        mm = pe.matmul(S[:, w, k0:2 * P], QT[o:o + HD, h // 2, i * P:(i + 1) * P],
                                       KT[o:o + HD, h // 2, (i - 1) * P + k0:(i + 1) * P], start=True, stop=True)
                mm.then_inc(sc_ps, 1)

            def transpose_probs(s):
                pe.wait_ge(sc_exp, s + 1)
                b = s_bank(s)
                for h in range(NH):
                    for g in range(key_from(s) // P, 2):
                        mm = pe.transpose(psf[:, b * CH + (2 * h + g) * P:b * CH + (2 * h + g + 1) * P],
                                          sm[:, s % 2, h, g * P:(g + 1) * P], ident[:])
                mm.then_inc(pT_ps, 1)

            def values(s):
                pe.wait_ge(pT_act, s + 1)
                pe.wait_ge(pT_dve, s + 1)
                if s >= 2:
                    pe.wait_ge(u_kept, s - 1)
                if s - 2 >= NT:
                    pe.wait_ge(oT_ok, s - 1 - NT)
                for h in range(NH):
                    gs = range(key_from(s) // P, 2)
                    for g in gs:
                        if s < NT:
                            v = VR[:, s, g * GW + h * HD:g * GW + (h + 1) * HD]
                        else:
                            v = VN[:, s - NT - 1 + g, h * HD:(h + 1) * HD]
                        w = place(h)
                        mm = pe.matmul(ps[:, 4 + s % 2, w * HD:(w + 1) * HD],
                                       pT[:, s % 2, (2 * w + g) * P:(2 * w + g + 1) * P], v,
                                       start=(g == gs[0]), stop=(g == 1))
                mm.then_inc(u_ps, 1)

            def out_transposes(i):
                pe.wait_ge(o_ok, i + 1)
                for q in range(2):
                    mm = pe.transpose(ps[:, 4 + i % 2, 256 + q * P:256 + (q + 1) * P],
                                      o_dil[:, q * P:(q + 1) * P], ident[:])
                mm.then_inc(oT_ps, 1)

            scores(0)
            for s in range(2 * NT):
                gate(s)
                transpose_probs(s)
                if s + 1 < 2 * NT:
                    scores(s + 1)
                if s >= 1:
                    values(s - 1)
                if s - 2 >= NT:
                    out_transposes(s - 2 - NT)

            def sb_z(h):
                b = 3 * (h % 2)
                if h == 0:
                    pe.wait_ge(pT_act, 2 * NT)
                    pe.wait_ge(pT_dve, 2 * NT)
                if h == 1:
                    pe.wait_ge(oT_ok, NT)
                if h >= 2:
                    pe.wait_ge(osb_ok, h - 1)
                o = HD * (h % 2)
                for j in range(NT):
                    a = b * CH + SB_OFF[j]
                    mm = pe.matmul(psf[:, a:a + SEQ - j * P], SBT[o:o + HD, 2 + h // 2, j * P:(j + 1) * P],
                                   SBT[o:o + HD, h // 2, j * P:SEQ], start=True, stop=True)
                mm.then_inc(z_ps, 1)

            def sb_suffix(h):
                b = 3 * (h % 2)
                pe.wait_ge(sp_ok, h + 1)
                for j in range(NT):
                    for j2 in range(j, NT):
                        a = b * CH + SB_OFF[j] + (j2 - j) * P
                        mm = pe.matmul(psf[:, a:a + SEQ - j2 * P], (tri if j2 == j else ones)[:],
                                       sp_[:, SB_OFF[j2]:SB_OFF[j2] + SEQ - j2 * P],
                                       start=(j2 == j), stop=(j2 == NT - 1), skip_group_check=True)
                mm.then_inc(sf_ps, 1)

            def sb_values(h):
                pe.wait_ge(a_ok, h + 1)
                o = HD * (h % 2)
                for j in range(NT):
                    mm = pe.matmul(ps[o:o + HD, 3 * (h % 2), j * P:SEQ], VN[:, j, GW + h * HD:GW + (h + 1) * HD],
                                   zs[:, SB_OFF[j]:SB_OFF[j] + SEQ - j * P], start=(j == 0), stop=(j == NT - 1),
                                   skip_group_check=True)
                mm.then_inc(osb_ps, 1)

            gate(8)
            values(2 * NT - 1)
            out_transposes(2)
            sb_z(0)
            gate(9)
            out_transposes(3)
            for h in range(NH):
                sb_suffix(h)
                if h + 1 < NH:
                    sb_z(h + 1)
                    gate(10 + 2 * h)
                sb_values(h)
                if h + 1 < NH:
                    gate(11 + 2 * h)

            pe.wait_ge(gate_exp, 2 * KC)
            pe.wait_ge(gates_kept, 2)
            for j in range(2):
                mm = pe.matmul(ps[:, 6 + j, :], ones[32 * j:32 * j + 1, :], grow[32 * j:32 * j + 1, :],
                               start=True, stop=True)
            mm.then_inc(g1_ps, 1)
            pe.wait_ge(wb_in, 32)
            pe.wait_ge(osb_ok, NH)
            for f in range(KC):
                if f >= 2:
                    pe.wait_ge(merged, 2 * (f - 1))
                for b, oT in enumerate((OT_DIL, OT_SB)):
                    for k in range(2):
                        mm = pe.matmul(ps[:, 2 * (f % 2) + b, :], wbr[:, b, k, f * P:(f + 1) * P], oT[:, k, :],
                                       start=(k == 0), stop=(k == 1))
                mm.then_inc(br_ps, 1)
            pe.wait_ge(g1_ok, 2)
            for j in range(2):
                r = 64 + 32 * j
                mm = pe.matmul(ps[64 * j:64 * j + 64, 6, :], ones[r:r + 1, 0:64], grow[r:r + 1, :],
                               start=True, stop=True)
            mm.then_inc(g2_ps, 1)
            def transpose_h2(t):
                pe.wait_ge(xn2_ok, t + 1)
                if t >= 2:
                    pe.wait_ge(h2_dve, 4 * (t - 1))
                    pe.wait_ge(h2_act, 4 * (t - 1))
                for k in range(KC):
                    mm = pe.transpose(ps[:, 2 * (t % 2) + k // 4, (k % 4) * P:(k % 4 + 1) * P],
                                      xn[:, t, k * P:(k + 1) * P], ident[:])
                mm.then_inc(h2_ps, 1)

            def logits(t):
                pe.wait_ge(h2_dve, 4 * (t + 1))
                pe.wait_ge(h2_act, 4 * (t + 1))
                if t == 0:
                    pe.wait_ge(wr_in, 16 * 4)
                at = t * (NG + NE)
                for k in range(KC):
                    pe.matmul(ps[:, 7, at:at + NG + NE], h2t[:, t % 2, k, :], wr[:, k, :], start=(k == 0), stop=False)
                mm = pe.matmul(ps[:, 7, at:at + NG + NE], ones[0:1, :], br[:], start=False, stop=True)
                mm.then_inc(lg_ps, 1)

            pe.wait_ge(mlo_ok, KC)
            pe.wait_ge(mhi_ok, KC)
            for u in range(2 * NT):
                t, j = divmod(u, 2)
                if u < 2:
                    pe.wait_ge(whi_ok, 2 * (10 + j) + 2)
                    pe.wait_ge(wlo_ok, 2 * (10 + j) + 2)
                if u >= 2:
                    pe.wait_ge(x1_ok, u - 1)
                for k in range(KC):
                    a = [m[:, k, t * P:(t + 1) * P] for m in (m_hi, h_lo)]
                    mm = split_product(ps[:, 4 + j, :], a, [w(10 + j)[:, k, :] for w in (w_hi, w_lo)], k)
                mm.then_inc(o_ps, 1)
                if j == 1 and t >= 1:
                    transpose_h2(t - 1)
                if j == 0 and t >= 2:
                    logits(t - 2)
            logits(NT - 2)
            transpose_h2(NT - 1)
            logits(NT - 1)

            def slot_tables(done):
                for i in range(2 * NT):
                    pe.wait_ge(tb_in, done + i + 1)
                    mm = pe.matmul(ps[:, 7, 0:2 * NE], oh_view(i), tb_view(i), start=(i == 0), stop=(i == 2 * NT - 1))
                    mm.then_inc(tb_ps, 1)

            pe.wait_ge(rk_in, 2)
            pe.matmul(ps[:, 5, 0:(NT + 1) * NE], strict[:], AA5, start=True, stop=False, skip_group_check=True)
            for back in range(1, NT + 1):
                mm = pe.matmul(ps[:, 5, back * NE:(NT + 1) * NE], ones[:], AA5[:, 0:(NT + 1 - back) * NE],
                               start=False, stop=(back == NT), skip_group_check=True)
            mm.then_inc(rk_ps, 1)

            def gather(e, hb):
                pe.wait_ge(hot_ok, e + 1)
                if later(e):
                    pe.wait_ge(xe_ok, e)
                for t in range(NT):
                    for h in range(2):
                        mm = pe.matmul(ps[64 * h:64 * h + 64, 0, :], hot[:, hb, t, :],
                                       xn[:, t, h * CH:(h + 1) * CH], start=(t == 0), stop=(t == NT - 1),
                                       skip_group_check=True)
                mm.then_inc(gx_ps, 1)

            def transpose_x(e):
                pe.wait_ge(xe_ok, e + 1)
                if later(e):
                    pe.wait_ge(xt_ok, e)
                for q in range(4):
                    mm = pe.transpose(ps[:, 1, q * P:(q + 1) * P], xe[:, q * P:(q + 1) * P], ident[:])
                mm.then_inc(xt_ps, 1)

            def gate_up(e, b, loads):
                pe.wait_ge(gu_in[b], loads * 32)
                pe.wait_ge(xt_ok, e + 1)
                if later(e):
                    pe.wait_ge(h_ok, e)
                for k in range(KC):
                    for h in range(2):
                        mm = pe.matmul(ps[64 * h:64 * h + 64, 2, :], xeT[:, k % 4, k // 4, :],
                                       w_gu(b)[:, :, k, 256 * h:256 * h + 256], start=(k == 0),
                                       stop=(k == KC - 1), skip_group_check=True)
                mm.then_inc(gu_ps, 1)

            def transpose_h(e):
                pe.wait_ge(h_ok, e + 1)
                for q in range(2):
                    mm = pe.transpose(ps[:, 3, q * P:(q + 1) * P], hh[:, q * P:(q + 1) * P], ident[:])
                mm.then_inc(ht_ps, 1)

            def down(e, b, loads):
                pe.wait_ge(dn_in[b], loads * 16)
                pe.wait_ge(ht_ok, e + 1)
                if later(e):
                    pe.wait_ge(y_ok, e)
                for f in range(FE // P):
                    for h in range(2):
                        mm = pe.matmul(ps[64 * h:64 * h + 64, 4, :],
                                       hhT[:, f % 2, 64 * (f // 2):64 * (f // 2) + 64],
                                       w_dn(b)[:, f, h * CH:(h + 1) * CH], start=(f == 0),
                                       stop=(f == FE // P - 1), skip_group_check=True)
                mm.then_inc(dn_ps, 1)

            def expert(e, b, hb, loads, more=True):
                gate_up(e, b, loads)
                if not later(e):
                    slot_tables(0)
                if more:
                    gather(e + 1, 1 - hb)
                transpose_h(e)
                if more:
                    transpose_x(e + 1)
                down(e, b, loads)

            gather(0, 0)
            transpose_x(0)
            expert(0, buffer_of(0), 0, 1)
            with pe.Fori(0, (NE - 2) // (2 * NBUF)) as i:
                for j in range(1, 2 * NBUF + 1):
                    expert(i * (2 * NBUF) + j, buffer_of(j), j % 2, i * 2 + (j // NBUF + 1))
            expert(NE - 1, buffer_of(NE - 1), 1, (NE - 1) // NBUF + 1, more=False)

            def pe_round(rnd):
                slot_tables(rnd * (2 * NT))
                with pe.Fori(0, NE) as e:
                    k = rnd * NE + e
                    gather(k, 0)
                    transpose_x(k)
                    gate_up(k, 0, rnd * NE + (e - (NE - 12)))
                    transpose_h(k)
                    down(k, 0, rnd * NE + (e - (NE - 12)))

            more_rounds(pe, pe_round)

        @block.scalar
        def _(act):
            n = [0]

            def link(ins):
                n[0] += 1
                ins.then_inc(act_seq, 1)
                act.wait_ge(act_seq, n[0])

            act.dma_start(c_in[:], c[0].rearrange("(p k) -> p k", k=KC)).then_inc(c_ld, 16)
            act.wait_ge(c_ld, 16)
            act.activation(st[:, 0:KC], c_in[:], ACT.Exp, scale=-1.0).then_inc(act_seq, 1)
            n[0] += 1
            for t in range(NT):
                act.wait_ge(x_in[t], 16)
                act.activation(xn[:, t, :], xs[:, t, :], ACT.Square, accum_out=st[:, 16 + t:17 + t]
                               ).then_inc(ss_ok, 1)

            def seed(v, y, ready, count, done):
                act.wait_ge(ready, count)
                link(act.activation(y, v, ACT.Ln))
                act.activation(y, y, ACT.Exp, scale=-0.5).then_inc(done, 1)

            seed(st[:, 20:24], st[:, 24:28], var_ok, 1, seed_ok)
            for i, g in enumerate((g_norm_mix, g_norm_ffn)):
                act.dma_start(gn_rows[8 * i:8 * i + 8, :], g[0].rearrange("(k p) -> k p", p=P)
                              ).then_inc(gn_in, 16)

            def load_bias(r):
                for j in range(4):
                    lo = 2048 * r + CH * j
                    act.dma_start(modr[32 * j:32 * j + 32, :],
                                  b_ada[0:1, lo:lo + CH].to_broadcast([32, CH])).then_inc(bias_in, 16)

            load_bias(0)
            for i, g in enumerate((q_norm_g, k_norm_g)):
                act.dma_start(gains[:, i, :], g[0:1, :].to_broadcast([P, HD])).then_inc(gains_in, 16)
            act.dma_start(wr[:, :, 0:NG], w_router_group[0].rearrange("(k p) n -> p k n", p=P)).then_inc(wr_in, 16)
            act.dma_start(wr[:, :, NG:], w_router_expert[0].rearrange("(k p) n -> p k n", p=P)).then_inc(wr_in, 16)
            act.dma_start(br[:, 0:NG], b_router_group).then_inc(wr_in, 16)
            act.dma_start(br[:, NG:], b_router_expert).then_inc(wr_in, 16)

            with nc.allow_non_contiguous_dma(reason="512 positions, by token tile"):
                act.dma_start(pos_i[:, 0:NT], positions[0].rearrange("(t p) -> p t", p=P)).then_inc(pos_in, 16)
            act.dma_start(pos_i[:, NT:2 * NT], positions[0].rearrange("(p r) -> p r", r=NT)).then_inc(pos_in, 16)

            def split_hi(j, half):
                act.wait_ge(w_ld[j], 32 if j < 6 else 16)
                if half == 0:
                    if j < 3:
                        if j == 2:
                            act.wait_ge(ada_used, KC)
                    elif j < 8:
                        act.wait_ge(proj_done, NT * (j - 2))
                    else:
                        act.wait_ge(gate_ps, NT * (j - 7))
                k = half * KC // 2
                act.activation(w_hi(j)[:, k:k + KC // 2, :], w_raw(j)[:, k:k + KC // 2, :], ACT.Copy
                               ).then_inc(whi_ok, 1)

            for cc in range(1, KC, 2):
                act.wait_ge(hT_ps, cc + 1)
                act.activation(hT[:, cc, :], ps[:, cc % 4, :], ACT.Copy).then_inc(hT_act, 1)
            split_hi(0, 0)
            split_hi(0, 1)
            act.wait_ge(xn_ok, NT)
            for cc in range(KC):
                if cc % 2 == 1:
                    act.wait_ge(cols_ok, 1)
                    act.activation(hT[:, cc, :], hT[:, cc, :], ACT.Identity, scale=cols[:, 0, cc:cc + 1],
                                   bias=cols[:, 1, cc:cc + 1]).then_inc(hT_act, 1)
                    act.wait_ge(hT_act, KC // 2 + cc // 2 + 1)
                else:
                    act.wait_ge(h_full, cc // 2 + 1)
                act.activation(h_hi[:, cc, :], hT[:, cc, :], ACT.Copy).then_inc(hi_ok, 1)
            act.wait_ge(trig_arg, 1)
            act.activation(cos16[:, :, 0:HALF], cos_arg, ACT.Sin).then_inc(trig_ok, 1)
            act.activation(sin16[:, :, HALF:ROPE_DIM], sin_arg, ACT.Sin).then_inc(trig_ok, 1)
            for r in (1,):
                act.wait_ge(mod_cols, r)
                load_bias(r)

            def store_qk(u):
                m, t, ch = u - QK_FIRST, u % NT, u // NT
                act.wait_ge(qk_tr, m + 1)
                src = ps[:, 4 + m % 2, :].rearrange("p (c n) -> p c n", c=4)
                if ch == C_QK0:
                    act.activation(QT[:, 0:2, t * P:(t + 1) * P], src[:, 0:2, :], ACT.Copy).then_inc(act_seq, 1)
                    n[0] += 1
                    act.wait_ge(act_seq, n[0])
                    act.activation(KT[:, 0:2, t * P:(t + 1) * P], src[:, 2:4, :], ACT.Copy).then_inc(qk_stored, 1)
                else:
                    dst = QT if ch == C_QRES else KT
                    act.activation(dst[:, 2:6, t * P:(t + 1) * P], src, ACT.Copy).then_inc(qk_stored, 1)

            for u in range(NU):
                ch, t = divmod(u, NT)
                act.wait_ge(proj_done, u + 1)
                bank = ps[:, u % 3, :]
                if ch == C_SB:
                    act.activation(SBT[:, t, :], bank, ACT.Copy, scale=HD ** -0.5 if t < 2 else 1.0
                                   ).then_inc(proj_act, 1)
                elif ch == C_VNAT:
                    act.activation(VN[:, t, :], bank, ACT.Copy).then_inc(proj_act, 1)
                elif ch == C_VRES:
                    act.activation(VR[:, t, :], bank, ACT.Copy).then_inc(proj_act, 1)
                else:
                    m = u - QK_FIRST
                    if m >= 2:
                        act.wait_ge(rope_ok, m - 1)
                    act.activation(sq[:, m % 2, :], bank, ACT.Square).then_inc(proj_act, 1)
                    seed(st[:, 32:40], st[:, 40:48], var_ok, 1 + m + 1, seed_ok)
                if u == KC + 1:
                    act.wait_ge(mod_cols, 2)
                    act.wait_ge(gates_kept, 1)
                    load_bias(2)
                if t in (1, 2):
                    split_hi(ch + 1, t - 1)
                if QK_FIRST <= u - 1 <= QK_LAST:
                    store_qk(u - 1)

            def gate_exp_(f):
                act.wait_ge(gate_ps, f + 1)
                act.activation(gT[:, f, :], ps[:, 6 + f % 2, :], ACT.Exp, scale=-1.0).then_inc(gate_exp, 1)

            def softmax_exp(s):
                act.wait_ge(sc_max, s + 1)
                k0 = key_from(s)
                for h in range(NH):
                    ins = act.activation(sm[:, s % 2, h, k0:], sm[:, s % 2, h, k0:], ACT.Exp,
                                         bias=stat(s)[:, 8 + h:9 + h], accum_out=stat(s)[:, h:h + 1])
                    if h < NH - 1:
                        link(ins)
                ins.then_inc(sc_exp, 1)

            def probs_store(s):
                act.wait_ge(pT_ps, s + 1)
                if s >= 2:
                    act.wait_ge(u_ps, s - 1)
                b, k0 = s_bank(s), key_from(s)
                src = ps[:, b, :].rearrange("p (h n) -> p h n", h=2)[:, :, k0:]
                dst = pT[:, s % 2, 0:CH].rearrange("p (h n) -> p h n", h=2)[:, :, k0:]
                act.activation(dst, src, ACT.Copy).then_inc(pT_act, 1)

            def mix_exp(i):
                act.wait_ge(mx_ok, i + 1)
                act.activation(cstat(i)[:, 0:8], cstat(i)[:, 0:8], ACT.Exp).then_inc(mx_exp, 1)

            for s in range(2 * NT):
                softmax_exp(s)
                gate_exp_(s)
                probs_store(s)
                if s % NT in (1, 2):
                    split_hi(7 + s // NT, s % NT - 1)
                if s >= NT + 1:
                    mix_exp(s - NT - 1)
            gate_exp_(8)
            mix_exp(NT - 1)

            def sb_logs(h):
                act.wait_ge(z_ps, h + 1)
                a = lg1[:, 0:SB_COLS]
                b = 3 * (h % 2) * CH
                if h == 0:
                    act.wait_ge(u_ps, 2 * NT)
                act.activation(a, psf[:, b:b + SB_COLS], ACT.Abs).then_inc(z_abs, 1)
                act.wait_ge(z_abs, h + 1)
                link(act.activation(a, a, ACT.Exp, scale=-1.0))
                act.activation(a, a, ACT.Ln, bias=1.0).then_inc(lnz, 1)

            def sb_exp(h):
                act.wait_ge(arg_ok, h + 1)
                act.activation(zs[:, 0:SB_COLS], zs[:, 0:SB_COLS], ACT.Exp).then_inc(a_ok, 1)

            def sb_store(h):
                o = HD * (h % 2)
                act.wait_ge(osb_ps, h + 1)
                act.activation(OT_SB[o:o + HD, h // 2, :], ps[o:o + HD, 3 * (h % 2), :], ACT.Copy
                               ).then_inc(osb_ok, 1)

            sb_logs(0)
            gate_exp_(9)
            for h in range(NH):
                if h == 0:
                    split_hi(9, 0)
                    split_hi(9, 1)
                sb_exp(h)
                if h + 1 < NH:
                    sb_logs(h + 1)
                    gate_exp_(10 + 2 * h)
                if h in (1, 2):
                    split_hi(10, h - 1)
                sb_store(h)
                if h + 1 < NH:
                    gate_exp_(11 + 2 * h)
            act.wait_ge(g1_ps, 1)
            for j in range(2):
                act.activation(gate1b[:, j * CH:(j + 1) * CH], ps[:, 6 + j, :], ACT.Copy).then_inc(g1_ok, 1)
            split_hi(11, 0)
            split_hi(11, 1)
            for f in range(KC):
                act.wait_ge(m_full, f + 1)
                act.activation(m_hi[:, f, :], hT[:, f, :], ACT.Copy).then_inc(mhi_ok, 1)

            act.wait_ge(g2_ps, 1)
            act.activation(gate2h, ps[:, 6, :], ACT.Copy).then_inc(g2_ok, 1)
            def store_h2(t):
                act.wait_ge(h2_ps, t + 1)
                if t >= 2:
                    act.wait_ge(lg_ps, t - 1)
                for k in range(4, KC):
                    act.activation(h2t[:, t % 2, k, :], ps[:, 2 * (t % 2) + 1, (k - 4) * P:(k - 3) * P], ACT.Identity,
                                   scale=cols[:, 2, k:k + 1], bias=cols[:, 3, k:k + 1]).then_inc(h2_act, 1)

            for t in range(NT):
                act.wait_ge(x1_ok, 2 * t + 2)
                act.activation(xn[:, t, :], xs[:, t, :], ACT.Square, accum_out=st[:, 16 + t:17 + t]
                               ).then_inc(ss2_ok, 1)
                seed(st[:, 20 + t:21 + t], st[:, 24 + t:25 + t], var2_ok, t + 1, seed2_ok)
                if t > 0:
                    store_h2(t - 1)
            store_h2(NT - 1)
            act.wait_ge(r_arg, 1)
            act.activation(rs[:, 0:16], rs[:, 0:16], ACT.Exp).then_inc(r_exp, 1)
            act.wait_ge(r_arg, 2)
            act.activation(rs[:, 40:44], rs[:, 40:44], ACT.Exp).then_inc(r_exp, 1)

            def store_x(e):
                act.wait_ge(gx_ps, e + 1)
                if later(e):
                    act.wait_ge(xt_ps, e)
                act.activation(xe, ps[:, 0, :], ACT.Copy).then_inc(xe_ok, 1)

            def sig(e):
                act.wait_ge(gu_ps, e + 1)
                act.activation(tsig, ps[:, 2, 0:256], ACT.Exp, scale=-1.0).then_inc(sig_exp, 1)

            def expert(e, more=True):
                sig(e)
                if more:
                    store_x(e + 1)

            store_x(0)
            expert(0)
            with act.Fori(1, NE - 1) as e:
                expert(e)
            sig(NE - 1)

            def act_round(rnd):
                with act.Fori(0, NE) as e:
                    store_x(rnd * NE + e)
                    sig(rnd * NE + e)

            more_rounds(act, act_round)

        @block.vector
        def _(dve):
            n = [0]

            def link(ins):
                n[0] += 1
                ins.then_inc(dve_seq, 1)
                dve.wait_ge(dve_seq, n[0])

            dve.wait_ge(act_seq, 1)
            link(dve.tensor_scalar(st[:, 0:8], st[:, 0:8], 1.0, None, ALU.add))
            link(dve.reciprocal(st[:, 0:8], st[:, 0:8]))
            link(dve.tensor_tensor(st[:, 0:8], st[:, 0:8], c_in[:], ALU.mult))
            dve.tensor_copy(crep[:], st[:, 0:8].unsqueeze(2).to_broadcast([P, KC, 32])).then_inc(crep_ok, 1)
            def refine(v, y, tmp):
                link(dve.tensor_tensor(tmp, y, y, ALU.mult))
                link(dve.scalar_tensor_tensor(out=tmp, in0=tmp, scalar=-0.5, in1=v, op0=ALU.mult, op1=ALU.mult))
                link(dve.scalar_tensor_tensor(out=y, in0=tmp, scalar=1.5, in1=y, op0=ALU.add, op1=ALU.mult))

            dve.wait_ge(ss_ok, NT)
            dve.tensor_scalar(st[:, 20:24], st[:, 16:20], 1.0 / D, RMS_EPS, ALU.mult, ALU.add).then_inc(var_ok, 1)
            dve.wait_ge(seed_ok, 1)
            refine(st[:, 20:24], st[:, 24:28], st[:, 28:32])
            for t in range(NT):
                dve.tensor_scalar(xn[:, t, :], xs[:, t, :], st[:, 24 + t:25 + t], None, ALU.mult).then_inc(xn_ok, 1)

            def mod_round(r):
                dve.wait_ge(ada_used, KC * (r + 1))
                dve.wait_ge(bias_in, 64 * (r + 1))
                dve.tensor_tensor(modr[:], modr[:], ps[:, 7, :], ALU.add).then_inc(mod_rows, 1)
                dve.wait_ge(mod_rows, r + 1)
                if r == 1:
                    dve.tensor_copy(grow[0:64, :], modr[0:64, :]).then_inc(gates_kept, 1)
                if r == 2:
                    dve.tensor_copy(grow[64:128, :], modr[64:128, :]).then_inc(gates_kept, 1)

            def split_lo(j, half):
                dve.wait_ge(whi_ok, 2 * j + half + 1)
                k = half * KC // 2
                w = w_raw(j)[:, k:k + KC // 2, :]
                dve.tensor_tensor(w_lo(j)[:, k:k + KC // 2, :], w, w_hi(j)[:, k:k + KC // 2, :].bitcast(F32),
                                  ALU.subtract).then_inc(wlo_ok, 1)

            for cc in range(0, KC, 2):
                dve.wait_ge(hT_ps, cc + 1)
                dve.tensor_copy(hT[:, cc, :], ps[:, cc % 4, :]).then_inc(hT_dve, 1)
            split_lo(0, 0)
            split_lo(0, 1)
            mod_round(0)
            dve.wait_ge(gn_T, 1)
            link(dve.tensor_copy(gn[:], ps[:, 5, 0:16].rearrange("p (g k) -> p g k", g=2)))
            dve.wait_ge(gains_in, 32)
            link(dve.tensor_scalar(gains[:, 0, :], gains[:, 0, :], HD ** -0.5, None, ALU.mult))

            dve.wait_ge(mod_cols, 1)
            by_chunk = ps[:, 6, :].rearrange("p (q j m) -> p j q m", q=4, j=4)[:, :, :, 0]

            def two(v):
                return v.rearrange("p (j q) -> p j q", j=2)

            link(dve.tensor_copy(two(cols[:, 1, :]), by_chunk[:, 0:2, :]))
            dve.scalar_tensor_tensor(out=two(cols[:, 0, :]), in0=by_chunk[:, 2:4, :], scalar=1.0, in1=two(gn[:, 0, :]),
                                     op0=ALU.add, op1=ALU.mult).then_inc(cols_ok, 1)
            dve.wait_ge(cols_ok, 1)

            def h_low(cc):
                dve.wait_ge(hi_ok, cc + 1)
                dve.tensor_tensor(h_lo[:, cc, :], hT[:, cc, :], h_hi[:, cc, :].bitcast(F32), ALU.subtract
                                  ).then_inc(lo_ok, 1)

            dve.wait_ge(hT_dve, KC // 2)
            dve.wait_ge(hT_act, KC // 2)
            for cc in range(KC):
                if cc % 2 == 0:
                    dve.tensor_scalar(hT[:, cc, :], hT[:, cc, :], cols[:, 0, cc:cc + 1], cols[:, 1, cc:cc + 1],
                                      ALU.mult, ALU.add).then_inc(h_full, 1)
                if cc >= 1:
                    h_low(cc - 1)
            h_low(KC - 1)

            dve.wait_ge(consts, 4)
            dve.wait_ge(pool_seq, 8)
            link(dve.tensor_scalar(diff_i, diff_i, 3, None, ALU.bitwise_and))
            link(dve.tensor_scalar(diff_m, diff_i, 0.0, NEG, ALU.not_equal, ALU.mult))
            link(dve.tensor_tensor(mask12[:, 1, :], mask12[:, 1, :], diff_m, ALU.add))

            dve.wait_ge(pos_in, 32)
            A, K, C = sin_arg, trig_k, cos_arg
            link(dve.tensor_copy(grow[:, 192:200], pos_i[:]))
            for f in range(HALF):
                dve.memset(grow[:, 200 + f:201 + f], float(inv_freq[f])).then_inc(dve_seq, 1)
                n[0] += 1
            dve.wait_ge(dve_seq, n[0])
            link(dve.tensor_tensor(A, grow[:, 192:200].unsqueeze(2).to_broadcast([P, 2 * NT, HALF]),
                                   grow[:, 200:208].unsqueeze(1).to_broadcast([P, 2 * NT, HALF]), ALU.mult))
            magic = 1.5 * 2.0 ** 23
            link(dve.tensor_scalar(K, A, float(1 / (2 * np.pi)), magic, ALU.mult, ALU.add))
            link(dve.tensor_scalar(K, K, magic, None, ALU.subtract))
            for part in two_pi_parts():
                link(dve.scalar_tensor_tensor(out=A, in0=K, scalar=-part, in1=A, op0=ALU.mult, op1=ALU.add))
            link(dve.tensor_scalar(C, A, float(np.pi / 2), None, ALU.add))
            link(dve.tensor_scalar(K, C, float(np.pi), -2 * float(np.pi), ALU.is_gt, ALU.mult))
            link(dve.tensor_tensor(C, C, K, ALU.add))
            pi_in = float(np.nextafter(np.float32(np.pi), np.float32(0)))
            link(dve.tensor_scalar(C, C, pi_in, -pi_in, ALU.min, ALU.max))
            dve.tensor_scalar(A, A, pi_in, -pi_in, ALU.min, ALU.max).then_inc(trig_arg, 1)
            for u in range(NU):
                ch, t = divmod(u, NT)
                if u == 1:
                    dve.wait_ge(trig_ok, 2)
                    link(dve.tensor_copy(cos16[:, :, HALF:], cos16[:, :, 0:HALF]))
                    dve.tensor_scalar(sin16[:, :, 0:HALF], sin16[:, :, HALF:], -1.0, None, ALU.mult).then_inc(trig_ok, 1)

                if QK_FIRST <= u <= QK_LAST:
                    m = u - QK_FIRST
                    dve.wait_ge(proj_act, u + 1)
                    if m >= 2:
                        dve.wait_ge(qk_tr, m - 1)
                    if m == 0:
                        dve.wait_ge(hT_ps, KC)
                    src = ps[:, u % 3, :].rearrange("p (g h d) -> p g h d", g=2, h=4)
                    if ch == C_QK0:
                        g = gains[:].unsqueeze(2).to_broadcast([P, 2, 4, HD])
                    else:
                        g = gains[:, ch - C_QRES, :].unsqueeze(1).unsqueeze(1).to_broadcast([P, 2, 4, HD])
                    xgu = xg[:, m % 2, :]
                    dve.tensor_tensor(xgu.rearrange("p (g h d) -> p g h d", g=2, h=4), src, g, ALU.mult
                                      ).then_inc(gain_ok, 1)
                    link(dve.tensor_reduce(st[:, 48:56], sq[:, m % 2, :].rearrange("p (h d) -> p h d", h=8),
                                           AX_X, ALU.add))
                    dve.tensor_scalar(st[:, 32:40], st[:, 48:56], 1.0 / HD, RMS_EPS, ALU.mult, ALU.add
                                      ).then_inc(var_ok, 1)
                    dve.wait_ge(seed_ok, 1 + m + 1)
                    refine(st[:, 32:40], st[:, 40:48], st[:, 48:56])
                    dve.wait_ge(rope_ok, m + 1)
                    xh = xgu.rearrange("p (h d) -> p h d", h=8)
                    dve.tensor_tensor(xh, xh, st[:, 40:48].unsqueeze(2).to_broadcast([P, 8, HD]), ALU.mult
                                      ).then_inc(qk_ready, 1)
                if t in (1, 2):
                    split_lo(ch + 1, t - 1)
                if u == KC - 1:
                    mod_round(1)
                if u == KC + 1:
                    dve.wait_ge(mod_cols, 2)
                    dve.tensor_copy(two(cols[:, 3, :]), by_chunk[:, 2:4, :]).then_inc(cols_ok, 1)
                if u == 2 * KC - 1:
                    mod_round(2)
                if u == 2 * KC + 1:
                    dve.wait_ge(mod_cols, 3)
                    dve.scalar_tensor_tensor(out=two(cols[:, 2, :]), in0=by_chunk[:, 0:2, :], scalar=1.0,
                                             in1=two(gn[:, 1, :]), op0=ALU.add, op1=ALU.mult).then_inc(cols_ok, 1)

            def softmax_max(s):
                dve.wait_ge(sc_ps, s + 1)
                if s == 0:
                    dve.wait_ge(qk_tr, QK_LAST - QK_FIRST + 1)
                    dve.wait_ge(ada_used, 3 * KC)
                if s >= 2:
                    dve.wait_ge(pT_ps, s - 1)
                k0 = key_from(s)
                m = mask12 if s < NT else mask0.rearrange("p (g n) -> p g n", g=2)
                m = m[:, k0 // P:2, :].unsqueeze(1).to_broadcast([P, NH, 2 - k0 // P, P])
                S = scores_view(s)[:, :, k0:].rearrange("p h (g n) -> p h g n", n=P)
                d = sm[:, s % 2, :, k0:]
                link(dve.tensor_tensor(d.rearrange("p h (g n) -> p h g n", n=P), S, m, ALU.add))
                link(dve.tensor_reduce(stat(s)[:, 4:8], d, AX_X, ALU.max))
                dve.tensor_scalar(stat(s)[:, 8:12], stat(s)[:, 4:8], -1.0, None, ALU.mult).then_inc(sc_max, 1)

            def probs_store(s):
                dve.wait_ge(pT_ps, s + 1)
                if s >= 2:
                    dve.wait_ge(u_ps, s - 1)
                b, k0 = s_bank(s), key_from(s)
                src = ps[:, b + 1, :].rearrange("p (h n) -> p h n", h=2)[:, :, k0:]
                dst = pT[:, s % 2, CH:2 * CH].rearrange("p (h n) -> p h n", h=2)[:, :, k0:]
                dve.tensor_copy(dst, src).then_inc(pT_dve, 1)

            def keep_u(s):
                dve.wait_ge(u_ps, s + 1)
                if s >= 2:
                    dve.wait_ge(u_out[s % 2], 16)
                dve.tensor_copy(ustage[:, s % 2, 0:GW], ps[:, 4 + s % 2, 0:GW]).then_inc(u_kept, 1)
                dve.tensor_copy(ustage[:, s % 2, GW:GW + 8], stat(s)[:, 0:8]).then_inc(stats_kept, 1)

            def mix_args(i):
                s = NT + i
                dve.wait_ge(sc_exp, s + 1)
                dve.wait_ge(u_back[i % 2], 16 * (i // 2 + 1))
                m12, m0 = ustage[:, i % 2, GW + 4:GW + 8], stat(s)[:, 4:8]
                cs = cstat(i)
                link(dve.tensor_tensor(cs[:, 8:12], m0, m12, ALU.max))
                link(dve.tensor_tensor(cs[:, 0:4], m0, cs[:, 8:12], ALU.subtract))
                dve.tensor_tensor(cs[:, 4:8], m12, cs[:, 8:12], ALU.subtract).then_inc(mx_ok, 1)

            def mix(i):
                s, cs = NT + i, cstat(i)
                dve.wait_ge(mx_exp, i + 1)
                link(dve.tensor_tensor(cs[:, 8:12], cs[:, 0:4], stat(s)[:, 0:4], ALU.mult))
                link(dve.tensor_tensor(cs[:, 12:16], cs[:, 4:8], ustage[:, i % 2, GW:GW + 4], ALU.mult))
                link(dve.tensor_tensor(cs[:, 8:12], cs[:, 8:12], cs[:, 12:16], ALU.add))
                link(dve.reciprocal(cs[:, 8:12], cs[:, 8:12]))
                link(dve.tensor_tensor(cs[:, 0:4], cs[:, 0:4], cs[:, 8:12], ALU.mult))
                link(dve.tensor_tensor(cs[:, 4:8], cs[:, 4:8], cs[:, 8:12], ALU.mult))
                dve.wait_ge(u_ps, s + 1)
                if i > 0:
                    dve.wait_ge(oT_ps, i)
                od = o_dil.rearrange("p (b a d) -> p a b d", a=2, b=2)
                u12 = ustage[:, i % 2, 0:GW].rearrange("p (a b d) -> p a b d", a=2, b=2)

                def by_head(v):
                    return v.rearrange("p (a b) -> p a b", a=2).unsqueeze(3).to_broadcast([P, 2, 2, HD])

                link(dve.tensor_tensor(u12, u12, by_head(cs[:, 4:8]), ALU.mult))
                dve.tensor_tensor(od, ps[:, 4 + s % 2, 0:GW].rearrange("p (a b d) -> p a b d", a=2, b=2),
                                  by_head(cs[:, 0:4]), ALU.mult).then_inc(u_kept, 1)
                dve.wait_ge(u_kept, s + 1)
                dve.tensor_tensor(od, od, u12, ALU.add).then_inc(o_ok, 1)

            def out_T(i):
                dve.wait_ge(oT_ps, i + 1)
                dve.tensor_copy(OT_DIL[:, :, i * P:(i + 1) * P],
                                ps[:, 4 + i % 2, 256:512].rearrange("p (c n) -> p c n", c=2)).then_inc(oT_ok, 1)

            def gate_finish(f):
                dve.wait_ge(gate_exp, f + 1)
                link(dve.tensor_scalar(gT[:, f, :], gT[:, f, :], 1.0, None, ALU.add))
                dve.reciprocal(gT[:, f, :], gT[:, f, :]).then_inc(gate_ok, 1)

            softmax_max(0)
            for s in range(2 * NT):
                gate_finish(s)
                probs_store(s)
                if s + 1 < 2 * NT:
                    softmax_max(s + 1)
                if s % NT in (1, 2):
                    split_lo(7 + s // NT, s % NT - 1)
                if 1 <= s <= NT:
                    keep_u(s - 1)
                if s >= NT + 1:
                    mix_args(s - NT - 1)
                    mix(s - NT - 1)
                if s - 2 >= NT:
                    out_T(s - 2 - NT)
            gate_finish(8)
            mix_args(NT - 1)
            mix(NT - 1)
            out_T(2)

            def sb_copy(h):
                dve.wait_ge(z_ps, h + 1)
                dve.wait_ge(z_abs, h + 1)
                if h == 0:
                    dve.wait_ge(u_ps, 2 * NT)
                else:
                    dve.wait_ge(osb_ps, h)
                b = 3 * (h % 2) * CH
                dve.tensor_copy(zs[:, 0:SB_COLS], psf[:, b:b + SB_COLS]).then_inc(z_cp, 1)

            def diag(v):
                return v[:, 0:1536].rearrange("p (a n) -> p a n", a=3)[:, :, 0:P], v[:, SB_OFF[3]:SB_OFF[3] + P]

            def sb_softplus(h):
                dve.wait_ge(lnz, h + 1)
                dve.wait_ge(z_cp, h + 1)
                if h > 0:
                    dve.wait_ge(sf_ps, h)
                link(dve.scalar_tensor_tensor(out=sp_[:, 0:SB_COLS], in0=zs[:, 0:SB_COLS], scalar=0.0,
                                              in1=lg1[:, 0:SB_COLS], op0=ALU.max, op1=ALU.add))
                a, b = diag(sp_)
                link(dve.tensor_tensor(a, a, strict[:].unsqueeze(1).to_broadcast([P, 3, P]), ALU.mult))
                dve.tensor_tensor(b, b, strict[:], ALU.mult).then_inc(sp_ok, 1)

            def sb_args(h):
                dve.wait_ge(sf_ps, h + 1)
                b = 3 * (h % 2) * CH
                link(dve.tensor_tensor(zs[:, 0:SB_COLS], zs[:, 0:SB_COLS], psf[:, b:b + SB_COLS], ALU.subtract))
                a, b = diag(zs)
                link(dve.tensor_tensor(a, a, negstrict.unsqueeze(1).to_broadcast([P, 3, P]), ALU.add))
                dve.tensor_tensor(b, b, negstrict, ALU.add).then_inc(arg_ok, 1)

            sb_copy(0)
            sb_softplus(0)
            gate_finish(9)
            out_T(3)
            for h in range(NH):
                if h == 0:
                    split_lo(9, 0)
                    split_lo(9, 1)
                sb_args(h)
                if h >= 2:
                    split_lo(10, h - 2)
                if h + 1 < NH:
                    gate_finish(10 + 2 * h)
                    sb_copy(h + 1)
                    sb_softplus(h + 1)
                    gate_finish(11 + 2 * h)

            dve.wait_ge(gate_ok, 2 * KC)
            def merged_low(f):
                dve.wait_ge(mhi_ok, f + 1)
                dve.tensor_tensor(h_lo[:, f, :], hT[:, f, :], m_hi[:, f, :].bitcast(F32), ALU.subtract
                                  ).then_inc(mlo_ok, 1)

            for f in range(KC):
                dve.wait_ge(br_ps, f + 1)
                dve.tensor_tensor(gT[:, f, :], gT[:, f, :], ps[:, 2 * (f % 2), :], ALU.mult).then_inc(merged, 1)
                dve.tensor_tensor(gT[:, KC + f, :], gT[:, KC + f, :], ps[:, 2 * (f % 2) + 1, :], ALU.mult
                                  ).then_inc(merged, 1)
                dve.wait_ge(merged, 2 * f + 2)
                dve.tensor_tensor(hT[:, f, :], gT[:, f, :], gT[:, KC + f, :], ALU.add).then_inc(m_full, 1)
                if f in (0, 1):
                    split_lo(11, f)
                if f >= 1:
                    merged_low(f - 1)
            merged_low(KC - 1)

            def store_h2(t):
                dve.wait_ge(h2_ps, t + 1)
                if t >= 2:
                    dve.wait_ge(lg_ps, t - 1)
                for k in range(4):
                    dve.tensor_scalar(h2t[:, t % 2, k, :], ps[:, 2 * (t % 2), k * P:(k + 1) * P], cols[:, 2, k:k + 1],
                                      cols[:, 3, k:k + 1], ALU.mult, ALU.add).then_inc(h2_dve, 1)

            dve.wait_ge(g1_ok, 2)
            for u in range(2 * NT):
                t, j = divmod(u, 2)
                dve.wait_ge(o_ps, u + 1)
                link(dve.tensor_tensor(ps[:, 4 + j, :], ps[:, 4 + j, :], gate1b[:, j * CH:(j + 1) * CH], ALU.mult))
                if j == 0:
                    dve.wait_ge(x_in[t], 32)
                xt = xs[:, t, j * CH:(j + 1) * CH]
                dve.tensor_tensor(xt, xt, ps[:, 4 + j, :], ALU.add).then_inc(x1_ok, 1)
                if j == 1:
                    dve.wait_ge(ss2_ok, t + 1)
                    dve.tensor_scalar(st[:, 20 + t:21 + t], st[:, 16 + t:17 + t], 1.0 / D, RMS_EPS,
                                      ALU.mult, ALU.add).then_inc(var2_ok, 1)
                    dve.wait_ge(seed2_ok, t + 1)
                    refine(st[:, 20 + t:21 + t], st[:, 24 + t:25 + t], st[:, 28 + t:29 + t])
                    dve.tensor_scalar(xn[:, t, :], xs[:, t, :], st[:, 24 + t:25 + t], None, ALU.mult
                                      ).then_inc(xn2_ok, 1)
                    if t > 0:
                        store_h2(t - 1)
            store_h2(NT - 1)

            def one_hot(e, hb, gathers=None):
                if gathers is None:
                    gathers = e - 1
                if later(e) and later(gathers):
                    dve.wait_ge(gx_ps, gathers)
                dve.tensor_tensor(hot[:, hb], iot[:, 0:1, :].to_broadcast([P, NT, CAP]),
                                  RE[:, :, bass.ds(e, 1)].to_broadcast([P, NT, CAP]), ALU.is_equal
                                  ).then_inc(hot_ok, 1)

            dve.wait_ge(lg_ps, NT)
            dve.wait_ge(slot_consts, 3)
            dve.memset(RK[:, 0, :], 0.0).then_inc(rk_in, 1)
            link(dve.tensor_copy(lg, ps[:, 7, 0:NT * (NG + NE)].rearrange("p (t n) -> p t n", t=NT)))
            G, E = lg[:, :, 0:NG], lg[:, :, NG:].rearrange("p t (g e) -> p t g e", g=NG)
            row = lambda i: rs[:, 44 + 4 * i:48 + 4 * i]
            gmax, best, v1, v2, pg, w1, w2, tmp4 = (row(i) for i in range(8))
            gex = rs[:, 0:16].rearrange("p (t g) -> p t g", t=NT)
            goh = rs[:, 76:92].rearrange("p (t g) -> p t g", t=NT)
            lsel = rs[:, 92:124].rearrange("p (t e) -> p t e", t=NT)
            o1 = rs[:, 124:156].rearrange("p (t e) -> p t e", t=NT)
            o2 = rs[:, 156:188].rearrange("p (t e) -> p t e", t=NT)
            num = iot[:, 0, 0:EPG]

            def first_max(onehot, vals, top, width):
                full = [P, NT, width]
                link(dve.tensor_reduce(top, vals, AX_X, ALU.max))
                link(dve.tensor_tensor(onehot, vals, top.unsqueeze(2).to_broadcast(full), ALU.is_equal))
                back = rt[:, 0:NT * width].rearrange("p (t e) -> p t e", t=NT)
                link(dve.tensor_scalar(rt[:, 64:64 + width], num[:, 0:width], -float(EPG), None, ALU.add))
                link(dve.tensor_tensor(back, onehot, rt[:, 64:64 + width].unsqueeze(1).to_broadcast(full), ALU.mult))
                link(dve.tensor_reduce(best, back, AX_X, ALU.min))
                link(dve.tensor_tensor(onehot, back, best.unsqueeze(2).to_broadcast(full), ALU.is_equal))

            first_max(goh, G, gmax, NG)
            dve.tensor_tensor(gex, G, gmax.unsqueeze(2).to_broadcast([P, NT, NG]), ALU.subtract).then_inc(r_arg, 1)
            pick = rt.rearrange("p (t g e) -> p t g e", t=NT, g=NG)
            link(dve.tensor_tensor(pick, E, goh.unsqueeze(3).to_broadcast([P, NT, NG, EPG]), ALU.mult))
            link(dve.tensor_reduce(lsel, pick.rearrange("p t g e -> p t e g"), AX_X, ALU.add))
            first_max(o1, lsel, v1, EPG)
            link(dve.scalar_tensor_tensor(out=lsel, in0=o1, scalar=NEG, in1=lsel, op0=ALU.mult, op1=ALU.add))
            first_max(o2, lsel, v2, EPG)
            dve.tensor_tensor(rs[:, 40:44], v2, v1, ALU.subtract).then_inc(r_arg, 1)
            dve.wait_ge(r_exp, 2)
            link(dve.tensor_reduce(pg, gex, AX_X, ALU.add))
            link(dve.tensor_scalar(w1, rs[:, 40:44], 1.0, None, ALU.add))
            link(dve.tensor_tensor(w1, w1, pg, ALU.mult))
            link(dve.reciprocal(w1, w1))
            link(dve.tensor_tensor(w2, w1, rs[:, 40:44], ALU.mult))
            full = [P, NT, NG, EPG]
            for a, o in ((A1, o1), (A2, o2)):
                link(dve.tensor_tensor(a.rearrange("p t (g e) -> p t g e", g=NG),
                                       goh.unsqueeze(3).to_broadcast(full), o.unsqueeze(2).to_broadcast(full), ALU.mult))
            dve.tensor_tensor(AA, A1, A2, ALU.add).then_inc(rk_in, 1)
            dve.wait_ge(rk_in, 2)
            dve.wait_ge(rk_ps, 1)
            link(dve.tensor_copy(RK, ps[:, 5, 0:NT * NE].rearrange("p (t e) -> p t e", t=NT)))
            link(dve.scalar_tensor_tensor(out=RE, in0=RK, scalar=1.0, in1=AA, op0=ALU.add, op1=ALU.mult))
            link(dve.tensor_scalar(RE, RE, -1.0, None, ALU.add))
            one_hot(0, 0)
            link(dve.tensor_reduce(tmp4[:, 0:1], ps[:, 5, 4 * NE:5 * NE], AX_X, ALU.max))
            link(dve.tensor_scalar(cnt_i[:], tmp4[:, 0:1], -1.0, None, ALU.add))
            rk4 = rs[:, 188:196].rearrange("p (j t) -> p j t", j=2)
            rt3 = rt.rearrange("p (t e) -> p t e", t=NT)
            for j, a in enumerate((A1, A2)):
                link(dve.tensor_tensor(rt3, a, RK, ALU.mult))
                link(dve.tensor_reduce(rk4[:, j, :], rt3, AX_X, ALU.add))
            code = rs[:, 196:204].rearrange("p (j t) -> p j t", j=2)
            for j in range(2):
                link(dve.tensor_scalar(code[:, j, :], tokc[:], float(j), None, ALU.add))

            def slot_tables(done, step):
                for i in range(2 * NT):
                    j, t = divmod(i, NT)
                    dve.wait_ge(tb_ps, done + max(i - 1, 0))
                    step(dve.tensor_scalar(oh_view(i), iot[:].rearrange("p a s -> p (a s)"), rk4[:, j, t:t + 1],
                                           None, ALU.is_equal))
                    a, w = (A1, w1) if j == 0 else (A2, w2)
                    step(dve.tensor_scalar(tb_view(i)[:, 0:NE], a[:, t, :], code[:, j, t:t + 1], None, ALU.mult))
                    dve.tensor_scalar(tb_view(i)[:, NE:2 * NE], a[:, t, :], w[:, t:t + 1], None, ALU.mult
                                      ).then_inc(tb_in, 1)
                dve.wait_ge(tb_ps, done + 2 * NT)
                step(dve.tensor_copy(slotW, ps[:, 7, NE:2 * NE]))
                dve.tensor_scalar(slotI, ps[:, 7, 0:NE], 2.0, halfc[:, 0:1], ALU.mult, ALU.add
                                  ).then_inc(tables_ok, 1)


            def store_xT(e):
                dve.wait_ge(xt_ps, e + 1)
                full = [P, 4, 2, CAP]
                a2 = cols[:, 2, :].rearrange("p (h q) -> p q h", h=2).unsqueeze(3).to_broadcast(full)
                b2 = cols[:, 3, :].rearrange("p (h q) -> p q h", h=2).unsqueeze(3).to_broadcast(full)
                xm = xmul.rearrange("p (q h s) -> p q h s", q=4, h=2)
                dve.tensor_tensor(xm, ps[:, 1, :].rearrange("p (q h s) -> p q h s", q=4, h=2), a2, ALU.mult
                                  ).then_inc(moe_dve, 1)
                return xm, b2

            NSTEP = 5

            def store_xT2(e, xm, b2, step):
                dve.wait_ge(moe_dve, step)
                if later(e):
                    dve.wait_ge(gu_ps, e)
                dve.tensor_tensor(xeT, xm, b2, ALU.add).then_inc(xt_ok, 1)

            def expert(e, hb, stores, more=True, col=None):
                s0 = e * NSTEP + 1
                if more:
                    one_hot(e + 1, 1 - hb)
                if later(e):
                    dve.wait_ge(y_ok, e)
                col = e if col is None else col
                dve.tensor_copy(wcol[:], slotW[:, bass.ds(col, 1)]).then_inc(moe_dve, 1)
                dve.wait_ge(sig_exp, e + 1)
                dve.tensor_scalar(tden, tsig, 1.0, None, ALU.add).then_inc(moe_dve, 1)
                dve.wait_ge(moe_dve, s0 + 2)
                dve.reciprocal(tden, tden).then_inc(moe_dve, 1)
                dve.wait_ge(moe_dve, s0 + 3)
                dve.tensor_tensor(tden, tden, ps[:, 2, 0:256], ALU.mult).then_inc(moe_dve, 1)
                dve.wait_ge(moe_dve, s0 + 4)
                dve.tensor_tensor(hh, tden, ps[:, 2, 256:512], ALU.mult).then_inc(h_ok, 1)
                dve.wait_ge(ht_ps, e + 1)
                dve.tensor_copy(hhT, ps[:, 3, 0:256].rearrange("p (q n) -> p q n", q=2)).then_inc(ht_ok, 1)
                if more:
                    xm, b2 = store_xT(e + 1)
                    store_xT2(e + 1, xm, b2, s0 + 5)
                dve.wait_ge(dn_ps, e + 1)
                if later(stores):
                    dve.wait_ge(y_out[hb], stores * 16)
                dve.scalar_tensor_tensor(out=ye[:, hb, :], in0=ps[:, 4, :], scalar=wcol[:, 0:1], in1=gate2h,
                                         op0=ALU.mult, op1=ALU.mult).then_inc(y_ok, 1)

            xm, b2 = store_xT(0)
            store_xT2(0, xm, b2, 1)
            slot_tables(0, link)
            dve.wait_ge(tables_ok, 1)
            dve.wait_ge(g2_ok, 1)
            for j in range(2):
                expert(j, j, 0)
            with dve.Fori(1, NE // 2 - 1) as i:
                for j in range(2):
                    expert(i * 2 + j, j, i)
            expert(NE - 2, 0, NE // 2 - 1)
            expert(NE - 1, 1, NE // 2 - 1, more=False)

            def dve_round(rnd):
                dve.wait_ge(y_out[1], 16 * (NE // 2))
                dve.wait_ge(y_out[0], rnd * (16 * NE) - 16 * (NE // 2))
                at = [0]

                def step(ins):
                    at[0] += 1
                    ins.then_inc(round_seq, 1)
                    dve.wait_ge(round_seq, (rnd - 1) * ROUND_STEPS + at[0])

                step(dve.tensor_scalar(rs[:, 188:196], rs[:, 188:196], -float(CAP), None, ALU.add))
                step(dve.tensor_scalar(RE, RE, -float(CAP), None, ALU.add))
                slot_tables(rnd * (2 * NT), step)
                assert at[0] == ROUND_STEPS
                with dve.Fori(0, NE) as e:
                    dve.wait_ge(tables_ok, rnd + 1)
                    k = rnd * NE + e
                    one_hot(e, 0, k)
                    xm, b2 = store_xT(k)
                    store_xT2(k, xm, b2, k * NSTEP + 1)
                    expert(k, 0, rnd * NE + (e - NE // 2), more=False, col=e)

            ROUND_STEPS = 3 + 4 * NT
            more_rounds(dve, dve_round)

            for t in range(NT):
                dve.wait_ge(y_back[t], 16)
                y = arena[:, 2048 * t:2048 * (t + 1)].rearrange("p (j n) -> p j n", j=2)
                link(dve.tensor_tensor(xs[:, t, :], xs[:, t, :], y[:, 0, :], ALU.add))
                dve.tensor_tensor(xs[:, t, :], xs[:, t, :], y[:, 1, :], ALU.add).then_inc(fin_ok, 1)


_INS = ['x', 'c', 'positions', 'w_ada', 'b_ada', 'g_norm_mix', 'g_norm_ffn', 'w_in', 'w_branch_gate',
        'q_norm_g', 'k_norm_g', 'w_branch_dil', 'w_branch_sb', 'w_out', 'w_router_group',
        'b_router_group', 'w_router_expert', 'b_router_expert', 'w_expert_gate', 'w_expert_up',
        'w_expert_down']


def kernel(**inputs):
    import numpy as _np
    import concourse.bacc as _bacc
    from concourse import mybir as _mybir
    from concourse.bass_utils import run_bass_kernel_spmd as _run

    nc = _bacc.Bacc("TRN2", target_bir_lowering=False, num_devices=1)
    arrays, args = {}, []
    for name in _INS:
        a = _np.ascontiguousarray(inputs[name])
        arrays[f"in_{name}"] = a
        args.append(nc.dram_tensor(f"in_{name}", a.shape, _mybir.dt.from_np(a.dtype), kind="ExternalInput").ap())
    out = nc.dram_tensor("out", (1, SEQ, D), F32, kind="ExternalOutput").ap()
    hybrid_layer(nc, *args, out)
    r = _run(nc, [arrays], core_ids=[0])
    return r.results[0]["out"]
```

```python
from contextlib import ExitStack

import numpy as np

import concourse.bass as bass
from concourse import mybir

ALU = mybir.AluOpType
ACT = mybir.ActivationFunctionType
F32 = mybir.dt.float32
F32R = mybir.dt.float32r
I32 = mybir.dt.int32
AX_X = mybir.AxisListType.X

P = 128
D = 1024
SEQ = 512
NT = SEQ // P
KC = D // P
HD = 64
NH = 4
GW = NH * HD
ROPE_DIM = HD // 4
HALF = ROPE_DIM // 2
ROPE_THETA = 500000.0
RMS_EPS = 1e-6
NG = 4
EPG = 8
NE = NG * EPG
FE = 512
CAP = 64
ROUNDS = SEQ // CAP
CH = 512
NEG = -1e30
UNUSED = 4096.0
SLOT_W = KC * CH
EXP_W = 3 * SLOT_W
NBUF = 3

QA, KA, VA = 0, 3 * GW, 6 * GW
QB, KB, VB = 9 * GW, 10 * GW, 11 * GW
C_SB, C_VNAT, C_QK0, C_QRES, C_KRES, C_VRES = range(6)
SB_OFF = [0, 512, 1024, 896]
SB_COLS = 1280


def two_pi_parts():
    rest, parts = np.float64(2 * np.pi), []
    for bits in (8, 8, 8):
        e = int(np.floor(np.log2(rest))) - bits + 1
        part = np.floor(rest / 2.0 ** e) * 2.0 ** e
        parts.append(float(part))
        rest = rest - part
    return parts + [float(np.float32(rest))]


def hybrid_layer(nc, x, c, positions, w_ada, b_ada, g_norm_mix, g_norm_ffn, w_in, w_branch_gate,
                 q_norm_g, k_norm_g, w_branch_dil, w_branch_sb, w_out, w_router_group,
                 b_router_group, w_router_expert, b_router_expert, w_expert_gate, w_expert_up,
                 w_expert_down, out):
    inv_freq = np.float32(ROPE_THETA) ** (-np.arange(0, ROPE_DIM, 2, dtype=np.float32) / np.float32(ROPE_DIM))

    ctx = ExitStack()
    with ctx:
        def sb(name, shape, dt=F32):
            return ctx.enter_context(nc.sbuf_tensor(name, shape, dt))

        def sem(name):
            return ctx.enter_context(nc.semaphore(name))

        dil_rows = nc.dram_tensor("dil_rows", (SEQ, GW + 2 * NH), F32, kind="Internal").ap()
        y_rows = nc.dram_tensor("y_rows", (SEQ * 2 * 2, CH), F32, kind="Internal").ap()

        with nc.sbuf_tensor("arena", [P, NBUF * EXP_W], F32) as arena, \
                nc.sbuf_tensor("xs", [P, NT, D], F32) as xs, \
                nc.sbuf_tensor("hT", [P, KC, SEQ], F32) as hT:
            pass
        slot_r = [sb(f"slot_r{j}", [P, KC, CH], F32R) for j in range(3 * NBUF)]
        xs_r = sb("xs_r", [P, NT, D], F32R)
        hT_r = sb("hT_r", [P, KC, SEQ], F32R)
        xn = sb("xn", [P, NT, D])
        ident = sb("ident", [P, P])
        ones = sb("ones", [P, P])
        strict = sb("strict", [P, P])
        tri = sb("tri", [P, P])
        small = sb("small", [P, 1168])
        wr = sb("wr", [P, KC, NG + NE])
        br = sb("br", [1, NG + NE])
        gains = sb("gains", [P, 2, HD])
        trig = sb("trig", [P, 2 * 2 * NT * ROPE_DIM])
        cos16, sin16 = (trig[:, P * i:P * i + P].rearrange("p (t d) -> p t d", t=2 * NT) for i in range(2))
        crep_f = sb("crep", [P, KC * 32])
        crep = crep_f[:].rearrange("p (k m) -> p k m", k=KC)
        modr = sb("modr", [P, CH])
        grow = sb("grow", [P, CH])
        cols = sb("cols", [P, 4, KC])
        gn = sb("gn", [P, 2, KC])
        st = sb("st", [P, 64])
        pos_i = sb("pos_i", [P, 2 * NT], I32)
        c_in = sb("c_in", [P, KC])

        mask12 = small[:, 0:256].rearrange("p (g n) -> p g n", g=2)
        mask0 = small[:, 256:512]
        negstrict = small[:, 512:640]
        ustage = small[:, 640:1168].rearrange("p (b n) -> p b n", b=2)

        gn_rows = small[0:16, 640:768]
        diff_i, diff_m = small[:, 912:1040].bitcast(I32), small[:, 1040:1168]
        stats = sb("stats", [P, 4, 12])
        cstats = sb("cstats", [P, 2, 16])
        o_dil = small[:, 0:GW]

        def stat(s):
            return stats[:, s % 4, :]

        def cstat(i):
            return cstats[:, i % 2, :]

        def pair(j):
            return j % 3 if j < 6 else j % 2

        def w_raw(j):
            at = 2 * pair(j) * SLOT_W
            return arena[:, at:at + SLOT_W].rearrange("p (k n) -> p k n", k=KC)

        def w_part(j, i):
            return slot_r[2 * pair(j) + i]

        def w_half(w, j, half):
            return w[:, :, half * 256:half * 256 + 256] if j == 0 else w[:, half * KC // 2:(half + 1) * KC // 2, :]

        def w_lo(j):
            return w_part(j, 0)

        def w_hi(j):
            return w_part(j, 1)

        base = 2 * EXP_W
        QT = arena[:, base:base + 3072].rearrange("p (c n) -> p c n", c=6)
        KT = arena[:, base + 3072:base + 6144].rearrange("p (c n) -> p c n", c=6)
        VN = arena[:, base + 6144:base + 8192].rearrange("p (t n) -> p t n", t=NT)
        VR = arena[:, base + 8192:base + 10240].rearrange("p (t n) -> p t n", t=NT)
        SBT = arena[:, base + 10240:base + 12288].rearrange("p (c n) -> p c n", c=4)
        OT_DIL = QT[:, 0:2, :]
        OT_SB = SBT[:, 0:2, :]
        gT = arena[:, 4 * SLOT_W:6 * SLOT_W].rearrange("p (c n) -> p c n", c=2 * KC)
        wbr = arena[:, base + 1024:base + 1024 + SLOT_W].rearrange("p (b k n) -> p b k n", b=2, k=2)

        h_hi = xs_r[:].rearrange("p t n -> p (t n)").rearrange("p (c n) -> p c n", c=KC)
        h_lo = hT_r[:]
        m_hi = slot_r[4]
        x1t = arena[:, 5 * SLOT_W:5 * SLOT_W + 2 * KC * P].rearrange("p (b k n) -> p b k n", b=2, k=KC)
        xnf = xn[:].rearrange("p t n -> p (t n)")
        ada_slot = xnf[:, 0:2048]
        xg = xnf[:, 2048:3072].rearrange("p (b n) -> p b n", b=2)
        sq = xnf[:, 3072:4096].rearrange("p (b n) -> p b n", b=2)
        sm = xnf[:, 0:2048].rearrange("p (b h n) -> p b h n", b=2, h=NH)
        pT = xnf[:, 2048:4096].rearrange("p (b n) -> p b n", b=2)
        zs, lg1, sp_ = xnf[:, 0:1536], xnf[:, 1280:2816], xnf[:, 2560:4096]
        gate1b = xn[:, NT - 1, :]

        def ada_piece(k):
            at = base + 2048 * k if k < 6 else 5 * SLOT_W + 2048 * (k - 6)
            return arena[:, at:at + 2048]

        def w_gu(b):
            return arena[:, b * EXP_W:b * EXP_W + 2 * SLOT_W].rearrange("p (g k n) -> p g k n", g=2, k=KC)

        def w_dn(b):
            return arena[:, b * EXP_W + 2 * SLOT_W:(b + 1) * EXP_W].rearrange("p (f n) -> p f n", f=FE // P)

        wk = hT[:].rearrange("p c n -> p (c n)")
        xe = wk[:, 0:512]
        xeT = wk[:, 512:1024].rearrange("p (q h s) -> p q h s", q=4, h=2)
        xmul = wk[:, 1024:1536]
        hh = wk[:, 1536:1792]
        hhT = wk[:, 1792:2048].rearrange("p (q n) -> p q n", q=2)
        tsig = wk[:, 2048:2304]
        tden = wk[:, 2304:2560]
        ye = wk[:, 2560:3584].rearrange("p (b n) -> p b n", b=2)
        hot = wk[:, 3584:4096].rearrange("p (b t s) -> p b t s", b=2, t=NT)
        gate2h = modr[:]

        RA = small[:, 0:640]
        AA5 = RA[:, 2 * P:2 * P + (NT + 1) * NE]
        A1, A2, AA, RK, RE = (RA[:, 128 * i:128 * i + 128].rearrange("p (t e) -> p t e", t=NT) for i in range(5))
        lg = small[:, 640:784].rearrange("p (t n) -> p t n", t=NT)
        rt = small[:, 784:912]
        slotW = small[:, 912:944]
        slotI = small[:, 944:976].bitcast(I32)

        tb_rows = wk[:, 2560:3520].rearrange("p (b n) -> p b n", b=5)
        tb_more = grow[:, 0:2 * 3 * HD].rearrange("p (b n) -> p b n", b=2)

        def tb_buffer(i):
            return small[:, 976:1168] if i == 0 else tb_rows[:, i - 1, :] if i < 6 else tb_more[:, i - 6, :]

        def oh_view(i):
            return tb_buffer(i)[:, 0:2 * CAP]

        def tb_view(i):
            return tb_buffer(i)[:, 2 * CAP:2 * CAP + 2 * NE]

        rs = trig[:, 0:208]
        sin_arg, trig_k, cos_arg = (grow[:, 64 * i:64 * i + 64].rearrange("p (t f) -> p t f", t=2 * NT)
                                    for i in range(3))
        idx = [sb(f"idx{b}", [P, 1], I32) for b in range(2)]
        wcol = sb("wcol", [P, 1])
        iot = crep_f[:, 0:2 * CAP].rearrange("p (a s) -> p a s", a=2)
        tokc = crep_f[:, 2 * CAP:2 * CAP + NT]
        lgc = crep_f[:, 3 * CAP:3 * CAP + NG + NE]
        halfc = crep_f[:, 2 * CAP + NT:2 * CAP + NT + 1]
        cnt_i = sb("cnt_i", [P, 1], I32)

        ps = ctx.enter_context(nc.psum_tensor("ps", [P, 8, CH], F32))
        psf = ps[:].rearrange("p b n -> p (b n)")

        x_in = [sem(f"x_in{t}") for t in range(NT)]
        pos_in, c_ld, gains_in, wr_in = sem("pos_in"), sem("c_ld"), sem("gains_in"), sem("wr_in")
        bias_in = sem("bias_in")
        ada_in = [sem(f"ada_in{k}") for k in range(8)]
        ada2_in = sem("ada2_in")
        w_ld = [sem(f"w_ld{j}") for j in range(10)]
        w_first = sem("w_first")
        wb_in = [sem(f"wb_in{b}") for b in range(2)]
        consts = sem("consts")
        slot_consts = sem("slot_consts")
        pool_seq = sem("pool_seq")
        dve_seq = sem("dve_seq")
        act_seq = sem("act_seq")
        gn_T = sem("gn_T")
        crep_ok = sem("crep_ok")
        ada_used = sem("ada_used")
        mod_rows = sem("mod_rows")
        mod_cols = sem("mod_cols")
        gates_kept = sem("gates_kept")
        cols_ok = sem("cols_ok")
        trig_arg, trig_ok = sem("trig_arg"), sem("trig_ok")
        ss_ok, var_ok, seed_ok, xn_ok = sem("ss_ok"), sem("var_ok"), sem("seed_ok"), sem("xn_ok")
        hT_ps, hT_dve, hT_act = sem("hT_ps"), sem("hT_dve"), sem("hT_act")
        h_full, hi_ok, lo_ok = sem("h_full"), sem("hi_ok"), sem("lo_ok")
        whi_ok, wlo_ok, wlo_pool = sem("whi_ok"), sem("wlo_ok"), sem("wlo_pool")
        m_full, mhi_ok, mlo_ok = sem("m_full"), sem("mhi_ok"), sem("mlo_ok")
        proj_done, proj_act, gain_ok = sem("proj_done"), sem("proj_act"), sem("gain_ok")
        rope_ok, qk_ready, qk_tr, qk_stored = sem("rope_ok"), sem("qk_ready"), sem("qk_tr"), sem("qk_stored")
        gate_ps, gate_exp, gate_ok = sem("gate_ps"), sem("gate_exp"), sem("gate_ok")
        sc_ps, sc_max, sc_exp = sem("sc_ps"), sem("sc_max"), sem("sc_exp")
        pT_ps, pT_act, pT_dve = sem("pT_ps"), sem("pT_act"), sem("pT_dve")
        u_ps, u_kept, stats_kept = sem("u_ps"), sem("u_kept"), sem("stats_kept")
        u_out = [sem(f"u_out{i}") for i in range(2)]
        u_back = [sem(f"u_back{i}") for i in range(2)]
        mx_ok, mx_exp, o_ok, oT_ps, oT_ok = sem("mx_ok"), sem("mx_exp"), sem("o_ok"), sem("oT_ps"), sem("oT_ok")
        z_ps, z_abs, z_cp, lnz, sp_ok = sem("z_ps"), sem("z_abs"), sem("z_cp"), sem("lnz"), sem("sp_ok")
        sf_ps, arg_ok, a_ok, osb_ps, osb_ok = sem("sf_ps"), sem("arg_ok"), sem("a_ok"), sem("osb_ps"), sem("osb_ok")
        dil_ps, dil_ok, br_ps, merged = sem("dil_ps"), sem("dil_ok"), sem("br_ps"), sem("merged")
        g1_ps, g1_ok, o_ps, x1_ok = sem("g1_ps"), sem("g1_ok"), sem("o_ps"), sem("x1_ok")
        ss2_ok, var2_ok, seed2_ok, xn2_ok = sem("ss2_ok"), sem("var2_ok"), sem("seed2_ok"), sem("xn2_ok")
        rstd_ok = sem("rstd_ok")
        x1t_ps, x1t_dve, x1t_act, lg_ps = sem("x1t_ps"), sem("x1t_dve"), sem("x1t_act"), sem("lg_ps")
        b2w_ps, b2w_ok = sem("b2w_ps"), sem("b2w_ok")
        r_arg, r_exp, rk_in, rk_ps, tb_in, tb_ps, tables_ok = (
            sem("r_arg"), sem("r_exp"), sem("rk_in"), sem("rk_ps"), sem("tb_in"), sem("tb_ps"), sem("tables_ok"))
        g2_ps, g2_ok = sem("g2_ps"), sem("g2_ok")
        gu_in = [[sem(f"gu_in{b}_{kh}") for kh in range(2)] for b in range(NBUF)]
        dn_in = [sem(f"dn_in{b}") for b in range(NBUF)]
        hot_ok, gx_ps, xe_ok, xt_ps, xt_ok = sem("hot_ok"), sem("gx_ps"), sem("xe_ok"), sem("xt_ps"), sem("xt_ok")
        gu_ps, sig_exp, h_ok, ht_ps, ht_ok = sem("gu_ps"), sem("sig_exp"), sem("h_ok"), sem("ht_ps"), sem("ht_ok")
        dn_ps, idx_ok, y_ok = sem("dn_ps"), sem("idx_ok"), sem("y_ok")
        y_out = [sem(f"y_out{b}") for b in range(2)]
        moe_dve = sem("moe_dve")
        round_seq = sem("round_seq")
        fin_ok, out_st = sem("fin_ok"), sem("out_st")

        block = ctx.enter_context(nc.Block())

        def w_in_cols(ch):
            return {C_SB: (QB, KB), C_VNAT: (VA, VB), C_QK0: (QA, KA), C_QRES: (QA + GW, QA + 2 * GW),
                    C_KRES: (KA + GW, KA + 2 * GW), C_VRES: (VA + GW, VA + 2 * GW)}[ch]

        def tokens(ch, t):
            return slice(t, SEQ, NT) if ch in (C_QRES, C_KRES, C_VRES) else slice(t * P, (t + 1) * P)

        NU = 6 * NT
        QK_FIRST, QK_LAST = C_QK0 * NT, C_KRES * NT + NT - 1

        def s_bank(s):
            return 2 * (s % 2)

        def scores_view(s):
            b = s_bank(s)
            return psf[:, b * CH:(b + 2) * CH].rearrange("p (h n) -> p h n", h=NH)

        def gate_bank(f):
            return 6 + f % 2 if f < 10 else 6

        def dil_bank(f):
            return 6 if f == 6 else 7

        def place(h):
            return 2 * (h % 2) + h // 2

        def key_from(s):
            return P if s == NT else 0

        def buffer_of(e):
            return (NBUF - 1 + e) % NBUF

        def later(e):
            return not isinstance(e, int) or e > 0

        def more_rounds(eng, body):
            eng.wait_ge(tables_ok, 1)
            top = eng.value_load(cnt_i[0:1, 0:1], min_val=0, max_val=SEQ - 1)
            with eng.If(top + 1 > CAP):
                with eng.Fori(1, ROUNDS) as rnd:
                    with eng.If(top + 1 > rnd * CAP):
                        body(rnd)
            return top

        @block.sync
        def _(sp):
            for t in range(NT):
                sp.dma_start(xs[:, t, :], x[0, t * P:(t + 1) * P, :]).then_inc(x_in[t], 16)
            ada_rows = w_ada[0].rearrange("(p k) n -> p k n", k=KC)

            w_in_r = w_in[0].rearrange("(k p) n -> p k n", p=P)
            w_bg_r = w_branch_gate[0].rearrange("(k p) n -> p k n", p=P)

            def load_half(ch, h):
                c0 = w_in_cols(ch)[h]
                sp.dma_start(w_raw(ch)[:, :, h * 256:(h + 1) * 256], w_in_r[:, :, c0:c0 + 256]
                             ).then_inc(w_first if (ch, h) == (0, 0) else w_ld[ch], 16)

            for k in range(KC):
                sp.dma_start(ada_piece(k), ada_rows[:, k, 0:2048]).then_inc(ada_in[k], 16)
                if k == 4:
                    load_half(0, 0)
            load_half(0, 1)
            sp.wait_ge(hT_ps, KC)
            sp.dma_start(ada_slot, ada_rows[:, 0, 2048:4096]).then_inc(ada2_in, 16)
            load_half(1, 0)
            load_half(1, 1)
            for n in range(1, 2 * KC):
                sp.wait_ge(ada_used, KC + n)
                lo = 2048 * (1 + n // KC)
                sp.dma_start(ada_slot, ada_rows[:, n % KC, lo:lo + 2048]).then_inc(ada2_in, 16)
                if n in (1, 2):
                    load_half(2, n - 1)
                elif n % NT in (0, 1):
                    ch = n // NT + 2
                    sp.wait_ge(proj_done, NT * (ch - 2))
                    load_half(ch, n % NT)
            for j in range(4):
                if j < 2:
                    sp.wait_ge(proj_done, NT * (j + 4))
                else:
                    sp.wait_ge(gate_ps, NT * (j - 1))
                sp.dma_start(w_raw(6 + j), w_bg_r[:, :, j * CH:(j + 1) * CH]).then_inc(w_ld[6 + j], 16)
            sp.wait_ge(sc_ps, 2 * NT)
            for b, w in enumerate((w_branch_dil, w_branch_sb)):
                sp.dma_start(wbr[:, b], w[0].rearrange("(k p) n -> p k n", p=P)).then_inc(wb_in[b], 16)
            for j in range(2):
                sp.wait_ge(gate_ps, NT * (j + 3))
                sp.dma_start(w_raw(10 + j), w_out[0].rearrange("(k p) n -> p k n", p=P)[:, :, j * CH:(j + 1) * CH]
                             ).then_inc(w_ld[6 + j], 16)
            for t in range(NT):
                sp.dma_start(xs[:, t, :], x[0, t * P:(t + 1) * P, :]).then_inc(x_in[t], 16)

            def load_gu_half(e, b, kh):
                rows = slice(kh * D // 2, (kh + 1) * D // 2)
                ks = slice(kh * KC // 2, (kh + 1) * KC // 2)
                for g, w in enumerate((w_expert_gate, w_expert_up)):
                    src = w[0, bass.ds(e, 1), rows].rearrange("e (k p) n -> p (e k) n", p=P)
                    sp.dma_start(w_gu(b)[:, g, ks], src).then_inc(gu_in[b][kh], 16)

            def load_gu(e, b):
                for kh in range(2):
                    load_gu_half(e, b, kh)

            def load_dn(e, b):
                src = w_expert_down[0, bass.ds(e, 1)].rearrange("e (k p) n -> p (e k) n", p=P)
                sp.dma_start(w_dn(b), src).then_inc(dn_in[b], 16)

            sp.wait_ge(br_ps, KC)
            load_gu(0, 2)
            load_dn(0, 2)
            sp.wait_ge(o_ps, NT)
            load_gu(1, 0)
            sp.wait_ge(o_ps, 2 * NT)
            load_dn(1, 0)
            sp.wait_ge(lg_ps, NT)
            load_gu(2, 1)
            load_dn(2, 1)

            def refill(e, b, last, loads):
                sp.wait_ge(gu_ps, e + 1)
                load_gu_half(e + NBUF, b, 0)
                sp.wait_ge(gu_in[last][1], loads * 32)
                load_gu_half(e + NBUF, b, 1)
                sp.wait_ge(dn_ps, e + 1)
                load_dn(e + NBUF, b)

            with sp.Fori(0, 9) as i:
                for j in range(NBUF):
                    refill(i * NBUF + j, buffer_of(j), buffer_of(j + 2), i + ((j + 2) // NBUF + 1))
            for e in (27, 28):
                refill(e, buffer_of(e), buffer_of(e + 2), (e + 2) // NBUF + 1)


            def sp_round(rnd):
                with sp.Fori(0, NE) as e:
                    sp.wait_ge(dn_ps, rnd * NE + e)
                    load_gu(e, 0)
                    load_dn(e, 0)

            top = more_rounds(sp, sp_round)
            sp.wait_ge(y_out[1], 16 * (NE // 2))
            sp.wait_ge(y_out[0], (top // CAP) * (16 * NE) + 16 * (NE // 2))
            for t in range(NT):
                sp.dma_start(arena[:, 2048 * t:2048 * (t + 1)],
                             y_rows[4 * P * t:4 * P * (t + 1), :].rearrange("(p r) n -> p (r n)", r=4)
                             ).then_inc(x_in[t], 16)
            for t in range(NT):
                sp.wait_ge(fin_ok, t + 1)
                sp.dma_start(out[0, t * P:(t + 1) * P, :], xs[:, t, :]).then_inc(out_st, 16)
            sp.wait_ge(out_st, 16 * NT)

        @block.gpsimd
        def _(pool):
            n = [0]

            def link(ins):
                n[0] += 1
                ins.then_inc(pool_seq, 1)
                pool.wait_ge(pool_seq, n[0])

            link(pool.memset(ident[:], 0.0))
            link(pool.affine_select(ident[:], ident[:], [[-1, P]], ALU.not_equal, 1.0, base=0, channel_multiplier=1))
            pool.memset(ones[:], 1.0).then_inc(consts, 1)
            link(pool.memset(strict[:], 0.0))
            pool.affine_select(strict[:], strict[:], [[-1, P]], ALU.is_ge, 1.0, base=0,
                               channel_multiplier=1).then_inc(consts, 1)
            link(pool.memset(tri[:], 0.0))
            pool.affine_select(tri[:], tri[:], [[1, P]], ALU.is_gt, 1.0, base=0,
                               channel_multiplier=-1).then_inc(consts, 1)
            link(pool.memset(small[:, 0:640], 0.0))
            link(pool.affine_select(mask12, mask12, [[0, 2], [-1, P]], ALU.is_ge, NEG, base=0, channel_multiplier=1))
            pool.iota(diff_i, [[-1, P]], base=2 * P, channel_multiplier=1).then_inc(consts, 1)
            link(pool.affine_select(mask0, mask0, [[1, 2 * P]], ALU.is_ge, NEG, base=0, channel_multiplier=-1))
            link(pool.affine_select(mask0, mask0, [[-1, 2 * P]], ALU.is_ge, NEG, base=P, channel_multiplier=1))
            link(pool.affine_select(negstrict, negstrict, [[1, P]], ALU.is_gt, NEG, base=0, channel_multiplier=-1))
            for u in range(QK_FIRST, QK_LAST + 1):
                m, t, ch = u - QK_FIRST, u % NT, u // NT
                tt = t + (NT if ch != C_QK0 else 0)
                v = xg[:, m % 2, :].rearrange("p (h d) -> p h d", h=8)
                xr = v[:, :, 0:ROPE_DIM]
                swp = sq[:, m % 2, 0:128].rearrange("p (h d) -> p h d", h=8)
                csb = cos16[:, tt:tt + 1, :].to_broadcast([P, 8, ROPE_DIM])
                snb = sin16[:, tt:tt + 1, :].to_broadcast([P, 8, ROPE_DIM])
                if m == 0:
                    pool.wait_ge(trig_ok, 3)
                pool.wait_ge(var_ok, 1 + m + 1)
                pool.wait_ge(gain_ok, m + 1)
                pool.tensor_tensor(swp[:, :, 0:HALF], xr[:, :, HALF:ROPE_DIM], snb[:, :, 0:HALF],
                                   ALU.mult).then_inc(pool_seq, 1)
                pool.tensor_tensor(swp[:, :, HALF:ROPE_DIM], xr[:, :, 0:HALF], snb[:, :, HALF:ROPE_DIM],
                                   ALU.mult).then_inc(pool_seq, 1)
                n[0] += 2
                pool.wait_ge(pool_seq, n[0])
                link(pool.tensor_tensor(xr, xr, csb, ALU.mult))
                pool.tensor_tensor(xr, xr, swp, ALU.add).then_inc(rope_ok, 1)

            pool.wait_ge(ada_used, 3 * KC)
            pool.iota(iot[:], [[0, 2], [1, CAP]], base=1, channel_multiplier=0,
                      allow_small_or_imprecise_dtypes=True).then_inc(slot_consts, 1)
            pool.iota(tokc[:], [[2 * P, NT]], base=-int(UNUSED), channel_multiplier=2,
                      allow_small_or_imprecise_dtypes=True).then_inc(slot_consts, 1)
            link(pool.memset(halfc[:, :], 2 * UNUSED))
            pool.wait_ge(slot_consts, 2)
            pool.memset(halfc[64:128, :], 2 * UNUSED + 1).then_inc(slot_consts, 1)
            pool.wait_ge(slot_consts, 3)

            def split_lo(j, half):
                pool.wait_ge(whi_ok, 2 * j + half + 1)
                pool.tensor_tensor(w_half(w_lo(j), j, half), w_half(w_raw(j), j, half),
                                   w_half(w_hi(j), j, half).bitcast(F32), ALU.subtract).then_inc(wlo_pool, 1)

            rows = dil_rows.rearrange("(a r) n -> r a n", r=NT)
            for r in range(NT):
                pool.wait_ge(u_kept, r + 1)
                pool.wait_ge(stats_kept, r + 1)
                pool.dma_start(rows[r], ustage[:, r % 2, :]).then_inc(u_out[r % 2], 16)
                if r < 2:
                    split_lo(7, r)
            for b in range(2):
                pool.wait_ge(u_out[b], 32)
            for i in range(NT):
                if i >= 2:
                    pool.wait_ge(o_ok, i - 1)
                pool.dma_start(ustage[:, i % 2, :], dil_rows[i * P:(i + 1) * P, :]).then_inc(u_back[i % 2], 16)
                if i in (1, 2):
                    split_lo(8, i - 1)

            for j in (9, 10, 11):
                for half in range(2):
                    split_lo(j, half)
            for f in range(KC):
                pool.wait_ge(mhi_ok, f + 1)
                pool.tensor_tensor(h_lo[:, f, :], hT[:, f, :], m_hi[:, f, :].bitcast(F32), ALU.subtract
                                   ).then_inc(mlo_ok, 1)

            pool.wait_ge(tables_ok, 1)

            last_row = pool.to_reg(4 * SEQ - 1)

            def store(e, b, n, on_buffer):
                pool.wait_ge(y_ok, n + 1)
                if later(on_buffer):
                    pool.wait_ge(y_out[b], on_buffer * 16)
                pool.tensor_copy(idx[b][:], slotI[:, bass.ds(e, 1)]).then_inc(idx_ok, 1)
                pool.wait_ge(tables_ok, 1)
                pool.wait_ge(idx_ok, n + 1)
                pool.indirect_dma_start(
                    out=y_rows, out_offset=bass.IndirectOffsetOnAxis(ap=idx[b][:, 0:1], axis=0),
                    in_=ye[:, b, :], in_offset=None, bounds_check=last_row, oob_is_err=False,
                ).then_inc(y_out[b], 16)

            for b in range(2):
                store(b, b, b, 0)
            with pool.Fori(1, NE // 2) as i:
                for b in range(2):
                    store(i * 2 + b, b, i * 2 + b, i)

            def pool_round(rnd):
                with pool.Fori(0, NE) as e:
                    pool.wait_ge(tables_ok, rnd + 1)
                    store(e, 0, rnd * NE + e, rnd * NE + (e - NE // 2))

            more_rounds(pool, pool_round)

        @block.tensor
        def _(pe):
            pe.wait_ge(consts, 4)

            def ada(lhs_k, rhs, first, last):
                for j in range(4):
                    mm = pe.matmul(ps[32 * j:32 * j + 32, 7, :], crep[:, lhs_k, :], rhs[:, j * CH:(j + 1) * CH],
                                   start=first, stop=last, tile_position=(0, 32 * j))
                mm.then_inc(ada_used, 1)

            def mod_columns(r):
                pe.wait_ge(mod_rows, r + 1)
                if r > 0:
                    pe.wait_ge(cols_ok, r)
                for q in range(4):
                    mm = pe.transpose(ps[:, 6, q * P:(q + 1) * P], modr[:, q * P:(q + 1) * P], ident[:])
                mm.then_inc(mod_cols, 1)

            for cc in range(KC):
                if cc == 0:
                    pe.wait_ge(xn_ok, NT)
                if cc >= 4:
                    pe.wait_ge(hT_dve if cc % 2 == 0 else hT_act, (cc - 4) // 2 + 1)
                for t in range(NT):
                    mm = pe.transpose(ps[:, cc % 4, t * P:(t + 1) * P], xn[:, t, cc * P:(cc + 1) * P], ident[:])
                mm.then_inc(hT_ps, 1)

            pe.wait_ge(crep_ok, 1)
            for k in range(KC):
                pe.wait_ge(ada_in[k], 16)
                ada(k, ada_piece(k), k == 0, k == KC - 1)
            pe.wait_ge(gains_in, 64)
            pe.transpose(ps[:, 5, 0:16], gn_rows, ident[0:16, 0:16]).then_inc(gn_T, 1)
            mod_columns(0)

            def transposes_of(u):
                m = u - QK_FIRST
                pe.wait_ge(qk_ready, m + 1)
                if m >= 2:
                    pe.wait_ge(qk_stored, m - 1)
                for q in range(4):
                    mm = pe.transpose(ps[:, 4 + m % 2, q * P:(q + 1) * P], xg[:, m % 2, q * P:(q + 1) * P], ident[:])
                mm.then_inc(qk_tr, 1)

            def split_product(out_ps, a, b, k):
                passes = ((a[0], b[0]), (a[1], b[0]), (a[0], b[1]))
                for i, (lhsT, rhs) in enumerate(passes):
                    mm = pe.matmul(out_ps, lhsT, rhs, start=(k == 0 and i == 0), stop=(k == KC - 1 and i == 2))
                return mm

            for u in range(NU):
                ch, t = divmod(u, NT)
                if u == 0:
                    pe.wait_ge(whi_ok, 1)
                    pe.wait_ge(wlo_ok, 1)
                elif t == 0 or u == 2:
                    pe.wait_ge(whi_ok, 2 * ch + 2)
                    pe.wait_ge(wlo_ok, 2 * ch + 2)
                if u >= 3:
                    pe.wait_ge(proj_act, u - 2)
                    if QK_FIRST <= u - 3 <= QK_LAST:
                        pe.wait_ge(gain_ok, u - 3 - QK_FIRST + 1)
                for k in range(KC):
                    if u == 0:
                        pe.wait_ge(hi_ok, k + 1)
                        pe.wait_ge(lo_ok, k + 1)
                    if ch == C_SB:
                        a = [w(ch)[:, k, t * P:(t + 1) * P] for w in (w_hi, w_lo)]
                        b = [h[:, k, :] for h in (h_hi, h_lo)]
                    else:
                        a = [h[:, k, tokens(ch, t)] for h in (h_hi, h_lo)]
                        b = [w(ch)[:, k, :] for w in (w_hi, w_lo)]
                    mm = split_product(ps[:, u % 3, :], a, b, k)
                mm.then_inc(proj_done, 1)
                if u < 2 * KC:
                    if u == 0:
                        pe.wait_ge(mod_rows, 1)
                    if u == KC:
                        mod_columns(1)
                    pe.wait_ge(ada2_in, 16 * (u + 1))
                    ada(u % KC, ada_slot, u % KC == 0, u % KC == KC - 1)
                if u == 2 * KC:
                    mod_columns(2)
                if QK_FIRST <= u - 1 <= QK_LAST:
                    transposes_of(u - 1)

            def gate(f):
                j = 6 + f // NT
                if f == 0:
                    pe.wait_ge(cols_ok, 3)
                if f % NT == 0:
                    pe.wait_ge(whi_ok, 2 * j + 2)
                    if j == 6:
                        pe.wait_ge(wlo_ok, 2 * j + 2)
                    else:
                        pe.wait_ge(wlo_pool, 2 * (j - 7) + 2)
                if f > 10:
                    pe.wait_ge(gate_exp, f)
                elif f >= 2:
                    pe.wait_ge(gate_exp, f - 1)
                for k in range(KC):
                    a = [w(j)[:, k, (f % NT) * P:(f % NT + 1) * P] for w in (w_hi, w_lo)]
                    mm = split_product(ps[:, gate_bank(f), :], a, [h[:, k, :] for h in (h_hi, h_lo)], k)
                mm.then_inc(gate_ps, 1)

            def scores(s):
                if s == 0:
                    pe.wait_ge(qk_stored, QK_LAST - QK_FIRST + 1)
                    pe.wait_ge(proj_act, NU)
                if s >= 2:
                    pe.wait_ge(pT_act, s - 1)
                    pe.wait_ge(pT_dve, s - 1)
                S = scores_view(s)
                for h in range(NH):
                    o = HD * (h % 2)
                    w = place(h)
                    if s < NT:
                        for g in range(2):
                            pair = 2 + 2 * g + h // 2
                            mm = pe.matmul(S[:, w, g * P:(g + 1) * P], QT[o:o + HD, pair, s * P:(s + 1) * P],
                                           KT[o:o + HD, pair, s * P:(s + 1) * P], start=True, stop=True)
                    else:
                        i, k0 = s - NT, key_from(s)
                        mm = pe.matmul(S[:, w, k0:2 * P], QT[o:o + HD, h // 2, i * P:(i + 1) * P],
                                       KT[o:o + HD, h // 2, (i - 1) * P + k0:(i + 1) * P], start=True, stop=True)
                mm.then_inc(sc_ps, 1)

            def transpose_probs(s):
                pe.wait_ge(sc_exp, s + 1)
                b = s_bank(s)
                for h in range(NH):
                    for g in range(key_from(s) // P, 2):
                        mm = pe.transpose(psf[:, b * CH + (2 * h + g) * P:b * CH + (2 * h + g + 1) * P],
                                          sm[:, s % 2, h, g * P:(g + 1) * P], ident[:])
                mm.then_inc(pT_ps, 1)

            def values(s):
                pe.wait_ge(pT_act, s + 1)
                pe.wait_ge(pT_dve, s + 1)
                if s >= 2:
                    pe.wait_ge(u_kept, s - 1)
                if s - 2 >= NT:
                    pe.wait_ge(oT_ok, s - 1 - NT)
                for h in range(NH):
                    gs = range(key_from(s) // P, 2)
                    for g in gs:
                        if s < NT:
                            v = VR[:, s, g * GW + h * HD:g * GW + (h + 1) * HD]
                        else:
                            v = VN[:, s - NT - 1 + g, h * HD:(h + 1) * HD]
                        w = place(h)
                        mm = pe.matmul(ps[:, 4 + s % 2, w * HD:(w + 1) * HD],
                                       pT[:, s % 2, (2 * w + g) * P:(2 * w + g + 1) * P], v,
                                       start=(g == gs[0]), stop=(g == 1))
                mm.then_inc(u_ps, 1)

            def out_transposes(i):
                pe.wait_ge(o_ok, i + 1)
                for q in range(2):
                    mm = pe.transpose(ps[:, 4 + i % 2, 256 + q * P:256 + (q + 1) * P],
                                      o_dil[:, q * P:(q + 1) * P], ident[:])
                mm.then_inc(oT_ps, 1)

            scores(0)
            for s in range(2 * NT):
                gate(s)
                transpose_probs(s)
                if s + 1 < 2 * NT:
                    scores(s + 1)
                if s >= 1:
                    values(s - 1)
                if s - 2 >= NT:
                    out_transposes(s - 2 - NT)

            def sb_z(h):
                b = 3 * (h % 2)
                if h == 0:
                    pe.wait_ge(pT_act, 2 * NT)
                    pe.wait_ge(pT_dve, 2 * NT)
                if h == 1:
                    pe.wait_ge(oT_ok, NT)
                if h >= 2:
                    pe.wait_ge(osb_ok, h - 1)
                o = HD * (h % 2)
                for j in range(NT):
                    a = b * CH + SB_OFF[j]
                    mm = pe.matmul(psf[:, a:a + SEQ - j * P], SBT[o:o + HD, 2 + h // 2, j * P:(j + 1) * P],
                                   SBT[o:o + HD, h // 2, j * P:SEQ], start=True, stop=True)
                mm.then_inc(z_ps, 1)

            def sb_suffix(h):
                b = 3 * (h % 2)
                pe.wait_ge(sp_ok, h + 1)
                for j in range(NT):
                    for j2 in range(j, NT):
                        a = b * CH + SB_OFF[j] + (j2 - j) * P
                        mm = pe.matmul(psf[:, a:a + SEQ - j2 * P], (tri if j2 == j else ones)[:],
                                       sp_[:, SB_OFF[j2]:SB_OFF[j2] + SEQ - j2 * P],
                                       start=(j2 == j), stop=(j2 == NT - 1), skip_group_check=True)
                mm.then_inc(sf_ps, 1)

            def sb_values(h):
                pe.wait_ge(a_ok, h + 1)
                o = HD * (h % 2)
                for j in range(NT):
                    mm = pe.matmul(ps[o:o + HD, 3 * (h % 2), j * P:SEQ], VN[:, j, GW + h * HD:GW + (h + 1) * HD],
                                   zs[:, SB_OFF[j]:SB_OFF[j] + SEQ - j * P], start=(j == 0), stop=(j == NT - 1),
                                   skip_group_check=True)
                mm.then_inc(osb_ps, 1)

            def dil_product(f):
                if f == 0:
                    pe.wait_ge(wb_in[0], 16)
                    pe.wait_ge(oT_ok, NT)
                    pe.wait_ge(gate_exp, 10)
                elif f == 6:
                    pe.wait_ge(gate_exp, 2 * KC)
                else:
                    pe.wait_ge(dil_ok, f if f < 6 else f - 1)
                for k in range(2):
                    mm = pe.matmul(ps[:, dil_bank(f), :], wbr[:, 0, k, f * P:(f + 1) * P], OT_DIL[:, k, :],
                                   start=(k == 0), stop=(k == 1))
                mm.then_inc(dil_ps, 1)

            EARLY = 3

            def sb_product(f, k):
                return pe.matmul(ps[:, f % 4, :], wbr[:, 1, k, f * P:(f + 1) * P], OT_SB[:, k, :],
                                 start=(k == 0), stop=(k == 1), skip_group_check=True)

            gate(8)
            values(2 * NT - 1)
            out_transposes(2)
            sb_z(0)
            gate(9)
            out_transposes(3)
            for h in range(NH):
                sb_suffix(h)
                if h + 1 < NH:
                    sb_z(h + 1)
                    gate(10 + 2 * h)
                dil_product(2 * h)
                if h == NH - 1:
                    dil_product(2 * h + 1)
                    pe.wait_ge(wb_in[1], 16)
                    pe.wait_ge(osb_ok, NH - 1)
                    for f in range(EARLY):
                        sb_product(f, 0)
                sb_values(h)
                if h + 1 < NH:
                    gate(11 + 2 * h)
                    dil_product(2 * h + 1)
            pe.wait_ge(osb_ok, NH)
            for f in range(KC):
                if f >= 4:
                    pe.wait_ge(merged, f - 3)
                if f >= EARLY:
                    sb_product(f, 0)
                sb_product(f, 1).then_inc(br_ps, 1)
            pe.wait_ge(gate_exp, 2 * KC)
            pe.wait_ge(dil_ok, KC)
            pe.wait_ge(gates_kept, 2)
            for j in range(2):
                mm = pe.matmul(ps[:, 6 + j, :], ones[32 * j:32 * j + 1, :], grow[32 * j:32 * j + 1, :],
                               start=True, stop=True)
            mm.then_inc(g1_ps, 1)
            pe.wait_ge(g1_ok, 2)
            for j in range(2):
                r = 64 + 32 * j
                mm = pe.matmul(ps[64 * j:64 * j + 64, 6, :], ones[r:r + 1, 0:64], grow[r:r + 1, :],
                               start=True, stop=True)
            mm.then_inc(g2_ps, 1)
            pe.wait_ge(wr_in, 16 * 4)
            pe.wait_ge(cols_ok, 3)
            for k in range(KC):
                mm = pe.matmul(ps[0:1, 7, 0:NG + NE], cols[:, 3, k:k + 1], wr[:, k, :], start=(k == 0), stop=(k == KC - 1))
            mm.then_inc(b2w_ps, 1)

            def transpose_x1(t):
                pe.wait_ge(x1_ok, NT + t + 1)
                if t >= 2:
                    pe.wait_ge(x1t_dve, t - 1)
                    pe.wait_ge(x1t_act, t - 1)
                for k in range(KC):
                    mm = pe.transpose(ps[:, 2 * (t % 2) + k // 4, (k % 4) * P:(k % 4 + 1) * P],
                                      xs[:, t, k * P:(k + 1) * P], ident[:])
                mm.then_inc(x1t_ps, 1)

            def logits(t):
                pe.wait_ge(x1t_dve, t + 1)
                pe.wait_ge(x1t_act, t + 1)
                if t == 0:
                    pe.wait_ge(b2w_ok, 3)
                    pe.wait_ge(g2_ok, 1)
                at = 64 * (t // 2)
                for k in range(KC):
                    mm = pe.matmul(ps[:, 6 + t % 2, at:at + NG + NE], x1t[:, t % 2, k, :], wr[:, k, :], start=(k == 0),
                                   stop=(k == KC - 1))
                mm.then_inc(lg_ps, 1)

            for u in range(2 * NT):
                j, t = divmod(u, NT)
                if t == 0:
                    pe.wait_ge(whi_ok, 2 * (10 + j) + 2)
                    pe.wait_ge(wlo_pool, 2 * (10 + j - 7) + 2)
                if u >= 2:
                    pe.wait_ge(x1_ok, u - 1)
                for k in range(KC):
                    if u == 0:
                        pe.wait_ge(mhi_ok, k + 1)
                        pe.wait_ge(mlo_ok, k + 1)
                    if j == 1 and t >= 1 and k == KC // 2:
                        transpose_x1(t - 1)
                    a = [m[:, k, t * P:(t + 1) * P] for m in (m_hi, h_lo)]
                    mm = split_product(ps[:, 4 + u % 2, :], a, [w(10 + j)[:, k, :] for w in (w_hi, w_lo)], k)
                mm.then_inc(o_ps, 1)
                if u == 0:
                    pe.wait_ge(b2w_ok, 1)
                    pe.matmul(ps[:, 7, 64:64 + NG + NE], ones[0:1, :], br[:], start=True, stop=True).then_inc(b2w_ps, 1)
                if j == 1 and t >= 1:
                    logits(t - 1)
            transpose_x1(NT - 1)
            logits(NT - 1)

            def slot_tables(done):
                for i in range(2 * NT):
                    pe.wait_ge(tb_in, done + i + 1)
                    mm = pe.matmul(ps[:, 7, 0:2 * NE], oh_view(i), tb_view(i), start=(i == 0), stop=(i == 2 * NT - 1))
                    mm.then_inc(tb_ps, 1)

            def keep_clock(n):
                for _ in range(n):
                    pe.matmul(ps[:, 5, 0:SEQ], ident[:], xs[:, 0, 0:CH], start=True, stop=True)

            keep_clock(6)
            pe.wait_ge(rk_in, 2)
            pe.matmul(ps[:, 5, 0:(NT + 1) * NE], strict[:], AA5, start=True, stop=False, skip_group_check=True)
            for back in range(1, NT + 1):
                mm = pe.matmul(ps[:, 5, back * NE:(NT + 1) * NE], ones[:], AA5[:, 0:(NT + 1 - back) * NE],
                               start=False, stop=(back == NT), skip_group_check=True)
            mm.then_inc(rk_ps, 1)

            def gather(e, hb):
                pe.wait_ge(hot_ok, e + 1)
                if not later(e):
                    pe.wait_ge(xn2_ok, NT)
                if later(e):
                    pe.wait_ge(xe_ok, e)
                for t in range(NT):
                    for h in range(2):
                        mm = pe.matmul(ps[64 * h:64 * h + 64, 0, :], hot[:, hb, t, :],
                                       xn[:, t, h * CH:(h + 1) * CH], start=(t == 0), stop=(t == NT - 1),
                                       skip_group_check=True)
                mm.then_inc(gx_ps, 1)

            def transpose_x(e):
                pe.wait_ge(xe_ok, e + 1)
                if later(e):
                    pe.wait_ge(xt_ok, e)
                for q in range(4):
                    mm = pe.transpose(ps[:, 1, q * P:(q + 1) * P], xe[:, q * P:(q + 1) * P], ident[:])
                mm.then_inc(xt_ps, 1)

            def gate_up(e, b, loads):
                pe.wait_ge(gu_in[b][0], loads * 32)
                pe.wait_ge(xt_ok, e + 1)
                if later(e):
                    pe.wait_ge(h_ok, e)
                for k in range(KC):
                    if k == KC // 2:
                        pe.wait_ge(gu_in[b][1], loads * 32)
                    for h in range(2):
                        mm = pe.matmul(ps[64 * h:64 * h + 64, 2, :], xeT[:, k % 4, k // 4, :],
                                       w_gu(b)[:, :, k, 256 * h:256 * h + 256], start=(k == 0),
                                       stop=(k == KC - 1), skip_group_check=True)
                mm.then_inc(gu_ps, 1)

            def transpose_h(e):
                pe.wait_ge(h_ok, e + 1)
                for q in range(2):
                    mm = pe.transpose(ps[:, 3, q * P:(q + 1) * P], hh[:, q * P:(q + 1) * P], ident[:])
                mm.then_inc(ht_ps, 1)

            def down(e, b, loads):
                pe.wait_ge(dn_in[b], loads * 16)
                pe.wait_ge(ht_ok, e + 1)
                if later(e):
                    pe.wait_ge(y_ok, e)
                for f in range(FE // P):
                    for h in range(2):
                        mm = pe.matmul(ps[64 * h:64 * h + 64, 4, :],
                                       hhT[:, f % 2, 64 * (f // 2):64 * (f // 2) + 64],
                                       w_dn(b)[:, f, h * CH:(h + 1) * CH], start=(f == 0),
                                       stop=(f == FE // P - 1), skip_group_check=True)
                mm.then_inc(dn_ps, 1)

            def expert(e, b, hb, loads, more=True):
                gate_up(e, b, loads)
                if not later(e):
                    slot_tables(0)
                if more:
                    gather(e + 1, 1 - hb)
                else:
                    keep_clock(3)
                transpose_h(e)
                if more:
                    transpose_x(e + 1)
                down(e, b, loads)

            gather(0, 0)
            transpose_x(0)
            expert(0, buffer_of(0), 0, 1)
            with pe.Fori(0, (NE - 2) // (2 * NBUF)) as i:
                for j in range(1, 2 * NBUF + 1):
                    expert(i * (2 * NBUF) + j, buffer_of(j), j % 2, i * 2 + (j // NBUF + 1))
            expert(NE - 1, buffer_of(NE - 1), 1, (NE - 1) // NBUF + 1, more=False)

            def pe_round(rnd):
                slot_tables(rnd * (2 * NT))
                with pe.Fori(0, NE) as e:
                    k = rnd * NE + e
                    gather(k, 0)
                    transpose_x(k)
                    gate_up(k, 0, rnd * NE + (e - (NE - 12)))
                    transpose_h(k)
                    down(k, 0, rnd * NE + (e - (NE - 12)))

            more_rounds(pe, pe_round)

        @block.scalar
        def _(act):
            n = [0]

            def link(ins):
                n[0] += 1
                ins.then_inc(act_seq, 1)
                act.wait_ge(act_seq, n[0])

            act.dma_start(c_in[:], c[0].rearrange("(p k) -> p k", k=KC)).then_inc(c_ld, 16)
            act.wait_ge(c_ld, 16)
            act.activation(st[:, 0:KC], c_in[:], ACT.Exp, scale=-1.0).then_inc(act_seq, 1)
            n[0] += 1
            for t in range(NT):
                act.wait_ge(x_in[t], 16)
                act.activation(xn[:, t, :], xs[:, t, :], ACT.Square, accum_out=st[:, 16 + t:17 + t]
                               ).then_inc(ss_ok, 1)

            def seed(v, y, ready, count, done):
                act.wait_ge(ready, count)
                link(act.activation(y, v, ACT.Ln))
                act.activation(y, y, ACT.Exp, scale=-0.5).then_inc(done, 1)

            seed(st[:, 20:24], st[:, 24:28], var_ok, 1, seed_ok)
            for i, g in enumerate((g_norm_mix, g_norm_ffn)):
                act.dma_start(gn_rows[8 * i:8 * i + 8, :], g[0].rearrange("(k p) -> k p", p=P)
                              ).then_inc(gains_in, 16)

            def load_bias(r):
                for j in range(4):
                    lo = 2048 * r + CH * j
                    act.dma_start(modr[32 * j:32 * j + 32, :],
                                  b_ada[0:1, lo:lo + CH].to_broadcast([32, CH])).then_inc(bias_in, 16)

            load_bias(0)
            for i, g in enumerate((q_norm_g, k_norm_g)):
                act.dma_start(gains[:, i, :], g[0:1, :].to_broadcast([P, HD])).then_inc(gains_in, 16)
            act.dma_start(wr[:, :, 0:NG], w_router_group[0].rearrange("(k p) n -> p k n", p=P)).then_inc(wr_in, 16)
            act.dma_start(wr[:, :, NG:], w_router_expert[0].rearrange("(k p) n -> p k n", p=P)).then_inc(wr_in, 16)
            act.dma_start(br[:, 0:NG], b_router_group).then_inc(wr_in, 16)
            act.dma_start(br[:, NG:], b_router_expert).then_inc(wr_in, 16)

            with nc.allow_non_contiguous_dma(reason="512 positions, by token tile"):
                act.dma_start(pos_i[:, 0:NT], positions[0].rearrange("(t p) -> p t", p=P)).then_inc(pos_in, 16)
            act.dma_start(pos_i[:, NT:2 * NT], positions[0].rearrange("(p r) -> p r", r=NT)).then_inc(pos_in, 16)

            def split_hi(j, half):
                if (j, half) == (0, 0):
                    act.wait_ge(w_first, 16)
                else:
                    act.wait_ge(w_ld[j] if j < 10 else w_ld[j - 4], 16 if j in (0, 6, 7, 8, 9) else 32)
                if half == 0:
                    if j < 3:
                        if j == 2:
                            act.wait_ge(ada_used, KC)
                    elif j < 8:
                        act.wait_ge(proj_done, NT * (j - 2))
                    else:
                        act.wait_ge(gate_ps, NT * (j - 7))
                act.activation(w_half(w_hi(j), j, half), w_half(w_raw(j), j, half), ACT.Copy).then_inc(whi_ok, 1)

            for cc in range(1, KC, 2):
                act.wait_ge(hT_ps, cc + 1)
                act.activation(hT[:, cc, :], ps[:, cc % 4, :], ACT.Copy).then_inc(hT_act, 1)
            split_hi(0, 0)
            act.wait_ge(xn_ok, NT)
            for cc in range(KC):
                if cc % 2 == 1:
                    act.wait_ge(cols_ok, 1)
                    act.activation(hT[:, cc, :], hT[:, cc, :], ACT.Identity, scale=cols[:, 0, cc:cc + 1],
                                   bias=cols[:, 1, cc:cc + 1]).then_inc(hT_act, 1)
                    act.wait_ge(hT_act, KC // 2 + cc // 2 + 1)
                else:
                    act.wait_ge(h_full, cc // 2 + 1)
                act.activation(h_hi[:, cc, :], hT[:, cc, :], ACT.Copy).then_inc(hi_ok, 1)
            split_hi(0, 1)
            act.wait_ge(trig_arg, 1)
            act.activation(cos16[:, :, 0:HALF], cos_arg, ACT.Sin).then_inc(trig_ok, 1)
            act.activation(sin16[:, :, HALF:ROPE_DIM], sin_arg, ACT.Sin).then_inc(trig_ok, 1)
            act.wait_ge(mod_cols, 1)
            load_bias(1)

            def store_qk(u):
                m, t, ch = u - QK_FIRST, u % NT, u // NT
                act.wait_ge(qk_tr, m + 1)
                src = ps[:, 4 + m % 2, :].rearrange("p (c n) -> p c n", c=4)
                if ch == C_QK0:
                    act.activation(QT[:, 0:2, t * P:(t + 1) * P], src[:, 0:2, :], ACT.Copy).then_inc(act_seq, 1)
                    n[0] += 1
                    act.wait_ge(act_seq, n[0])
                    act.activation(KT[:, 0:2, t * P:(t + 1) * P], src[:, 2:4, :], ACT.Copy).then_inc(qk_stored, 1)
                else:
                    dst = QT if ch == C_QRES else KT
                    act.activation(dst[:, 2:6, t * P:(t + 1) * P], src, ACT.Copy).then_inc(qk_stored, 1)

            for u in range(NU):
                ch, t = divmod(u, NT)
                act.wait_ge(proj_done, u + 1)
                bank = ps[:, u % 3, :]
                if ch == C_SB:
                    act.activation(SBT[:, t, :], bank, ACT.Copy, scale=HD ** -0.5 if t < 2 else 1.0
                                   ).then_inc(proj_act, 1)
                elif ch == C_VNAT:
                    act.activation(VN[:, t, :], bank, ACT.Copy).then_inc(proj_act, 1)
                elif ch == C_VRES:
                    act.activation(VR[:, t, :], bank, ACT.Copy).then_inc(proj_act, 1)
                else:
                    m = u - QK_FIRST
                    if m >= 2:
                        act.wait_ge(rope_ok, m - 1)
                    act.activation(sq[:, m % 2, :], bank, ACT.Square).then_inc(proj_act, 1)
                    seed(st[:, 32:40], st[:, 40:48], var_ok, 1 + m + 1, seed_ok)
                if u == KC + 1:
                    act.wait_ge(mod_cols, 2)
                    act.wait_ge(gates_kept, 1)
                    load_bias(2)
                if t in (1, 2):
                    split_hi(ch + 1, t - 1)
                if QK_FIRST <= u - 1 <= QK_LAST:
                    store_qk(u - 1)

            def gate_exp_(f):
                act.wait_ge(gate_ps, f + 1)
                act.activation(gT[:, f, :], ps[:, gate_bank(f), :], ACT.Exp, scale=-1.0).then_inc(gate_exp, 1)

            def softmax_exp(s):
                act.wait_ge(sc_max, s + 1)
                k0 = key_from(s)
                for h in range(NH):
                    ins = act.activation(sm[:, s % 2, h, k0:], sm[:, s % 2, h, k0:], ACT.Exp,
                                         bias=stat(s)[:, 8 + h:9 + h], accum_out=stat(s)[:, h:h + 1])
                    if h < NH - 1:
                        link(ins)
                ins.then_inc(sc_exp, 1)

            def probs_store(s):
                act.wait_ge(pT_ps, s + 1)
                if s >= 2:
                    act.wait_ge(u_ps, s - 1)
                b, k0 = s_bank(s), key_from(s)
                src = ps[:, b, :].rearrange("p (h n) -> p h n", h=2)[:, :, k0:]
                dst = pT[:, s % 2, 0:CH].rearrange("p (h n) -> p h n", h=2)[:, :, k0:]
                act.activation(dst, src, ACT.Copy).then_inc(pT_act, 1)

            def mix_exp(i):
                act.wait_ge(mx_ok, i + 1)
                act.activation(cstat(i)[:, 0:8], cstat(i)[:, 0:8], ACT.Exp).then_inc(mx_exp, 1)

            for s in range(2 * NT):
                softmax_exp(s)
                gate_exp_(s)
                probs_store(s)
                if s % NT in (1, 2):
                    split_hi(7 + s // NT, s % NT - 1)
                if s >= NT + 1:
                    mix_exp(s - NT - 1)
            gate_exp_(8)
            mix_exp(NT - 1)

            def sb_logs(h):
                act.wait_ge(z_ps, h + 1)
                a = lg1[:, 0:SB_COLS]
                b = 3 * (h % 2) * CH
                if h == 0:
                    act.wait_ge(u_ps, 2 * NT)
                act.activation(a, psf[:, b:b + SB_COLS], ACT.Abs).then_inc(z_abs, 1)
                act.wait_ge(z_abs, h + 1)
                link(act.activation(a, a, ACT.Exp, scale=-1.0))
                act.activation(a, a, ACT.Ln, bias=1.0).then_inc(lnz, 1)

            def sb_exp(h):
                act.wait_ge(arg_ok, h + 1)
                act.activation(zs[:, 0:SB_COLS], zs[:, 0:SB_COLS], ACT.Exp).then_inc(a_ok, 1)

            def sb_store(h):
                o = HD * (h % 2)
                act.wait_ge(osb_ps, h + 1)
                act.activation(OT_SB[o:o + HD, h // 2, :], ps[o:o + HD, 3 * (h % 2), :], ACT.Copy
                               ).then_inc(osb_ok, 1)

            sb_logs(0)
            gate_exp_(9)
            for h in range(NH):
                if h == 0:
                    split_hi(9, 0)
                    split_hi(9, 1)
                sb_exp(h)
                if h + 1 < NH:
                    sb_logs(h + 1)
                    gate_exp_(10 + 2 * h)
                if h in (1, 2):
                    split_hi(10, h - 1)
                sb_store(h)
                if h + 1 < NH:
                    gate_exp_(11 + 2 * h)
            split_hi(11, 0)
            split_hi(11, 1)
            for f in range(KC):
                act.wait_ge(m_full, f + 1)
                act.activation(m_hi[:, f, :], hT[:, f, :], ACT.Copy).then_inc(mhi_ok, 1)

            act.wait_ge(g1_ps, 1)
            for j in range(2):
                act.activation(gate1b[:, j * CH:(j + 1) * CH], ps[:, 6 + j, :], ACT.Copy).then_inc(g1_ok, 1)
            act.wait_ge(g2_ps, 1)
            act.activation(gate2h, ps[:, 6, :], ACT.Copy).then_inc(g2_ok, 1)
            def keep_x1t(t):
                act.wait_ge(x1t_ps, t + 1)
                if t >= 2:
                    act.wait_ge(lg_ps, t - 1)
                act.activation(x1t[:, t % 2, 4:KC, :], ps[:, 2 * (t % 2) + 1, :].rearrange("p (k n) -> p k n", k=4),
                               ACT.Copy).then_inc(x1t_act, 1)

            for t in range(NT):
                act.wait_ge(x1_ok, NT + t + 1)
                act.activation(xn[:, t, :], xs[:, t, :], ACT.Square, accum_out=st[:, 16 + t:17 + t]
                               ).then_inc(ss2_ok, 1)
                keep_x1t(t)
            seed(st[:, 20:24], st[:, 24:28], var2_ok, 1, seed2_ok)
            act.wait_ge(rstd_ok, 1)
            for t in range(NT):
                act.activation(xn[:, t, :], xs[:, t, :], ACT.Copy, scale=st[:, 24 + t:25 + t]).then_inc(xn2_ok, 1)
            act.wait_ge(r_arg, 1)
            act.activation(rs[:, 0:16], rs[:, 0:16], ACT.Exp).then_inc(r_exp, 1)
            act.wait_ge(r_arg, 2)
            act.activation(rs[:, 40:44], rs[:, 40:44], ACT.Exp).then_inc(r_exp, 1)

            def store_x(e):
                act.wait_ge(gx_ps, e + 1)
                if later(e):
                    act.wait_ge(xt_ps, e)
                act.activation(xe, ps[:, 0, :], ACT.Copy).then_inc(xe_ok, 1)

            def sig(e):
                act.wait_ge(gu_ps, e + 1)
                act.activation(tsig, ps[:, 2, 0:256], ACT.Exp, scale=-1.0).then_inc(sig_exp, 1)

            def expert(e, more=True):
                sig(e)
                if more:
                    store_x(e + 1)

            store_x(0)
            expert(0)
            with act.Fori(1, NE - 1) as e:
                expert(e)
            sig(NE - 1)

            def act_round(rnd):
                with act.Fori(0, NE) as e:
                    store_x(rnd * NE + e)
                    sig(rnd * NE + e)

            more_rounds(act, act_round)

        @block.vector
        def _(dve):
            n = [0]

            def link(ins):
                n[0] += 1
                ins.then_inc(dve_seq, 1)
                dve.wait_ge(dve_seq, n[0])

            dve.wait_ge(act_seq, 1)
            link(dve.tensor_scalar(st[:, 0:8], st[:, 0:8], 1.0, None, ALU.add))
            link(dve.reciprocal(st[:, 0:8], st[:, 0:8]))
            link(dve.tensor_tensor(st[:, 0:8], st[:, 0:8], c_in[:], ALU.mult))
            dve.tensor_copy(crep[:], st[:, 0:8].unsqueeze(2).to_broadcast([P, KC, 32])).then_inc(crep_ok, 1)
            def refine(v, y, tmp, done=None):
                link(dve.tensor_tensor(tmp, y, y, ALU.mult))
                link(dve.scalar_tensor_tensor(out=tmp, in0=tmp, scalar=-0.5, in1=v, op0=ALU.mult, op1=ALU.mult))
                step = dve.scalar_tensor_tensor(out=y, in0=tmp, scalar=1.5, in1=y, op0=ALU.add, op1=ALU.mult)
                if done is None:
                    link(step)
                else:
                    step.then_inc(done, 1)
                    dve.wait_ge(done, 1)

            dve.wait_ge(ss_ok, NT)
            dve.tensor_scalar(st[:, 20:24], st[:, 16:20], 1.0 / D, RMS_EPS, ALU.mult, ALU.add).then_inc(var_ok, 1)
            dve.wait_ge(seed_ok, 1)
            refine(st[:, 20:24], st[:, 24:28], st[:, 28:32])
            for t in range(NT):
                dve.tensor_scalar(xn[:, t, :], xs[:, t, :], st[:, 24 + t:25 + t], None, ALU.mult).then_inc(xn_ok, 1)

            def mod_round(r):
                dve.wait_ge(ada_used, KC * (r + 1))
                dve.wait_ge(bias_in, 64 * (r + 1))
                dve.tensor_tensor(modr[:], modr[:], ps[:, 7, :], ALU.add).then_inc(mod_rows, 1)
                dve.wait_ge(mod_rows, r + 1)
                if r == 1:
                    dve.tensor_copy(grow[0:64, :], modr[0:64, :]).then_inc(gates_kept, 1)
                if r == 2:
                    dve.tensor_copy(grow[64:128, :], modr[64:128, :]).then_inc(gates_kept, 1)

            def split_lo(j, half):
                dve.wait_ge(whi_ok, 2 * j + half + 1)
                dve.tensor_tensor(w_half(w_lo(j), j, half), w_half(w_raw(j), j, half),
                                  w_half(w_hi(j), j, half).bitcast(F32), ALU.subtract).then_inc(wlo_ok, 1)

            for cc in range(0, KC, 2):
                dve.wait_ge(hT_ps, cc + 1)
                dve.tensor_copy(hT[:, cc, :], ps[:, cc % 4, :]).then_inc(hT_dve, 1)
            split_lo(0, 0)
            mod_round(0)
            dve.wait_ge(gn_T, 1)
            link(dve.tensor_copy(gn[:], ps[:, 5, 0:16].rearrange("p (g k) -> p g k", g=2)))
            dve.wait_ge(gains_in, 64)
            link(dve.tensor_scalar(gains[:, 0, :], gains[:, 0, :], HD ** -0.5, None, ALU.mult))

            dve.wait_ge(mod_cols, 1)
            by_chunk = ps[:, 6, :].rearrange("p (q j m) -> p j q m", q=4, j=4)[:, :, :, 0]

            def two(v):
                return v.rearrange("p (j q) -> p j q", j=2)

            link(dve.tensor_copy(two(cols[:, 1, :]), by_chunk[:, 0:2, :]))
            dve.scalar_tensor_tensor(out=two(cols[:, 0, :]), in0=by_chunk[:, 2:4, :], scalar=1.0, in1=two(gn[:, 0, :]),
                                     op0=ALU.add, op1=ALU.mult).then_inc(cols_ok, 1)
            dve.wait_ge(cols_ok, 1)

            def h_low(cc):
                dve.wait_ge(hi_ok, cc + 1)
                dve.tensor_tensor(h_lo[:, cc, :], hT[:, cc, :], h_hi[:, cc, :].bitcast(F32), ALU.subtract
                                  ).then_inc(lo_ok, 1)

            dve.wait_ge(hT_dve, KC // 2)
            dve.wait_ge(hT_act, KC // 2)
            for cc in range(KC):
                if cc % 2 == 0:
                    dve.tensor_scalar(hT[:, cc, :], hT[:, cc, :], cols[:, 0, cc:cc + 1], cols[:, 1, cc:cc + 1],
                                      ALU.mult, ALU.add).then_inc(h_full, 1)
                if cc >= 1:
                    h_low(cc - 1)
            h_low(KC - 1)
            split_lo(0, 1)

            dve.wait_ge(consts, 4)
            dve.wait_ge(pool_seq, 8)
            link(dve.tensor_scalar(diff_i, diff_i, 3, None, ALU.bitwise_and))
            link(dve.tensor_scalar(diff_m, diff_i, 0.0, NEG, ALU.not_equal, ALU.mult))
            link(dve.tensor_tensor(mask12[:, 1, :], mask12[:, 1, :], diff_m, ALU.add))

            dve.wait_ge(pos_in, 32)
            A, K, C = sin_arg, trig_k, cos_arg
            link(dve.tensor_copy(grow[:, 192:200], pos_i[:]))
            for f in range(HALF):
                dve.memset(grow[:, 200 + f:201 + f], float(inv_freq[f])).then_inc(dve_seq, 1)
                n[0] += 1
            dve.wait_ge(dve_seq, n[0])
            link(dve.tensor_tensor(A, grow[:, 192:200].unsqueeze(2).to_broadcast([P, 2 * NT, HALF]),
                                   grow[:, 200:208].unsqueeze(1).to_broadcast([P, 2 * NT, HALF]), ALU.mult))
            magic = 1.5 * 2.0 ** 23
            link(dve.tensor_scalar(K, A, float(1 / (2 * np.pi)), magic, ALU.mult, ALU.add))
            link(dve.tensor_scalar(K, K, magic, None, ALU.subtract))
            for part in two_pi_parts():
                link(dve.scalar_tensor_tensor(out=A, in0=K, scalar=-part, in1=A, op0=ALU.mult, op1=ALU.add))
            link(dve.tensor_scalar(C, A, float(np.pi / 2), None, ALU.add))
            link(dve.tensor_scalar(K, C, float(np.pi), -2 * float(np.pi), ALU.is_gt, ALU.mult))
            link(dve.tensor_tensor(C, C, K, ALU.add))
            pi_in = float(np.nextafter(np.float32(np.pi), np.float32(0)))
            link(dve.tensor_scalar(C, C, pi_in, -pi_in, ALU.min, ALU.max))
            dve.tensor_scalar(A, A, pi_in, -pi_in, ALU.min, ALU.max).then_inc(trig_arg, 1)
            for u in range(NU):
                ch, t = divmod(u, NT)
                if u == 1:
                    dve.wait_ge(trig_ok, 2)
                    link(dve.tensor_copy(cos16[:, :, HALF:], cos16[:, :, 0:HALF]))
                    dve.tensor_scalar(sin16[:, :, 0:HALF], sin16[:, :, HALF:], -1.0, None, ALU.mult).then_inc(trig_ok, 1)

                if QK_FIRST <= u <= QK_LAST:
                    m = u - QK_FIRST
                    dve.wait_ge(proj_act, u + 1)
                    if m >= 2:
                        dve.wait_ge(qk_tr, m - 1)
                    if m == 0:
                        dve.wait_ge(hT_ps, KC)
                    src = ps[:, u % 3, :].rearrange("p (g h d) -> p g h d", g=2, h=4)
                    if ch == C_QK0:
                        g = gains[:].unsqueeze(2).to_broadcast([P, 2, 4, HD])
                    else:
                        g = gains[:, ch - C_QRES, :].unsqueeze(1).unsqueeze(1).to_broadcast([P, 2, 4, HD])
                    xgu = xg[:, m % 2, :]
                    dve.tensor_tensor(xgu.rearrange("p (g h d) -> p g h d", g=2, h=4), src, g, ALU.mult
                                      ).then_inc(gain_ok, 1)
                    link(dve.tensor_reduce(st[:, 48:56], sq[:, m % 2, :].rearrange("p (h d) -> p h d", h=8),
                                           AX_X, ALU.add))
                    dve.tensor_scalar(st[:, 32:40], st[:, 48:56], 1.0 / HD, RMS_EPS, ALU.mult, ALU.add
                                      ).then_inc(var_ok, 1)
                    dve.wait_ge(seed_ok, 1 + m + 1)
                    refine(st[:, 32:40], st[:, 40:48], st[:, 48:56])
                    dve.wait_ge(rope_ok, m + 1)
                    xh = xgu.rearrange("p (h d) -> p h d", h=8)
                    dve.tensor_tensor(xh, xh, st[:, 40:48].unsqueeze(2).to_broadcast([P, 8, HD]), ALU.mult
                                      ).then_inc(qk_ready, 1)
                if t in (1, 2):
                    split_lo(ch + 1, t - 1)
                if u == KC - 1:
                    mod_round(1)
                if u == KC + 1:
                    dve.wait_ge(mod_cols, 2)
                    dve.tensor_copy(two(cols[:, 3, :]), by_chunk[:, 2:4, :]).then_inc(cols_ok, 1)
                if u == 2 * KC - 1:
                    mod_round(2)
                if u == 2 * KC + 1:
                    dve.wait_ge(mod_cols, 3)
                    dve.scalar_tensor_tensor(out=two(cols[:, 2, :]), in0=by_chunk[:, 0:2, :], scalar=1.0,
                                             in1=two(gn[:, 1, :]), op0=ALU.add, op1=ALU.mult).then_inc(cols_ok, 1)

            def softmax_max(s):
                dve.wait_ge(sc_ps, s + 1)
                if s == 0:
                    dve.wait_ge(qk_tr, QK_LAST - QK_FIRST + 1)
                    dve.wait_ge(ada_used, 3 * KC)
                if s >= 2:
                    dve.wait_ge(pT_ps, s - 1)
                k0 = key_from(s)
                m = mask12 if s < NT else mask0.rearrange("p (g n) -> p g n", g=2)
                m = m[:, k0 // P:2, :].unsqueeze(1).to_broadcast([P, NH, 2 - k0 // P, P])
                S = scores_view(s)[:, :, k0:].rearrange("p h (g n) -> p h g n", n=P)
                d = sm[:, s % 2, :, k0:]
                link(dve.tensor_tensor(d.rearrange("p h (g n) -> p h g n", n=P), S, m, ALU.add))
                link(dve.tensor_reduce(stat(s)[:, 4:8], d, AX_X, ALU.max))
                dve.tensor_scalar(stat(s)[:, 8:12], stat(s)[:, 4:8], -1.0, None, ALU.mult).then_inc(sc_max, 1)

            def probs_store(s):
                dve.wait_ge(pT_ps, s + 1)
                if s >= 2:
                    dve.wait_ge(u_ps, s - 1)
                b, k0 = s_bank(s), key_from(s)
                src = ps[:, b + 1, :].rearrange("p (h n) -> p h n", h=2)[:, :, k0:]
                dst = pT[:, s % 2, CH:2 * CH].rearrange("p (h n) -> p h n", h=2)[:, :, k0:]
                dve.tensor_copy(dst, src).then_inc(pT_dve, 1)

            def keep_u(s):
                dve.wait_ge(u_ps, s + 1)
                if s >= 2:
                    dve.wait_ge(u_out[s % 2], 16)
                dve.tensor_copy(ustage[:, s % 2, 0:GW], ps[:, 4 + s % 2, 0:GW]).then_inc(u_kept, 1)
                dve.tensor_copy(ustage[:, s % 2, GW:GW + 8], stat(s)[:, 0:8]).then_inc(stats_kept, 1)

            def mix_args(i):
                s = NT + i
                dve.wait_ge(sc_exp, s + 1)
                dve.wait_ge(u_back[i % 2], 16 * (i // 2 + 1))
                m12, m0 = ustage[:, i % 2, GW + 4:GW + 8], stat(s)[:, 4:8]
                cs = cstat(i)
                link(dve.tensor_tensor(cs[:, 8:12], m0, m12, ALU.max))
                link(dve.tensor_tensor(cs[:, 0:4], m0, cs[:, 8:12], ALU.subtract))
                dve.tensor_tensor(cs[:, 4:8], m12, cs[:, 8:12], ALU.subtract).then_inc(mx_ok, 1)

            def mix(i):
                s, cs = NT + i, cstat(i)
                dve.wait_ge(mx_exp, i + 1)
                link(dve.tensor_tensor(cs[:, 8:12], cs[:, 0:4], stat(s)[:, 0:4], ALU.mult))
                link(dve.tensor_tensor(cs[:, 12:16], cs[:, 4:8], ustage[:, i % 2, GW:GW + 4], ALU.mult))
                link(dve.tensor_tensor(cs[:, 8:12], cs[:, 8:12], cs[:, 12:16], ALU.add))
                link(dve.reciprocal(cs[:, 8:12], cs[:, 8:12]))
                link(dve.tensor_tensor(cs[:, 0:4], cs[:, 0:4], cs[:, 8:12], ALU.mult))
                link(dve.tensor_tensor(cs[:, 4:8], cs[:, 4:8], cs[:, 8:12], ALU.mult))
                dve.wait_ge(u_ps, s + 1)
                if i > 0:
                    dve.wait_ge(oT_ps, i)
                od = o_dil.rearrange("p (b a d) -> p a b d", a=2, b=2)
                u12 = ustage[:, i % 2, 0:GW].rearrange("p (a b d) -> p a b d", a=2, b=2)

                def by_head(v):
                    return v.rearrange("p (a b) -> p a b", a=2).unsqueeze(3).to_broadcast([P, 2, 2, HD])

                link(dve.tensor_tensor(u12, u12, by_head(cs[:, 4:8]), ALU.mult))
                dve.tensor_tensor(od, ps[:, 4 + s % 2, 0:GW].rearrange("p (a b d) -> p a b d", a=2, b=2),
                                  by_head(cs[:, 0:4]), ALU.mult).then_inc(u_kept, 1)
                dve.wait_ge(u_kept, s + 1)
                dve.tensor_tensor(od, od, u12, ALU.add).then_inc(o_ok, 1)

            def out_T(i):
                dve.wait_ge(oT_ps, i + 1)
                dve.tensor_copy(OT_DIL[:, :, i * P:(i + 1) * P],
                                ps[:, 4 + i % 2, 256:512].rearrange("p (c n) -> p c n", c=2)).then_inc(oT_ok, 1)

            def gate_finish(f):
                dve.wait_ge(gate_exp, f + 1)
                link(dve.tensor_scalar(gT[:, f, :], gT[:, f, :], 1.0, None, ALU.add))
                dve.reciprocal(gT[:, f, :], gT[:, f, :]).then_inc(gate_ok, 1)

            softmax_max(0)
            for s in range(2 * NT):
                gate_finish(s)
                probs_store(s)
                if s + 1 < 2 * NT:
                    softmax_max(s + 1)
                if 1 <= s <= NT:
                    keep_u(s - 1)
                if s >= NT + 1:
                    mix_args(s - NT - 1)
                    mix(s - NT - 1)
                if s - 2 >= NT:
                    out_T(s - 2 - NT)
            gate_finish(8)
            mix_args(NT - 1)
            mix(NT - 1)
            out_T(2)

            def sb_copy(h):
                dve.wait_ge(z_ps, h + 1)
                dve.wait_ge(z_abs, h + 1)
                if h == 0:
                    dve.wait_ge(u_ps, 2 * NT)
                else:
                    dve.wait_ge(osb_ps, h)
                b = 3 * (h % 2) * CH
                dve.tensor_copy(zs[:, 0:SB_COLS], psf[:, b:b + SB_COLS]).then_inc(z_cp, 1)

            def diag(v):
                return v[:, 0:1536].rearrange("p (a n) -> p a n", a=3)[:, :, 0:P], v[:, SB_OFF[3]:SB_OFF[3] + P]

            def sb_softplus(h):
                dve.wait_ge(lnz, h + 1)
                dve.wait_ge(z_cp, h + 1)
                if h > 0:
                    dve.wait_ge(sf_ps, h)
                link(dve.scalar_tensor_tensor(out=sp_[:, 0:SB_COLS], in0=zs[:, 0:SB_COLS], scalar=0.0,
                                              in1=lg1[:, 0:SB_COLS], op0=ALU.max, op1=ALU.add))
                a, b = diag(sp_)
                link(dve.tensor_tensor(a, a, strict[:].unsqueeze(1).to_broadcast([P, 3, P]), ALU.mult))
                dve.tensor_tensor(b, b, strict[:], ALU.mult).then_inc(sp_ok, 1)

            def sb_args(h):
                dve.wait_ge(sf_ps, h + 1)
                b = 3 * (h % 2) * CH
                link(dve.tensor_tensor(zs[:, 0:SB_COLS], zs[:, 0:SB_COLS], psf[:, b:b + SB_COLS], ALU.subtract))
                a, b = diag(zs)
                link(dve.tensor_tensor(a, a, negstrict.unsqueeze(1).to_broadcast([P, 3, P]), ALU.add))
                dve.tensor_tensor(b, b, negstrict, ALU.add).then_inc(arg_ok, 1)

            def dil_gate(f):
                dve.wait_ge(dil_ps, f + 1)
                dve.wait_ge(gate_ok, KC)
                dve.tensor_tensor(gT[:, f, :], gT[:, f, :], ps[:, dil_bank(f), :], ALU.mult).then_inc(dil_ok, 1)

            sb_copy(0)
            sb_softplus(0)
            gate_finish(9)
            out_T(3)
            for h in range(NH):
                sb_args(h)
                if h < NH - 1:
                    dil_gate(2 * h)
                if h + 1 < NH:
                    gate_finish(10 + 2 * h)
                    sb_copy(h + 1)
                    sb_softplus(h + 1)
                    gate_finish(11 + 2 * h)
                    dil_gate(2 * h + 1)
            dil_gate(6)
            dil_gate(7)

            dve.wait_ge(gate_ok, 2 * KC)
            for f in range(KC):
                dve.wait_ge(br_ps, f + 1)
                dve.tensor_tensor(gT[:, KC + f, :], gT[:, KC + f, :], ps[:, f % 4, :], ALU.mult).then_inc(merged, 1)
                dve.wait_ge(merged, f + 1)
                dve.wait_ge(dil_ok, KC)
                dve.tensor_tensor(hT[:, f, :], gT[:, f, :], gT[:, KC + f, :], ALU.add).then_inc(m_full, 1)

            def keep_x1t(t):
                dve.wait_ge(x1t_ps, t + 1)
                if t >= 2:
                    dve.wait_ge(lg_ps, t - 1)
                dve.tensor_copy(x1t[:, t % 2, 0:4, :], ps[:, 2 * (t % 2), :].rearrange("p (k n) -> p k n", k=4)
                                ).then_inc(x1t_dve, 1)

            dve.wait_ge(b2w_ps, 1)
            dve.tensor_tensor(br[:], br[:], ps[0:1, 7, 0:NG + NE], ALU.add).then_inc(b2w_ok, 1)
            dve.tensor_tensor(wr[:], wr[:], cols[:, 2, :].unsqueeze(2).to_broadcast([P, KC, NG + NE]), ALU.mult
                              ).then_inc(b2w_ok, 1)

            dve.wait_ge(g1_ok, 2)
            dve.wait_ge(slot_consts, 3)
            for u in range(2 * NT):
                j, t = divmod(u, NT)
                if j == 1 and t >= 1:
                    keep_x1t(t - 1)
                dve.wait_ge(o_ps, u + 1)
                out_ps = ps[:, 4 + u % 2, :]
                link(dve.tensor_tensor(out_ps, out_ps, gate1b[:, j * CH:(j + 1) * CH], ALU.mult))
                if j == 0:
                    dve.wait_ge(x_in[t], 32)
                xt = xs[:, t, j * CH:(j + 1) * CH]
                dve.tensor_tensor(xt, xt, out_ps, ALU.add).then_inc(x1_ok, 1)
                if u == 0:
                    dve.wait_ge(b2w_ps, 2)
                    dve.tensor_copy(lgc, ps[:, 7, 64:64 + NG + NE]).then_inc(b2w_ok, 1)
            keep_x1t(NT - 1)
            dve.wait_ge(ss2_ok, NT)
            dve.tensor_scalar(st[:, 20:24], st[:, 16:20], 1.0 / D, RMS_EPS, ALU.mult, ALU.add).then_inc(var2_ok, 1)
            dve.wait_ge(seed2_ok, 1)
            refine(st[:, 20:24], st[:, 24:28], st[:, 28:32], rstd_ok)

            def one_hot(e, hb, gathers=None):
                if gathers is None:
                    gathers = e - 1
                if later(e) and later(gathers):
                    dve.wait_ge(gx_ps, gathers)
                dve.tensor_tensor(hot[:, hb], iot[:, 0:1, :].to_broadcast([P, NT, CAP]),
                                  RE[:, :, bass.ds(e, 1)].to_broadcast([P, NT, CAP]), ALU.is_equal
                                  ).then_inc(hot_ok, 1)

            G, E = lg[:, :, 0:NG], lg[:, :, NG:].rearrange("p t (g e) -> p t g e", g=NG)
            row = lambda i: rs[:, 44 + 4 * i:48 + 4 * i]
            gmax, best, v1, v2, pg, w1, w2, tmp4 = (row(i) for i in range(8))
            gex = rs[:, 0:16].rearrange("p (t g) -> p t g", t=NT)
            goh = rs[:, 76:92].rearrange("p (t g) -> p t g", t=NT)
            lsel = rs[:, 92:124].rearrange("p (t e) -> p t e", t=NT)
            o1 = rs[:, 124:156].rearrange("p (t e) -> p t e", t=NT)
            o2 = rs[:, 156:188].rearrange("p (t e) -> p t e", t=NT)
            num, from_last = iot[:, 0, 0:EPG], rs[:, 16:16 + EPG]
            link(dve.tensor_scalar(from_last, num, -float(EPG + 1), None, ALU.add))
            dve.memset(RK[:, 0, :], 0.0).then_inc(rk_in, 1)
            lg_all = ps[:, 6:8, 0:P].rearrange("p b (c n) -> p c b n", c=2)[:, :, :, 0:NG + NE]
            lg4 = lg.rearrange("p (c b) n -> p c b n", c=2)
            full = [P, 2, 2, NG + NE]
            dve.wait_ge(lg_ps, NT)
            link(dve.tensor_tensor(lg4, lg_all, st[:, 24:28].rearrange("p (c b) -> p c b", c=2).unsqueeze(3
                                   ).to_broadcast(full), ALU.mult))
            link(dve.tensor_tensor(lg4, lg4, lgc.unsqueeze(1).unsqueeze(1).to_broadcast(full), ALU.add))

            def first_max(onehot, vals, top, width):
                full = [P, NT, width]
                link(dve.tensor_reduce(top, vals, AX_X, ALU.max))
                link(dve.tensor_tensor(onehot, vals, top.unsqueeze(2).to_broadcast(full), ALU.is_equal))
                back = rt[:, 0:NT * width].rearrange("p (t e) -> p t e", t=NT)
                link(dve.tensor_tensor(back, onehot, from_last[:, 0:width].unsqueeze(1).to_broadcast(full), ALU.mult))
                link(dve.tensor_reduce(best, back, AX_X, ALU.min))
                link(dve.tensor_tensor(onehot, back, best.unsqueeze(2).to_broadcast(full), ALU.is_equal))

            first_max(goh, G, gmax, NG)
            pick = rt.rearrange("p (t g e) -> p t g e", t=NT, g=NG)
            link(dve.tensor_tensor(pick, E, goh.unsqueeze(3).to_broadcast([P, NT, NG, EPG]), ALU.mult))
            link(dve.tensor_reduce(lsel, pick.rearrange("p t g e -> p t e g"), AX_X, ALU.add))
            first_max(o1, lsel, v1, EPG)
            link(dve.scalar_tensor_tensor(out=lsel, in0=o1, scalar=NEG, in1=lsel, op0=ALU.mult, op1=ALU.add))
            first_max(o2, lsel, v2, EPG)
            full = [P, NT, NG, EPG]
            link(dve.tensor_tensor(lsel, o1, o2, ALU.add))
            dve.tensor_tensor(AA.rearrange("p t (g e) -> p t g e", g=NG), goh.unsqueeze(3).to_broadcast(full),
                              lsel.unsqueeze(2).to_broadcast(full), ALU.mult).then_inc(rk_in, 1)
            dve.tensor_tensor(gex, G, gmax.unsqueeze(2).to_broadcast([P, NT, NG]), ALU.subtract).then_inc(r_arg, 1)
            dve.tensor_tensor(rs[:, 40:44], v2, v1, ALU.subtract).then_inc(r_arg, 1)
            for a, o in ((A1, o1), (A2, o2)):
                link(dve.tensor_tensor(a.rearrange("p t (g e) -> p t g e", g=NG),
                                       goh.unsqueeze(3).to_broadcast(full), o.unsqueeze(2).to_broadcast(full), ALU.mult))
            dve.wait_ge(rk_in, 2)
            dve.wait_ge(rk_ps, 1)
            link(dve.scalar_tensor_tensor(out=RE, in0=ps[:, 5, 0:NT * NE].rearrange("p (t e) -> p t e", t=NT), scalar=1.0,
                                          in1=AA, op0=ALU.add, op1=ALU.mult))
            one_hot(0, 0)
            dve.wait_ge(r_exp, 2)
            link(dve.tensor_reduce(pg, gex, AX_X, ALU.add))
            link(dve.tensor_scalar(w1, rs[:, 40:44], 1.0, None, ALU.add))
            link(dve.tensor_tensor(w1, w1, pg, ALU.mult))
            link(dve.reciprocal(w1, w1))
            link(dve.tensor_tensor(w2, w1, rs[:, 40:44], ALU.mult))
            link(dve.tensor_reduce(tmp4[:, 0:1], ps[:, 5, 4 * NE:5 * NE], AX_X, ALU.max))
            link(dve.tensor_scalar(cnt_i[:], tmp4[:, 0:1], -1.0, None, ALU.add))
            rk4 = rs[:, 188:196].rearrange("p (j t) -> p j t", j=2)
            rt3 = rt.rearrange("p (t e) -> p t e", t=NT)
            for j, a in enumerate((A1, A2)):
                link(dve.tensor_tensor(rt3, a, RE, ALU.mult))
                link(dve.tensor_reduce(rk4[:, j, :], rt3, AX_X, ALU.add))
            code = rs[:, 196:204].rearrange("p (j t) -> p j t", j=2)
            for j in range(2):
                link(dve.tensor_scalar(code[:, j, :], tokc[:], float(j), None, ALU.add))

            def slot_tables(done, step):
                if later(done):
                    dve.wait_ge(tb_ps, done)
                for i in range(2 * NT):
                    j, t = divmod(i, NT)
                    step(dve.tensor_scalar(oh_view(i), iot[:].rearrange("p a s -> p (a s)"), rk4[:, j, t:t + 1],
                                           None, ALU.is_equal))
                    a, w = (A1, w1) if j == 0 else (A2, w2)
                    step(dve.tensor_scalar(tb_view(i)[:, 0:NE], a[:, t, :], code[:, j, t:t + 1], None, ALU.mult))
                    dve.tensor_scalar(tb_view(i)[:, NE:2 * NE], a[:, t, :], w[:, t:t + 1], None, ALU.mult
                                      ).then_inc(tb_in, 1)
                dve.wait_ge(tb_ps, done + 2 * NT)
                step(dve.tensor_copy(slotW, ps[:, 7, NE:2 * NE]))
                dve.tensor_scalar(slotI, ps[:, 7, 0:NE], 2.0, halfc[:, 0:1], ALU.mult, ALU.add
                                  ).then_inc(tables_ok, 1)


            def store_xT(e):
                dve.wait_ge(xt_ps, e + 1)
                full = [P, 4, 2, CAP]
                a2 = cols[:, 2, :].rearrange("p (h q) -> p q h", h=2).unsqueeze(3).to_broadcast(full)
                b2 = cols[:, 3, :].rearrange("p (h q) -> p q h", h=2).unsqueeze(3).to_broadcast(full)
                xm = xmul.rearrange("p (q h s) -> p q h s", q=4, h=2)
                dve.tensor_tensor(xm, ps[:, 1, :].rearrange("p (q h s) -> p q h s", q=4, h=2), a2, ALU.mult
                                  ).then_inc(moe_dve, 1)
                return xm, b2

            NSTEP = 5

            def store_xT2(e, xm, b2, step):
                dve.wait_ge(moe_dve, step)
                if later(e):
                    dve.wait_ge(gu_ps, e)
                dve.tensor_tensor(xeT, xm, b2, ALU.add).then_inc(xt_ok, 1)

            def expert(e, hb, stores, more=True, col=None):
                s0 = e * NSTEP + 1
                if more and later(e):
                    one_hot(e + 1, 1 - hb)
                if later(e):
                    dve.wait_ge(y_ok, e)
                col = e if col is None else col
                dve.tensor_copy(wcol[:], slotW[:, bass.ds(col, 1)]).then_inc(moe_dve, 1)
                dve.wait_ge(sig_exp, e + 1)
                dve.tensor_scalar(tden, tsig, 1.0, None, ALU.add).then_inc(moe_dve, 1)
                dve.wait_ge(moe_dve, s0 + 2)
                dve.reciprocal(tden, tden).then_inc(moe_dve, 1)
                dve.wait_ge(moe_dve, s0 + 3)
                dve.tensor_tensor(tden, tden, ps[:, 2, 0:256], ALU.mult).then_inc(moe_dve, 1)
                dve.wait_ge(moe_dve, s0 + 4)
                dve.tensor_tensor(hh, tden, ps[:, 2, 256:512], ALU.mult).then_inc(h_ok, 1)
                dve.wait_ge(ht_ps, e + 1)
                dve.tensor_copy(hhT, ps[:, 3, 0:256].rearrange("p (q n) -> p q n", q=2)).then_inc(ht_ok, 1)
                if more:
                    xm, b2 = store_xT(e + 1)
                    store_xT2(e + 1, xm, b2, s0 + 5)
                dve.wait_ge(dn_ps, e + 1)
                if later(stores):
                    dve.wait_ge(y_out[hb], stores * 16)
                dve.scalar_tensor_tensor(out=ye[:, hb, :], in0=ps[:, 4, :], scalar=wcol[:, 0:1], in1=gate2h,
                                         op0=ALU.mult, op1=ALU.mult).then_inc(y_ok, 1)

            xm, b2 = store_xT(0)
            store_xT2(0, xm, b2, 1)
            one_hot(1, 1)
            slot_tables(0, link)
            dve.wait_ge(tables_ok, 1)
            dve.wait_ge(g2_ok, 1)
            for j in range(2):
                expert(j, j, 0)
            with dve.Fori(1, NE // 2 - 1) as i:
                for j in range(2):
                    expert(i * 2 + j, j, i)
            expert(NE - 2, 0, NE // 2 - 1)
            expert(NE - 1, 1, NE // 2 - 1, more=False)

            def dve_round(rnd):
                dve.wait_ge(y_out[1], 16 * (NE // 2))
                dve.wait_ge(y_out[0], rnd * (16 * NE) - 16 * (NE // 2))
                at = [0]

                def step(ins):
                    at[0] += 1
                    ins.then_inc(round_seq, 1)
                    dve.wait_ge(round_seq, (rnd - 1) * ROUND_STEPS + at[0])

                step(dve.tensor_scalar(rs[:, 188:196], rs[:, 188:196], -float(CAP), None, ALU.add))
                step(dve.tensor_scalar(RE, RE, -float(CAP), None, ALU.add))
                slot_tables(rnd * (2 * NT), step)
                assert at[0] == ROUND_STEPS
                with dve.Fori(0, NE) as e:
                    dve.wait_ge(tables_ok, rnd + 1)
                    k = rnd * NE + e
                    one_hot(e, 0, k)
                    xm, b2 = store_xT(k)
                    store_xT2(k, xm, b2, k * NSTEP + 1)
                    expert(k, 0, rnd * NE + (e - NE // 2), more=False, col=e)

            ROUND_STEPS = 3 + 4 * NT
            more_rounds(dve, dve_round)

            for t in range(NT):
                dve.wait_ge(x_in[t], 48)
                y = arena[:, 2048 * t:2048 * (t + 1)].rearrange("p (j n) -> p j n", j=2)
                link(dve.tensor_tensor(xs[:, t, :], xs[:, t, :], y[:, 0, :], ALU.add))
                dve.tensor_tensor(xs[:, t, :], xs[:, t, :], y[:, 1, :], ALU.add).then_inc(fin_ok, 1)


_INS = ['x', 'c', 'positions', 'w_ada', 'b_ada', 'g_norm_mix', 'g_norm_ffn', 'w_in', 'w_branch_gate',
        'q_norm_g', 'k_norm_g', 'w_branch_dil', 'w_branch_sb', 'w_out', 'w_router_group',
        'b_router_group', 'w_router_expert', 'b_router_expert', 'w_expert_gate', 'w_expert_up',
        'w_expert_down']


def kernel(**inputs):
    import numpy as _np
    import concourse.bacc as _bacc
    from concourse import mybir as _mybir
    from concourse.bass_utils import run_bass_kernel_spmd as _run

    nc = _bacc.Bacc("TRN2", target_bir_lowering=False, num_devices=1)
    arrays, args = {}, []
    for name in _INS:
        a = _np.ascontiguousarray(inputs[name])
        arrays[f"in_{name}"] = a
        args.append(nc.dram_tensor(f"in_{name}", a.shape, _mybir.dt.from_np(a.dtype), kind="ExternalInput").ap())
    out = nc.dram_tensor("out", (1, SEQ, D), F32, kind="ExternalOutput").ap()
    hybrid_layer(nc, *args, out)
    r = _run(nc, [arrays], core_ids=[0])
    return r.results[0]["out"]
```
